# Optimizing a Trainium2 kernel written in Bass

```python
import math
import jax, jax.numpy as jnp
from jax import lax
import numpy as np

D_MODEL = 2048
BATCH = 1
SEQ = 256
DEPTH = 2

CHUNK = 64
Q_BLOCK = 128
N_A = DEPTH // 2
N_B = DEPTH - N_A
RWKV_HEAD = 64
RWKV_HEADS = D_MODEL // RWKV_HEAD
DECAY_LORA = max(32, int(round(1.8 * D_MODEL ** 0.5 / 32)) * 32)
AAA_LORA = max(32, int(round(1.8 * D_MODEL ** 0.5 / 32)) * 32)
GN_EPS = 64e-5
DIFF_HEADS = D_MODEL // 256
DIFF_HEAD_DIM = D_MODEL // DIFF_HEADS // 2
SUBLN_EPS = 1e-5
DEEPNORM_ALPHA = (2.0 * DEPTH) ** 0.25
DEEPNORM_BETA = (8.0 * DEPTH) ** -0.25
LN_EPS = 1e-5


def _layernorm(x, g, b):
    xf = x.astype(jnp.float32)
    mu = jnp.mean(xf, -1, keepdims=True)
    xc = xf - mu
    var = jnp.mean(xc * xc, -1, keepdims=True)
    return (xc * lax.rsqrt(var + LN_EPS) * g + b).astype(x.dtype)

def _wkv7_scan(r, w, k, v, kk, a):
    B, T, H, N = r.shape

    def step(S, inp):
        r_t, w_t, k_t, v_t, kk_t, a_t = inp
        sa = jnp.einsum('bhvk,bhk->bhv', S, kk_t)
        S = (S * w_t[:, :, None, :]
             - sa[..., None] * (kk_t * a_t)[:, :, None, :]
             + v_t[..., None] * k_t[:, :, None, :])
        y = jnp.einsum('bhvk,bhk->bhv', S, r_t)
        return S, y

    xs = tuple(jnp.moveaxis(t.astype(jnp.float32), 1, 0) for t in (r, w, k, v, kk, a))
    S0 = jnp.zeros((B, H, N, N), jnp.float32)
    _, ys = lax.scan(step, S0, xs)
    return jnp.moveaxis(ys, 0, 1)

def _rwkv7_mixer(x, mu_proj, mu_lora, w_in, w0, w1, w2, a0, a1, a2,
                 k_k, k_a, r_k, gn_g, gn_b, w_out):
    B, T, C = x.shape
    H, N = RWKV_HEADS, RWKV_HEAD
    xx = jnp.pad(x, ((0, 0), (1, 0), (0, 0)))[:, :-1] - x
    xs = x[None] + xx[None] * mu_proj[:, None, None, :]
    proj = jnp.einsum('sbtd,sde->sbte', xs, w_in)
    r, k, v, g = proj[0], proj[1], proj[2], proj[3]
    xw = x + xx * mu_lora[0]
    xa = x + xx * mu_lora[1]
    w_log = -jax.nn.softplus(-(w0 + jnp.tanh(xw @ w1) @ w2)) - 0.5
    decay = jnp.exp(-jnp.exp(w_log.astype(jnp.float32)))
    a = jax.nn.sigmoid(a0 + (xa @ a1) @ a2)
    kk = (k * k_k).reshape(B, T, H, N).astype(jnp.float32)
    kk = kk / jnp.maximum(jnp.sqrt(jnp.sum(kk * kk, -1, keepdims=True)), 1e-12)
    k = k * (1.0 + (a - 1.0) * k_a)
    rh = r.reshape(B, T, H, N)
    kh = k.reshape(B, T, H, N)
    vh = v.reshape(B, T, H, N)
    y = _wkv7_scan(rh, decay.reshape(B, T, H, N), kh, vh, kk, a.reshape(B, T, H, N))
    mu = jnp.mean(y, -1, keepdims=True)
    yc = y - mu
    var = jnp.mean(yc * yc, -1, keepdims=True)
    y = (yc * lax.rsqrt(var + GN_EPS)).reshape(B, T, C) * gn_g + gn_b
    bonus = jnp.sum(rh.astype(jnp.float32) * kh.astype(jnp.float32) * r_k, -1, keepdims=True) * vh.astype(jnp.float32)
    y = (y + bonus.reshape(B, T, C)).astype(x.dtype)
    return (y * jax.nn.silu(g)) @ w_out

def _diff_attention(q, k, v, lam):
    B, H2, T, dh = q.shape
    H = H2 // 2
    slopes = jnp.repeat(2.0 ** (-(8.0 / H) * jnp.arange(1, H + 1, dtype=jnp.float32)), 2)
    scale = dh ** -0.5
    outs = []
    for i in range(T // Q_BLOCK):
        q0, q1 = i * Q_BLOCK, (i + 1) * Q_BLOCK
        qb = q[:, :, q0:q1]
        kb = k[:, :, :q1]
        vb = v[:, :, :q1]
        s = jnp.einsum('bmqd,bmkd->bmqk', qb, kb).astype(jnp.float32) * scale
        tq = jnp.arange(q0, q1)
        tk = jnp.arange(q1)
        dist = jnp.abs(tq[:, None] - tk[None, :]).astype(jnp.float32)
        allowed = (tk[None, :] // CHUNK) <= (tq[:, None] // CHUNK)
        s = jnp.where(allowed, s - slopes[:, None, None] * dist, -jnp.inf)
        p = jax.nn.softmax(s, axis=-1).reshape(B, H, 2, Q_BLOCK, q1)
        attn = p[:, :, 0] - lam * p[:, :, 1]
        outs.append(jnp.einsum('bhqk,bhkd->bhqd', attn.astype(vb.dtype), vb))
    return jnp.concatenate(outs, axis=2)

def _diff_mixer(x, k_sh, v_sh, w_qg, lam_p, subln_g, w_out, layer):
    B, T, C = x.shape
    H, dh = DIFF_HEADS, DIFF_HEAD_DIM
    qg = x @ w_qg
    q = qg[..., :C].reshape(B, T, 2 * H, dh).transpose(0, 2, 1, 3)
    g = qg[..., C:]
    lam_init = 0.8 - 0.6 * math.exp(-0.3 * layer)
    lam_f = lam_p.astype(jnp.float32)
    lam = (jnp.exp(jnp.sum(lam_f[0] * lam_f[1])) - jnp.exp(jnp.sum(lam_f[2] * lam_f[3])) + lam_init)
    o = _diff_attention(q, k_sh, v_sh, lam).astype(jnp.float32)
    o = o * lax.rsqrt(jnp.mean(o * o, -1, keepdims=True) + SUBLN_EPS) * subln_g * (1.0 - lam_init)
    o = o.transpose(0, 2, 1, 3).reshape(B, T, C).astype(x.dtype)
    return (o * jax.nn.silu(g)) @ w_out

def first_inputs(seed: int = 0) -> dict:
    key = jax.random.key(seed)
    ks = jax.random.split(key, 32)
    C, H, N, dh = D_MODEL, RWKV_HEADS, RWKV_HEAD, DIFF_HEAD_DIM
    f32 = jnp.float32
    nrm = lambda k, shape, s: jax.random.normal(k, shape, f32) * s
    return {
        "x": jax.random.normal(ks[0], (BATCH, SEQ, C), f32),
        "a_mu_proj": jax.random.uniform(ks[1], (N_A, 4, C), f32),
        "a_mu_lora": jax.random.uniform(ks[2], (N_A, 2, C), f32),
        "a_w_in": nrm(ks[3], (N_A, 4, C, C), C ** -0.5),
        "a_w0": jax.random.uniform(ks[4], (N_A, C), f32, -6.0, 0.0),
        "a_w1": nrm(ks[5], (N_A, C, DECAY_LORA), C ** -0.5),
        "a_w2": nrm(ks[6], (N_A, DECAY_LORA, C), 0.1 * DECAY_LORA ** -0.5),
        "a_a0": nrm(ks[7], (N_A, C), 0.5),
        "a_a1": nrm(ks[8], (N_A, C, AAA_LORA), C ** -0.5),
        "a_a2": nrm(ks[9], (N_A, AAA_LORA, C), 0.3 * AAA_LORA ** -0.5),
        "a_k_k": 0.85 + nrm(ks[10], (N_A, C), 0.05),
        "a_k_a": 1.0 + nrm(ks[11], (N_A, C), 0.05),
        "a_r_k": -0.04 + nrm(ks[12], (N_A, H, N), 0.1),
        "a_gn_g": 1.0 + nrm(ks[13], (N_A, C), 0.05),
        "a_gn_b": nrm(ks[14], (N_A, C), 0.01),
        "a_w_out": nrm(ks[15], (N_A, C, C), C ** -0.5 * DEEPNORM_BETA),
        "w_k_shared": nrm(ks[16], (C, C), C ** -0.5),
        "w_v_shared": nrm(ks[17], (C, C), C ** -0.5),
        "b_w_qg": nrm(ks[18], (N_B, C, 2 * C), C ** -0.5),
        "b_lambda": nrm(ks[19], (N_B, 4, dh), 0.1),
        "b_subln_g": 1.0 + nrm(ks[20], (N_B, 2 * dh), 0.05),
        "b_w_out": nrm(ks[21], (N_B, C, C), C ** -0.5 * DEEPNORM_BETA),
        "ln_g": 1.0 + nrm(ks[22], (DEPTH, C), 0.05),
        "ln_b": nrm(ks[23], (DEPTH, C), 0.01),
    }

def first_block(x, a_mu_proj, a_mu_lora, a_w_in, a_w0, a_w1, a_w2, a_a0, a_a1, a_a2,
              a_k_k, a_k_a, a_r_k, a_gn_g, a_gn_b, a_w_out, w_k_shared, w_v_shared,
              b_w_qg, b_lambda, b_subln_g, b_w_out, ln_g, ln_b):
    B, T, C = x.shape
    k_sh = None
    v_sh = None
    for layer in range(DEPTH):
        if layer < N_A:
            i = layer
            y = _rwkv7_mixer(x, a_mu_proj[i], a_mu_lora[i], a_w_in[i], a_w0[i], a_w1[i], a_w2[i],
                             a_a0[i], a_a1[i], a_a2[i], a_k_k[i], a_k_a[i], a_r_k[i],
                             a_gn_g[i], a_gn_b[i], a_w_out[i])
        else:
            j = layer - N_A
            y = _diff_mixer(x, k_sh, v_sh, b_w_qg[j], b_lambda[j], b_subln_g[j], b_w_out[j], layer)
        x = _layernorm(DEEPNORM_ALPHA * x + y, ln_g[layer], ln_b[layer])
        if layer == N_A - 1:
            k_sh = (x @ w_k_shared).reshape(B, T, 2 * DIFF_HEADS, DIFF_HEAD_DIM).transpose(0, 2, 1, 3)
            v_sh = (x @ w_v_shared).reshape(B, T, DIFF_HEADS, 2 * DIFF_HEAD_DIM).transpose(0, 2, 1, 3)
    return x


DEPTH_2 = 1

NSA_HEADS = 8
NSA_KV_GROUPS = 2
NSA_HG = NSA_HEADS // NSA_KV_GROUPS
NSA_DK = 128
NSA_WIDTH = NSA_HEADS * NSA_DK
KV_W = NSA_KV_GROUPS * NSA_DK
CMP_BLOCK = 32
CMP_STRIDE = 16
SEL_BLOCK = 64
SEL_TOPN = 16
WINDOW = 512
FORCE = 1e4
NEG = -1e30
RET_HEADS = 4
RET_DK = 256
RET_DV = 256
RET_WIDTH = RET_HEADS * RET_DV
RET_CHUNK = 128
ROPE_BASE = 10000.0
GN_EPS_2 = 1e-6
MIX_WIDTH = NSA_WIDTH + RET_WIDTH
T5_BUCKETS = 32
T5_MAX_DIST = 128
D_FF = 4 * D_MODEL
NORM_EPS = 1e-6
IN_SIZES = [NSA_WIDTH, 6 * KV_W, 3 * NSA_HEADS, RET_HEADS * RET_DK, RET_HEADS * RET_DK, RET_WIDTH, RET_WIDTH]
D_IN = sum(IN_SIZES)
IN_OFFSETS = np.cumsum(IN_SIZES)[:-1].tolist()


def rms_norm(x, g):
    xf = x.astype(jnp.float32)
    y = xf * lax.rsqrt(jnp.mean(xf * xf, axis=-1, keepdims=True) + NORM_EPS)
    return (y * g.astype(jnp.float32)).astype(x.dtype)

def t5_bucket(rel):
    n = jnp.maximum(rel, 0)
    max_exact = T5_BUCKETS // 2
    nf = jnp.maximum(n, 1).astype(jnp.float32)
    large = max_exact + (jnp.log(nf / max_exact) / np.log(T5_MAX_DIST / max_exact)
                         * (T5_BUCKETS - max_exact)).astype(jnp.int32)
    large = jnp.minimum(large, T5_BUCKETS - 1)
    return jnp.where(n < max_exact, n, large)

def rope(x, pos):
    d = x.shape[-1]
    inv_freq = ROPE_BASE ** (-jnp.arange(0, d, 2, dtype=jnp.float32) / d)
    ang = pos.astype(jnp.float32)[:, None] * inv_freq[None, :]
    cos = jnp.cos(ang)[None, :, None, :]
    sin = jnp.sin(ang)[None, :, None, :]
    xf = x.astype(jnp.float32)
    x1, x2 = xf[..., : d // 2], xf[..., d // 2:]
    return jnp.concatenate([x1 * cos - x2 * sin, x2 * cos + x1 * sin], axis=-1).astype(x.dtype)

def compress_kv(kv, pe, w1, b1, w2):
    B, S, G, dk = kv.shape
    n_cmp = (S - CMP_BLOCK) // CMP_STRIDE + 1
    idx = jnp.arange(n_cmp)[:, None] * CMP_STRIDE + jnp.arange(CMP_BLOCK)[None, :]
    blocks = kv[:, idx] + pe[None, None, :, None, :]
    flat = blocks.transpose(0, 1, 3, 2, 4).reshape(B, n_cmp, G, CMP_BLOCK * dk)
    hid = jax.nn.gelu(flat @ w1 + b1)
    return hid @ w2

def nsa_attention(q, k_cmp, v_cmp, k_slc, v_slc, k_win, v_win, gates, t5_table):
    B, S, H, dk = q.shape
    G, Hg = NSA_KV_GROUPS, NSA_HG
    n_cmp = k_cmp.shape[1]
    n_sel = S // SEL_BLOCK
    top_n = min(SEL_TOPN, n_sel)
    scale = dk ** -0.5
    cmp_end = jnp.arange(n_cmp) * CMP_STRIDE + CMP_BLOCK - 1
    cs = np.arange(n_cmp) * CMP_STRIDE
    ss = np.arange(n_sel) * SEL_BLOCK
    overlap = (cs[:, None] <= ss[None, :] + SEL_BLOCK - 1) & (cs[:, None] + CMP_BLOCK - 1 >= ss[None, :])
    m_sel = jnp.asarray(overlap, jnp.float32)
    tbl = t5_table.astype(jnp.float32).reshape(T5_BUCKETS, G, Hg)
    ks_blocks = k_slc.reshape(B, n_sel, SEL_BLOCK, G, dk).transpose(0, 3, 1, 2, 4)
    vs_blocks = v_slc.reshape(B, n_sel, SEL_BLOCK, G, dk).transpose(0, 3, 1, 2, 4)
    kw_pad = jnp.pad(k_win, ((0, 0), (WINDOW, 0), (0, 0), (0, 0)))
    vw_pad = jnp.pad(v_win, ((0, 0), (WINDOW, 0), (0, 0), (0, 0)))
    qg = q.reshape(B, S, G, Hg, dk)
    gg = gates.reshape(B, S, G, Hg, 3)
    b_idx = jnp.arange(B)[:, None, None, None]
    g_idx = jnp.arange(G)[None, :, None, None]
    g_idx5 = jnp.arange(G)[None, :, None, None, None]
    jblk = jnp.arange(n_sel)

    def block(c):
        s0 = c * Q_BLOCK
        qc = lax.dynamic_slice_in_dim(qg, s0, Q_BLOCK, axis=1)
        tq = s0 + jnp.arange(Q_BLOCK)
        rel = tq[:, None] - cmp_end[None, :]
        s = jnp.einsum('bqghd,bngd->bghqn', qc, k_cmp).astype(jnp.float32) * scale
        s = s + tbl[t5_bucket(rel)].transpose(2, 3, 0, 1)[None]
        valid = rel >= 0
        p = jax.nn.softmax(jnp.where(valid, s, NEG), axis=-1)
        p = jnp.where(valid, p, 0.0)
        o_cmp = jnp.einsum('bghqn,bngd->bqghd', p.astype(v_cmp.dtype), v_cmp)
        imp = jnp.einsum('bghqn,nj->bgqj', p, m_sel)
        cur = tq // SEL_BLOCK
        blk_valid = jblk[None, :] * SEL_BLOCK <= tq[:, None]
        forced = (jblk[None, :] == 0) | (jblk[None, :] == cur[:, None]) | (jblk[None, :] == cur[:, None] - 1)
        imp = jnp.where(blk_valid, jnp.where(forced, FORCE, imp), -1.0)
        top_val, top_idx = lax.top_k(imp, top_n)
        ksel = ks_blocks[b_idx, g_idx, top_idx]
        vsel = vs_blocks[b_idx, g_idx, top_idx]
        kpos = top_idx[..., None] * SEL_BLOCK + jnp.arange(SEL_BLOCK)
        rel = tq[None, None, :, None, None] - kpos
        s = jnp.einsum('bqghd,bgqnld->bghqnl', qc, ksel).astype(jnp.float32) * scale
        s = s + tbl[t5_bucket(rel), g_idx5].transpose(0, 1, 5, 2, 3, 4)
        valid = ((rel >= 0) & (top_val >= 0)[..., None])[:, :, None]
        s = jnp.where(valid, s, NEG).reshape(B, G, Hg, Q_BLOCK, top_n * SEL_BLOCK)
        p = jax.nn.softmax(s, axis=-1).reshape(B, G, Hg, Q_BLOCK, top_n, SEL_BLOCK)
        o_slc = jnp.einsum('bghqnl,bgqnld->bqghd', p.astype(vsel.dtype), vsel)
        kw = lax.dynamic_slice_in_dim(kw_pad, s0, WINDOW + Q_BLOCK, axis=1)
        vw = lax.dynamic_slice_in_dim(vw_pad, s0, WINDOW + Q_BLOCK, axis=1)
        kpos = s0 - WINDOW + jnp.arange(WINDOW + Q_BLOCK)
        rel = tq[:, None] - kpos[None, :]
        valid = (rel >= 0) & (rel < WINDOW) & (kpos[None, :] >= 0)
        s = jnp.einsum('bqghd,bkgd->bghqk', qc, kw).astype(jnp.float32) * scale
        s = s + tbl[t5_bucket(rel)].transpose(2, 3, 0, 1)[None]
        p = jax.nn.softmax(jnp.where(valid, s, NEG), axis=-1)
        o_win = jnp.einsum('bghqk,bkgd->bqghd', p.astype(vw.dtype), vw)
        gc = lax.dynamic_slice_in_dim(gg, s0, Q_BLOCK, axis=1)
        o = gc[..., 0:1] * o_cmp + gc[..., 1:2] * o_slc + gc[..., 2:3] * o_win
        return o.reshape(B, Q_BLOCK, H * dk)

    out = lax.map(block, jnp.arange(S // Q_BLOCK))
    return out.transpose(1, 0, 2, 3).reshape(B, S, H * dk)

def retention(q, k, v, log_gamma):
    B, S, H, dk = q.shape
    dv = v.shape[-1]
    C = RET_CHUNK
    N = S // C
    k = k * (dk ** -0.5)
    qc = q.reshape(B, N, C, H, dk).transpose(1, 0, 3, 2, 4)
    kc = k.reshape(B, N, C, H, dk).transpose(1, 0, 3, 2, 4)
    vc = v.reshape(B, N, C, H, dv).transpose(1, 0, 3, 2, 4)
    idx = jnp.arange(C, dtype=jnp.float32)
    diff = idx[:, None] - idx[None, :]
    decay = jnp.where(diff[None] >= 0, jnp.exp(jnp.maximum(diff, 0.0)[None] * log_gamma[:, None, None]), 0.0)
    xi = jnp.exp((idx + 1.0)[None, :] * log_gamma[:, None])
    zeta = jnp.exp((C - 1.0 - idx)[None, :] * log_gamma[:, None])
    g_c = jnp.exp(C * log_gamma)
    inner = jnp.einsum('nbhcd,nbhmd->nbhcm', qc, kc).astype(jnp.float32) * decay
    inner = jnp.einsum('nbhcm,nbhme->nbhce', inner, vc.astype(jnp.float32))

    def step(R, xs):
        q_n, k_n, v_n = xs
        cross = jnp.einsum('bhcd,bhde->bhce', q_n.astype(jnp.float32), R) * xi[None, :, :, None]
        R = R * g_c[None, :, None, None] + jnp.einsum(
            'bhcd,bhce->bhde', k_n.astype(jnp.float32) * zeta[None, :, :, None], v_n.astype(jnp.float32))
        return R, cross

    R0 = jnp.zeros((B, H, dk, dv), jnp.float32)
    _, cross = lax.scan(step, R0, (qc, kc, vc))
    o = (inner + cross).transpose(1, 0, 3, 2, 4).reshape(B, S, H, dv)
    mu = jnp.mean(o, axis=-1, keepdims=True)
    var = jnp.mean(jnp.square(o - mu), axis=-1, keepdims=True)
    return (o - mu) * lax.rsqrt(var + GN_EPS_2)

def second_inputs(seed: int = 0) -> dict:
    key = jax.random.key(seed)
    ks = jax.random.split(key, 20)
    f32 = jnp.float32

    def nrm(k, shape, scale):
        return jax.random.normal(k, shape, f32) * scale

    def gain(k):
        return 1.0 + nrm(k, (DEPTH_2, D_MODEL), 0.05)

    LDK = CMP_BLOCK * NSA_DK
    return {
        "x": nrm(ks[0], (BATCH, SEQ, D_MODEL), 1.0),
        "norm_mix_pre": gain(ks[1]),
        "w_in": nrm(ks[2], (DEPTH_2, D_MODEL, D_IN), D_MODEL ** -0.5),
        "cmp_pe_k": nrm(ks[3], (DEPTH_2, CMP_BLOCK, NSA_DK), 0.1),
        "cmp_w1_k": nrm(ks[4], (DEPTH_2, LDK, NSA_DK), LDK ** -0.5),
        "cmp_b1_k": nrm(ks[5], (DEPTH_2, NSA_DK), 0.02),
        "cmp_w2_k": nrm(ks[6], (DEPTH_2, NSA_DK, NSA_DK), NSA_DK ** -0.5),
        "cmp_pe_v": nrm(ks[7], (DEPTH_2, CMP_BLOCK, NSA_DK), 0.1),
        "cmp_w1_v": nrm(ks[8], (DEPTH_2, LDK, NSA_DK), LDK ** -0.5),
        "cmp_b1_v": nrm(ks[9], (DEPTH_2, NSA_DK), 0.02),
        "cmp_w2_v": nrm(ks[10], (DEPTH_2, NSA_DK, NSA_DK), NSA_DK ** -0.5),
        "t5_bias": nrm(ks[11], (T5_BUCKETS, NSA_HEADS), 0.2),
        "w_out": nrm(ks[12], (DEPTH_2, MIX_WIDTH, D_MODEL), MIX_WIDTH ** -0.5),
        "norm_mix_post": gain(ks[13]),
        "norm_mlp_pre": gain(ks[14]),
        "w_up": nrm(ks[15], (DEPTH_2, D_MODEL, D_FF), D_MODEL ** -0.5),
        "w_down": nrm(ks[16], (DEPTH_2, D_FF, D_MODEL), D_FF ** -0.5),
        "norm_mlp_post": gain(ks[17]),
    }

def second_block(x, norm_mix_pre, w_in, cmp_pe_k, cmp_w1_k, cmp_b1_k, cmp_w2_k, cmp_pe_v, cmp_w1_v,
              cmp_b1_v, cmp_w2_v, t5_bias, w_out, norm_mix_post, norm_mlp_pre, w_up, w_down,
              norm_mlp_post):
    B, S, _ = x.shape
    pos = jnp.arange(S)
    log_gamma = jnp.log(1.0 - jnp.exp2(-5.0 - jnp.arange(RET_HEADS, dtype=jnp.float32)))
    for l in range(DEPTH_2):
        h = rms_norm(x, norm_mix_pre[l])
        proj = h @ w_in[l]
        q_a, kv_a, gate_a, q_r, k_r, v_r, g_r = jnp.split(proj, IN_OFFSETS, axis=-1)
        q_a = q_a.reshape(B, S, NSA_HEADS, NSA_DK)
        kv6 = kv_a.reshape(B, S, 6, NSA_KV_GROUPS, NSA_DK)
        k_cmp = compress_kv(kv6[:, :, 0], cmp_pe_k[l], cmp_w1_k[l], cmp_b1_k[l], cmp_w2_k[l])
        v_cmp = compress_kv(kv6[:, :, 1], cmp_pe_v[l], cmp_w1_v[l], cmp_b1_v[l], cmp_w2_v[l])
        gates = jax.nn.sigmoid(gate_a.reshape(B, S, NSA_HEADS, 3))
        o_a = nsa_attention(q_a, k_cmp, v_cmp, kv6[:, :, 2], kv6[:, :, 3], kv6[:, :, 4], kv6[:, :, 5],
                            gates, t5_bias)
        q_r = rope(q_r.reshape(B, S, RET_HEADS, RET_DK), pos)
        k_r = rope(k_r.reshape(B, S, RET_HEADS, RET_DK), pos)
        o_r = retention(q_r, k_r, v_r.reshape(B, S, RET_HEADS, RET_DV), log_gamma)
        o_r = (jax.nn.silu(g_r.astype(jnp.float32)) * o_r.reshape(B, S, RET_WIDTH)).astype(x.dtype)
        mix = jnp.concatenate([o_a.astype(x.dtype), o_r], axis=-1) @ w_out[l]
        x = x + rms_norm(mix, norm_mix_post[l])
        h = rms_norm(x, norm_mlp_pre[l])
        u = jnp.square(jax.nn.relu(h @ w_up[l]))
        x = x + rms_norm(u @ w_down[l], norm_mlp_post[l])
    return x


def setup_inputs(seed=0):
    out = dict(first_inputs(seed))
    for name, value in second_inputs(seed + 1).items():
        if name != "x":
            out[name + "_2"] = value
    return out


def reference(
    x, a_mu_proj, a_mu_lora, a_w_in, a_w0, a_w1, a_w2, a_a0, a_a1, a_a2, a_k_k, a_k_a, a_r_k,
    a_gn_g, a_gn_b, a_w_out, w_k_shared, w_v_shared, b_w_qg, b_lambda, b_subln_g, b_w_out, ln_g,
    ln_b, norm_mix_pre_2, w_in_2, cmp_pe_k_2, cmp_w1_k_2, cmp_b1_k_2, cmp_w2_k_2, cmp_pe_v_2,
    cmp_w1_v_2, cmp_b1_v_2, cmp_w2_v_2, t5_bias_2, w_out_2, norm_mix_post_2, norm_mlp_pre_2,
    w_up_2, w_down_2, norm_mlp_post_2,
):
    x = first_block(
        x, a_mu_proj, a_mu_lora, a_w_in, a_w0, a_w1, a_w2, a_a0, a_a1, a_a2, a_k_k, a_k_a,
        a_r_k, a_gn_g, a_gn_b, a_w_out, w_k_shared, w_v_shared, b_w_qg, b_lambda, b_subln_g,
        b_w_out, ln_g, ln_b,
    )
    return second_block(
        x, norm_mix_pre_2, w_in_2, cmp_pe_k_2, cmp_w1_k_2, cmp_b1_k_2, cmp_w2_k_2, cmp_pe_v_2,
        cmp_w1_v_2, cmp_b1_v_2, cmp_w2_v_2, t5_bias_2, w_out_2, norm_mix_post_2, norm_mlp_pre_2,
        w_up_2, w_down_2, norm_mlp_post_2,
    )


_drawn_inputs = setup_inputs


def setup_inputs(seed=0):
    import zlib

    import numpy as np

    out = dict(_drawn_inputs(seed))
    spreads = {}
    factors = {'a_mu_lora': 3.639,
     'a_w1': 8.0,
     'a_w2': 8.0,
     'a_k_k': 5.708,
     'a_k_a': 3.93,
     'a_gn_g': 4.117,
     'a_gn_b': 8.0,
     'b_lambda': 8.0,
     'b_subln_g': 5.415,
     'cmp_pe_k_2': 8.0,
     'cmp_b1_k_2': 51.568,
     'cmp_b1_v_2': 8.0}
    for name, (base, spread) in spreads.items():
        noise = np.random.default_rng([zlib.crc32(name.encode()), seed]).standard_normal(out[name].shape)
        drawn = base * np.exp(spread * noise) if base else spread * noise
        out[name] = __import__('jax').numpy.asarray(drawn.astype(out[name].dtype))
    for name, factor in factors.items():
        out[name] = (out[name] * factor).astype(out[name].dtype)
    return out
```

```python
from contextlib import ExitStack
import math

import numpy as np

import concourse.bass as bass
from concourse import mybir

F32 = mybir.dt.float32
ALU = mybir.AluOpType
ACT = mybir.ActivationFunctionType
AX = mybir.AxisListType

P = 128
D = 2048
T = 256
DT = D // P
TT = T // P
N = 64
NCH = T // N
LORA = 96
ALPHA = (2.0 * 2) ** 0.25
LN_EPS = 1e-5
RING = 8
DECAY = -math.exp(-0.5)
GN_EPS = 64e-5

DH = 8
D_SCALE = 128 ** -0.5
LAM_INIT = 0.8 - 0.6 * math.exp(-0.3 * 1)
SUBLN_EPS = 1e-5
A_SCALE = 128 ** -0.5
NCMP = 15
NEG = -1e30
EPS6 = 1e-6

PANELS = {}
_n = 0
for _name, _count in (("k", 4), ("r", 4), ("v", 4), ("g", 4), ("out0", 4), ("dk", 4), ("dq", 4), ("dv", 4), ("dg", 4),
                      ("out1", 4), ("cmp", 1), ("kk", 1), ("kr", 2), ("qr", 2), ("qa", 2), ("vv", 1), ("vr", 2),
                      ("gr", 2), ("out2", 4), ("up", 16), ("down", 4)):
    PANELS[_name] = _n
    _n += _count
SLOTS = 4 * PANELS["down"] + 4 * 16

PV = {name: i for i, name in enumerate(
    ("mu_w", "mu_a", "mu_k", "mu_r", "mu_v", "mu_g", "w0", "a0", "k_k", "k_a", "r_k", "gn_g", "gn_b", "mix_pre",
     "mlp_pre", "subln"))}
MIXES = ("mu_w", "mu_a", "mu_k", "mu_r", "mu_v", "mu_g")

C_ID, C_ONES64, C_ID64, C_NM1, C_NM1T, C_MB, C_U, C_UI, C_L = 0, 128, 256, 320, 384, 448, 768, 832, 896
C_COLS = 960


def resident_constants():
    c = np.zeros((P, C_COLS), np.float32)
    c[:, C_ID:C_ID + P] = np.eye(P)
    c[:64, C_ONES64:C_ONES64 + 64] = 1
    c[64:, C_ONES64 + 64:C_ONES64 + 128] = 1
    r, s = np.arange(P)[:, None] % 64, np.arange(64)[None, :]
    c[:, C_ID64:C_ID64 + 64] = r == s

    def merge(b, lo, hi):
        return (lo // (2 * b) == hi // (2 * b)) & (lo % (2 * b) < b) & (hi % (2 * b) >= b)

    c[:, C_NM1:C_NM1 + 64] = -1.0 * merge(1, r, s)
    c[:, C_NM1T:C_NM1T + 64] = -1.0 * merge(1, s, r)
    for i, b in enumerate((2, 4, 8, 16, 32)):
        c[:, C_MB + 64 * i:C_MB + 64 * i + 64] = merge(b, r, s)
    c[:, C_U:C_U + 64] = r < s
    c[:, C_UI:C_UI + 64] = r <= s
    c[:, C_L:C_L + 64] = r > s
    return c


def diff_constants():
    q, k = 128 + np.arange(P)[:, None], np.arange(T)[None, :]
    return np.where(k // 64 <= q // 64, np.abs(q - k), 1e30).astype(np.float32)


def t5_buckets(rel):
    n = np.maximum(rel, 0)
    nf = np.maximum(n, 1).astype(np.float32)
    large = 16 + (np.log(nf / np.float32(16)) / np.float32(np.log(128 / 16)) * np.float32(16)).astype(np.int32)
    return np.where(n < 16, n, np.minimum(large, 31))


def t5_constants():
    rel = np.concatenate([255 - np.arange(384), np.arange(512) - 255])
    one = np.zeros((33, 896), np.float32)
    one[np.where(rel < 0, 32, t5_buckets(rel)), np.arange(896)] = 1
    return one


def valid_constants():
    t = np.arange(T).reshape(TT, P).T[:, :, None]
    return (t >= 16 * np.arange(NCMP) + 31).astype(np.float32)


def rope_constants():
    inv = (np.float32(10000.0) ** (-np.arange(0, 256, 2, dtype=np.float32) / np.float32(256))).astype(np.float32)
    ang = (np.arange(T, dtype=np.float32)[:, None] * inv[None, :]).astype(np.float32)
    return np.stack([np.cos(ang).T, np.sin(ang).T], 1).astype(np.float32)


def decay_constants():
    lg = np.log(1.0 - np.exp2(-5.0 - np.arange(4)))
    m = np.arange(P)[:, None]
    out = np.zeros((P, 4, 384))
    for h in range(4):
        d0 = np.arange(T)[None, :] - m
        d1 = np.arange(P)[None, :] - m
        out[:, h, :256] = np.where(d0 >= 0, np.exp(np.maximum(d0, 0) * lg[h]), 0)
        out[:, h, 256:] = np.where(d1 >= 0, np.exp(np.maximum(d1, 0) * lg[h]), 0)
    return (out / 16.0).astype(np.float32)


def slot_panels(w, columns):
    part = w[:, columns]
    return part.reshape(-1, 4, P, 512).transpose(0, 2, 1, 3).reshape(-1, P, 2048)


def build(nc, d):
    ctx = ExitStack()
    with ctx:
        def sb(name, shape):
            return ctx.enter_context(nc.sbuf_tensor(name, shape, F32))

        def sem(name):
            return ctx.enter_context(nc.semaphore(name))

        ring = sb("ring", [P, RING, 4, 512])
        hall = sb("hall", [P, 8, DT, T])
        work = sb("work", [P, 2, DT, N])
        con = sb("con", [P, C_COLS])
        par = sb("par", [P, 16, DT])
        wl = sb("wl", [P, DT, NCH])
        small = sb("small", [P, 464])
        ps = ctx.enter_context(nc.psum_tensor("ps", [P, 8, 512], F32))

        XT, MIX, LD, AA, KK, KN, RR, VV = range(8)
        flat = [hall[:, i].rearrange("p a b -> p (a b)") for i in range(8)]
        ident = con[:, C_ID:C_ID + P]
        ones64 = con[:, C_ONES64:C_ONES64 + P]
        id64 = con[:, C_ID64:C_ID64 + 64]

        def pv(name):
            return par[:, PV[name], :]

        def over(ap, shape):
            return ap.unsqueeze(2).broadcast_to(shape)

        def mask(column, width=DT):
            return con[:, column:column + 64].unsqueeze(1).broadcast_to([P, width, 64])

        slot_landed = [sem(f"slot_landed{i}") for i in range(RING)]
        slots_used = sem("slots_used")
        panel_evacuated = [sem("even_panel_evacuated"), sem("odd_panel_evacuated")]
        const_in = sem("const_in")
        x_in = sem("x_in")
        lora_in = sem("lora_in")
        mix_ready = sem("mix_ready")
        lora_read = sem("lora_read")
        lora_hid_done = sem("lora_hid_done")
        lora_hid_copied = sem("lora_hid_copied")
        lora_up_done = sem("lora_up_done")
        lora_up_copied = sem("lora_up_copied")
        key_raw_ready = sem("key_raw_ready")
        key_squared = sem("key_squared")
        key_norm_summed = sem("key_norm_summed")
        key_norm_ready = sem("key_norm_ready")
        decay_summed = sem("decay_summed")
        decay_exp_ready = sem("decay_exp_ready")
        key_group_done = sem("key_group_done")
        receptance_done = sem("receptance_done")
        gram_done = sem("gram_done")
        dve_step = sem("dve_step")
        act_step = sem("act_step")
        gram_masked = sem("gram_masked")
        z_done = sem("z_done")
        z_masked = sem("z_masked")
        merge_done = sem("merge_done")
        merged = sem("merged")
        turned = sem("turned")
        turned_copied = sem("turned_copied")
        rhs_done = sem("rhs_done")
        rhs_ready = sem("rhs_ready")
        u_done = sem("u_done")
        u_ready = sem("u_ready")
        y_done = sem("y_done")
        y_copied = sem("y_copied")
        state_done = sem("state_done")
        state_ready = sem("state_ready")
        head_sum_done = sem("head_sum_done")
        head_in_ready = sem("head_in_ready")
        head_root_ready = sem("head_root_ready")
        out_rows_ready = sem("out_rows_ready")
        rows_in = sem("rows_in")
        ln_var_ready = sem("ln_var_ready")
        ln_root_ready = sem("ln_root_ready")
        act_rows_ready = sem("act_rows_ready")
        tok_ready = sem("tok_ready")
        tr_done = sem("tr_done")
        tr_copied_v = sem("tr_copied_v")
        tr_copied_a = sem("tr_copied_a")
        region_free = sem("region_free")
        diff_in = sem("diff_in")
        lam_parts = sem("lam_parts")
        lam_exp = sem("lam_exp")
        score_done = sem("score_done")
        score_max = sem("score_max")
        score_exp = sem("score_exp")
        attn_ready = sem("attn_ready")
        attn_turned = sem("attn_turned")
        attn_copied = sem("attn_copied")
        o_done = sem("o_done")
        o_copied = sem("o_copied")
        nsa_in = sem("nsa_in")
        t5_in = sem("t5_in")
        t5_done = sem("t5_done")
        t5_copied = sem("t5_copied")
        t5_stored = sem("t5_stored")
        blocks_ready = sem("blocks_ready")
        cmp_done = sem("cmp_done")
        cmp_step = sem("cmp_step")
        gate_done = sem("gate_done")
        gate_copied = sem("gate_copied")
        rope_ready = sem("rope_ready")
        ret_score_done = sem("ret_score_done")
        ret_score_ready = sem("ret_score_ready")
        ret_o_done = sem("ret_o_done")
        ret_o_ready = sem("ret_o_ready")
        ret_var_ready = sem("ret_var_ready")
        ret_root_ready = sem("ret_root_ready")
        out_stored = sem("out_stored")
        chunk_done = sem("chunk_done")
        eps_ready = sem("eps_ready")
        y_centred = sem("y_centred")
        finished = sem("finished")
        ret_in = sem("ret_in")


        more = ("squares_summed score_read post_in nsa_parts_in cmp_hid_done cmp_hid_ready cmp_hid_turned cmp_hid_copied "
                "cmp_made cmp_copied cmp_scored cmp_centred cmp_exp cmp_probs_ready cmp_turned cmp_turned_copied "
                "gate_sum_done gate_sum_copied gate_turned gates_ready rope_in mix_copied post_root_ready post_rows_ready "
                "up_squared down_copied ret_turned ret_turned_copied t5_table_in").split()
        (squares_summed, score_read, post_in, nsa_parts_in, cmp_hid_done, cmp_hid_ready, cmp_hid_turned, cmp_hid_copied,
         cmp_made, cmp_copied, cmp_scored, cmp_centred, cmp_exp, cmp_probs_ready, cmp_turned, cmp_turned_copied,
         gate_sum_done, gate_sum_copied, gate_turned, gates_ready, rope_in, mix_copied, post_root_ready, post_rows_ready,
         up_squared, down_copied, ret_turned, ret_turned_copied, t5_table_in) = (sem(x) for x in more)
        block = ctx.enter_context(nc.Block())

        def evacuated(eng, n):
            eng.wait_ge(panel_evacuated[n % 2], n // 2 + 1)

        def computed(eng, n, quarter=3):
            eng.wait_ge(slots_used, 4 * n + quarter + 1)

        def wide(w):
            return ps[:, 2 * w:2 * w + 2, :].rearrange("p b (j s) -> p (b j) s", s=N)

        def gram(w):
            return ps[:, 4 * w:4 * w + 4, :].rearrange("p b (j x s) -> p (b j) x s", x=2, s=N)

        bufs = [flat[i].rearrange("p (k j s) -> p k j s", k=4, s=N) for i in (XT, MIX)]
        X, XTR, AT, Z = (bufs[0][:, k] for k in range(4))
        ARB, AAK, ARK, VTOK = (bufs[1][:, k] for k in range(4))
        ST, KTOK = work[:, 0], work[:, 1]
        BTOK, RHS, U, YC, BON, SQ = AT, Z, XTR, ARB, AAK, ARK
        HEADS = [x for j in range(DT) for x in ((j, 0), ((j + DT // 2) % DT, 1))]
        rows = (slice(0, N), slice(N, P))
        lora_w1 = flat[VV][:, 0:2 * DT * LORA].rearrange("p (m a r) -> p m a r", m=2, r=LORA)
        lora_w2 = flat[KN][0:LORA, :].rearrange("p (m c) -> p m c", m=2)
        restart = work[:, 0].rearrange("p j s -> p (j s)")[:, 0:T]
        lora_hid = work[0:LORA, 1].rearrange("p j s -> p (j s)")[:, 0:2 * T].rearrange("p (m t) -> p m t", m=2)
        key_sq = [hall[:, VV, 0:4], hall[:, VV, 4:8]]
        key_tmp, key_exp = hall[:, VV, 8:12], hall[:, VV, 12:16]
        EPS_GN, EPS_LN, EPS_SUB, EPS_6 = (small[:, i:i + 1] for i in range(4))

        def token_rows(region, width=D):
            return flat[region][:, 0:TT * width].rearrange("p (a c) -> p a c", a=TT)

        X_TOK, ROWS, X_T, DK, DQ, DV, DG, O_TOK = range(8)
        prob = [flat[ROWS][:, 512 * i:512 * i + 512] for i in range(2)]
        prob_t = [flat[ROWS][:, 1024 + 512 * i:1536 + 512 * i] for i in range(2)]
        dist = flat[ROWS][:, 2048:2304]
        lam_rows = flat[ROWS][:, 2304:2816].rearrange("p (a b) -> p a b", a=4)
        lam_tmp = flat[ROWS][:, 2816:3072].rearrange("p (a b) -> p a b", a=2)
        junk = flat[ROWS][:, 3072:3328]
        stats = small[:, 8:56].rearrange("p (t k s) -> p t k s", t=TT, k=4)
        mean_var = small[:, 56:60].rearrange("p (t k) -> p t k", t=TT)
        root = small[:, 60:62]
        top = [small[:, 64 + 4 * i:66 + 4 * i] for i in range(2)]
        total = [small[:, 72 + 4 * i:74 + 4 * i] for i in range(2)]
        share = [small[:, 80 + 4 * i:82 + 4 * i] for i in range(2)]
        lam_sum, lam, neg_lam = small[:, 88:90], small[:, 90:91], small[:, 91:92]
        o_squares = small[:, 96:112]
        row_squares = small[:, 112:120].rearrange("p (t k) -> p t k", t=TT)
        row_root = small[:, 120:122]

        H_TOK, H_T, QA_CM_K4, QR_KR, VR_GR, CAT_T, BIAS_VV = 1, 2, 3, 4, 5, 6, 7
        qa, cm, k4 = hall[:, QA_CM_K4, 0:8], hall[:, QA_CM_K4, 8:12], hall[:, QA_CM_K4, 12:16]
        qr, kr = hall[:, QR_KR, 0:8], hall[:, QR_KR, 8:16]
        vr = flat[VR_GR][:, 0:2048].rearrange("p (t c) -> p t c", t=TT)
        gr = flat[VR_GR][:, 2048:4096].rearrange("p (t c) -> p t c", t=TT)
        bias = flat[BIAS_VV][:, 0:2048].rearrange("p (h k) -> p h k", h=8)
        vv = flat[BIAS_VV][:, 2048:3072].rearrange("p (t c) -> p t c", t=TT)
        misc = flat[BIAS_VV][:, 3072:4096]
        block_pe = misc[:, 0:64]
        cmp_w2 = misc[:, 64:320].rearrange("p (a b) -> p a b", a=2)
        cmp_b1 = misc[0:2 * NCMP, 320:576].rearrange("p (a b) -> p a b", a=2)
        cmp_hid = misc[0:2 * NCMP, 576:832].rearrange("p (a b) -> p a b", a=2)
        cmp_hid_t = misc[:, 832:892].rearrange("p (a b) -> p a b", a=2)
        gates = misc[:, 892:940].rearrange("p (t b) -> p t b", t=TT)
        gate_sum = flat[CAT_T][0:24, 0:T]
        work_flat = work[:].rearrange("p a j s -> p (a j s)")
        windows = [work_flat[:, 960 * i:960 * i + 960].rearrange("p (l g n) -> p l g n", l=32, g=2) for i in range(2)]
        cmp_prob_t = work_flat[0:NCMP, :].rearrange("p (i q) -> p i q", q=P)
        cmp_w1 = [flat[r].rearrange("p (l c) -> p l c", l=32) for r in (H_TOK, VR_GR)]
        gate_w = con[:, 256:640].rearrange("p (a b) -> p a b", a=DT)
        cmp_k = con[:, 640:670]
        cmp_v = con[0:NCMP, 670:926].rearrange("p (g c) -> p g c", g=2)
        cmp_bias = small[:, 224:464]
        cmp_p, cmp_valid = flat[H_TOK][:, 3072 - 512:3072 - 272], flat[H_TOK][:, 3072 - 256:3072 - 16]
        cmp_top, cmp_total = small[:, 128:144], small[:, 144:160]
        a_prob = [flat[H_TOK][:, 512 * i:512 * i + 512] for i in range(2)]
        a_prob_t = [flat[H_TOK][:, 1024 + 512 * i:1536 + 512 * i] for i in range(2)]
        cmp_p = flat[H_TOK][:, 2048:2288]
        cmp_valid = flat[H_TOK][:, 2304:2544]
        rope = flat[H_TOK][:, 2560:3072].rearrange("p (a t) -> p a t", a=2)
        decay_table = [flat[r][:, at + 384 * i:at + 384 * i + 384] for r, at in ((H_TOK, 3072), (QA_CM_K4, 2048)) for i in range(2)]
        rope_tmp = [hall[:, CAT_T, 8:12], hall[:, CAT_T, 12:16]]
        ret_p = [flat[H_TOK][:, 512 * i:512 * i + 384] for i in range(2)]
        ret_o = [flat[H_TOK][:, 1024 + 512 * i:1536 + 512 * i].rearrange("p (t c) -> p t c", t=TT) for i in range(4)]
        ret_stats = [small[:, 160 + 12 * i:172 + 12 * i].rearrange("p (t s) -> p t s", t=TT) for i in range(2)]
        ret_mv = [small[:, 184 + 4 * i:188 + 4 * i].rearrange("p (t s) -> p t s", t=TT) for i in range(2)]
        ret_root = [small[:, 192 + 2 * i:194 + 2 * i] for i in range(2)]
        up = hall[:, 4:8].rearrange("p r a t -> p (r a) t")
        MIX_TOK, POST = 4, 3
        t5_table, t5_one = flat[KK][0:33, 0:1024].rearrange("p (h q) -> p h q", h=8), flat[KK][0:33, 1024:1920]
        t5_rows = flat[RR][:, 0:3072].rearrange("p (h m) -> p h m", h=8)
        SCORES = 16

        @block.sync
        def _(sp):
            stream = d["stream"]
            turns = d["slots"] // RING
            for j in range(RING):
                sp.dma_start(ring[:, j].rearrange("p a b -> p (a b)"), stream[j]).then_inc(slot_landed[j], 16)
            with sp.Fori(1, turns) as i:
                for j in range(RING):
                    sp.wait_ge(slots_used, i * RING + (j + 1 - RING))
                    sp.dma_start(ring[:, j].rearrange("p a b -> p (a b)"),
                                 stream[bass.ds(i * RING + j, 1)].rearrange("o p c -> (o p) c")).then_inc(slot_landed[j], 16)
            for s in range(turns * RING, d["slots"]):
                sp.wait_ge(slots_used, s + 1 - RING)
                sp.dma_start(ring[:, s % RING].rearrange("p a b -> p (a b)"), stream[s])\
                  .then_inc(slot_landed[s % RING], 16)

        @block.gpsimd
        def _(pool):
            for dst, src in ((flat[KK][0:33, 0:1024], d["t5_table"]), (t5_one, d["t5_one"])):
                pool.dma_start(dst, src).then_inc(t5_table_in, 16)
            for dst, src in ((flat[XT], d["x_channels"]), (con[:], d["resident"]),
                             (par[:].rearrange("p a b -> p (a b)"), d["params"])):
                pool.dma_start(dst, src).then_inc(x_in, 16)
            for dst, src in ((flat[VV][:, 0:2 * DT * LORA], d["lora1"]), (flat[KN][0:LORA, :], d["lora2"]),
                             (restart, d["restart"])):
                pool.dma_start(dst, src).then_inc(lora_in, 16)
            pool.wait_ge(t5_copied, 8)
            pool.dma_start(d["t5_scratch"].rearrange("h p m -> p h m"), t5_rows).then_inc(t5_stored, 16)
            pool.wait_ge(chunk_done, NCH)
            pool.dma_start(flat[X_TOK], d["x_tokens"]).then_inc(rows_in, 16)
            for i in range(2):
                pool.dma_start(token_rows(ROWS)[:, i], d["rows"][i].partition_broadcast(P)).then_inc(rows_in, 16)
            pool.wait_ge(tok_ready, 2)
            pool.dma_start(dist, d["dist"]).then_inc(diff_in, 16)
            pool.dma_start(flat[ROWS][:, 2304:2816], d["lambda"].partition_broadcast(P)).then_inc(diff_in, 16)
            pool.wait_ge(o_copied, SCORES)
            for i in range(2):
                pool.dma_start(token_rows(ROWS)[:, i], d["rows"][2 + i].partition_broadcast(P)).then_inc(rows_in, 16)
            pool.wait_ge(tr_done, 16)
            pool.wait_ge(t5_stored, 16)
            scratch = d["t5_scratch"]
            pool.dma_start(bias, bass.AP(scratch.tensor, 127, [[383, P], [P * 384, 8], [1, T]])).then_inc(nsa_in, 16)
            for dst, src in ((misc[:, 0:320], d["cmp_small"]), (misc[0:2 * NCMP, 320:576], d["cmp_b1"].partition_broadcast(2 * NCMP)),
                             (con[:, 256:640], d["gate_w"]), (flat[VR_GR], d["cmp_w1"][1])):
                pool.dma_start(dst, src).then_inc(nsa_in, 16)
            pool.wait_ge(tr_done, 24)
            pool.dma_start(flat[H_TOK], d["cmp_w1"][0]).then_inc(nsa_in, 16)
            pool.wait_ge(cmp_hid_done, 2)
            pool.dma_start(flat[H_TOK][:, 2560:3072], d["rope"]).then_inc(rope_in, 16)
            pool.dma_start(cmp_valid, d["valid"]).then_inc(rope_in, 16)
            for h in range(4):
                pool.dma_start(decay_table[h], d["decay"][:, 384 * h:384 * h + 384]).then_inc(ret_in, 16)
            pool.wait_ge(ret_turned, 4)
            pool.wait_ge(ret_score_ready, 4)
            for i in range(2):
                pool.dma_start(token_rows(POST)[:, i], d["rows"][4 + i].partition_broadcast(P)).then_inc(post_in, 16)
            for t in range(TT):
                pool.wait_ge(out_rows_ready, t + 1)
                pool.dma_start(d["out"][t * P:(t + 1) * P, :], token_rows(H_TOK)[:, t]).then_inc(out_stored, 16)
            pool.wait_ge(out_stored, 32)

        @block.tensor
        def _(pe):
            def panel(n, kind, act, ready=None, hook=None, i=0, slots=4, slot=None):
                if n >= 2:
                    pe.wait_ge(panel_evacuated[n % 2], (n - 2) // 2 + 1 + i)
                for q in range(slots):
                    s = (4 * n if slot is None else slot) + q
                    if ready:
                        ready(q)
                    pe.wait_ge(slot_landed[s % RING], i * (4 * slots) + 16 * (s // RING + 1))
                    slot_products(kind, act, s % RING, q, 2 * (n % 2), last=4 * slots - 1).then_inc(slots_used, 1)
                    if hook:
                        hook(q)

            def product(name, panels, kind, act, ready=None):
                with pe.Fori(0, panels // 2) as i:
                    for p in range(2):
                        panel(PANELS[name] + p, kind, act, ready=ready if p == 0 else None, i=i)

            def turned_tiles(v, q):
                pe.wait_ge(tr_copied_v, 4 * v + q + 1)
                pe.wait_ge(tr_copied_a, 4 * v + q + 1)

            def turn_rows(v, src):
                for u in range(8):
                    if u >= 4:
                        pe.wait_ge((tr_copied_v, tr_copied_a)[u % 2], 4 * v + (u - 4) // 2 + 1)
                    for a in range(2):
                        for t in range(TT):
                            c = (2 * u + a) * P
                            mm = pe.transpose(ps[:, 4 + u % 4, a * T + t * P:a * T + (t + 1) * P], src[:, t, c:c + P], ident)
                    mm.then_inc(tr_done, 1)

            pe.wait_ge(t5_table_in, 32)
            for h in range(8):
                if h >= 2:
                    pe.wait_ge(t5_copied, h - 1)
                pe.matmul(ps[:, 4 + h % 2, 0:384], t5_table[:, h, :], t5_one[:, 0:384], start=True, stop=True)\
                  .then_inc(t5_done, 1)
            for t in range(TT):
                for n in range(NCMP):
                    at = 384 + 224 + P * t - 16 * n
                    mm = pe.matmul(ps[:, 6, 15 * t + n:240:30], t5_one[:, at:at + P], t5_table[:, :, 0], start=True, stop=True)
            mm.then_inc(t5_done, 1)
            pe.wait_ge(t5_copied, 9)

            def slot_products(kind, act, r, q, bank, first=0, last=DT - 1):
                for a in range(4):
                    t = 4 * q + a
                    if kind == "W":
                        for c in range(4):
                            mm = pe.matmul(ps[:, bank + c // 2, (c % 2) * T:(c % 2 + 1) * T],
                                           ring[:, r, a, c * P:(c + 1) * P], act[:, t, :],
                                           start=(t == first and c % 2 == 0), stop=(t == last), skip_group_check=True)
                    else:
                        for c in range(TT):
                            mm = pe.matmul(ps[:, bank + c, :], act[:, t, c * P:(c + 1) * P], ring[:, r, a, :],
                                           start=(t == first), stop=(t == last))
                return mm

            pe.wait_ge(lora_in, 48)
            for m in range(2):
                for t in range(DT):
                    if t % 4 == 0:
                        pe.wait_ge(mix_ready, 4 * m + t // 4 + 1)
                    mm = pe.matmul(ps[0:LORA, 4 + m, 0:T], lora_w1[:, m, t, :], hall[:, MIX, t, :],
                                   start=(t == 0), stop=(t == DT - 1))
                    if t % 4 == 3:
                        mm.then_inc(lora_read, 1)
            pe.wait_ge(lora_hid_copied, 2)
            for u in range(8):
                if u >= 2:
                    pe.wait_ge(lora_up_copied, u - 1)
                for c in range(4):
                    j = 4 * (u % 4) + c
                    mm = pe.matmul(ps[:, 4 + 2 * (u % 2) + c // 2, (c % 2) * T:(c % 2 + 1) * T],
                                   lora_w2[:, u // 4, j * P:(j + 1) * P], lora_hid[:, u // 4, :], start=True, stop=True)
                mm.then_inc(lora_up_done, 1)

            def key_norms(g):
                pe.wait_ge(key_squared, g + 1)
                if g >= 2:
                    pe.wait_ge(key_norm_ready, g - 1)
                for b in range(2):
                    mm = pe.matmul(ps[:, 4 + 2 * (g % 2) + b, :], ones64, key_sq[g % 2][:, 2 * b:2 * b + 2, :],
                                   start=True, stop=True)
                mm.then_inc(key_norm_summed, 1)

            for m, name in enumerate(("k", "r", "v", "g")):
                for p in range(4):
                    hook = None
                    if name == "r" and p < 2:
                        hook = lambda q, p=p: key_norms(2 * p + q // 2) if q % 2 else None
                    panel(PANELS[name] + p, "W", hall[:, MIX], hook=hook,
                          ready=(lambda q, m=m: pe.wait_ge(mix_ready, 4 * (m + 2) + q + 1)) if p == 0 else None)

            def head_sums(w, src, count):
                pe.wait_ge(head_in_ready, count)
                for b in range(2):
                    mm = pe.matmul(ps[:, 2 * w + b, :], ones64, src[:, 8 * b:8 * b + 8, :], start=True, stop=True)
                mm.then_inc(head_sum_done, 1)

            for c in range(NCH):
                cs = slice(c * N, (c + 1) * N)
                if c == 0:
                    pe.wait_ge(key_group_done, 4)
                    pe.wait_ge(receptance_done, 4)
                    evacuated(pe, PANELS["g"] + 2)
                    evacuated(pe, PANELS["g"] + 3)
                else:
                    pe.wait_ge(chunk_done, c)
                for w, lhs in ((0, AA), (1, KK)):
                    for j, h in HEADS:
                        mm = pe.matmul(gram(w)[rows[h], j], hall[rows[h], lhs, j, cs], hall[rows[h], KN:KN + 2, j, cs],
                                       start=True, stop=True)
                    mm.then_inc(gram_done, 1)
                pe.wait_ge(gram_masked, 3 * c + 1)
                for j, h in HEADS:
                    mm = pe.matmul(wide(0)[rows[h], j], hall[rows[h], KN, j, cs], hall[rows[h], AA, j, cs],
                                   start=True, stop=True)
                mm.then_inc(gram_done, 1)
                for i in range(5):
                    if i == 0:
                        pe.wait_ge(gram_masked, 3 * c + 3)
                    else:
                        pe.wait_ge(merged, 9 * c + 2 * i - 1)
                    for j, h in HEADS:
                        mm = pe.matmul(wide(1)[rows[h], j], AT[rows[h], j], X[rows[h], j], start=True, stop=True)
                    mm.then_inc(z_done, 1)
                    pe.wait_ge(z_masked, 5 * c + i + 1)
                    if i:
                        pe.wait_ge(merged, 9 * c + 2 * i)
                    for j, h in HEADS:
                        mm = pe.matmul(wide(2)[rows[h], j], XTR[rows[h], j], Z[rows[h], j], start=True, stop=True)
                    mm.then_inc(merge_done, 1)
                    if i < 4:
                        for j, h in HEADS:
                            mm = pe.matmul(wide(3)[rows[h], j], Z[rows[h], j], XTR[rows[h], j], start=True, stop=True)
                        mm.then_inc(merge_done, 1)
                for w, src in ((0, AA), (1, KK), (2, VV)):
                    if w == 2:
                        pe.wait_ge(merged, 9 * c + 9)
                    for j, h in HEADS:
                        mm = pe.matmul(wide(w)[rows[h], j], hall[rows[h], src, j, cs], id64[rows[h], :],
                                       start=True, stop=True)
                    mm.then_inc(turned, 1)
                pe.wait_ge(turned_copied, 3 * c + 3)
                if c:
                    pe.wait_ge(state_ready, c)
                for j, h in HEADS:
                    if c:
                        pe.matmul(wide(3)[rows[h], j], hall[rows[h], KN, j, cs], ST[rows[h], j], start=True, stop=False)
                    mm = pe.matmul(wide(3)[rows[h], j], AAK[rows[h], j], VTOK[rows[h], j], start=(c == 0), stop=True)
                mm.then_inc(rhs_done, 1)
                pe.wait_ge(rhs_ready, c + 1)
                for j, h in HEADS:
                    mm = pe.matmul(wide(0)[rows[h], j], X[rows[h], j], RHS[rows[h], j], start=True, stop=True)
                mm.then_inc(u_done, 1)
                pe.wait_ge(u_ready, c + 1)
                for j, h in HEADS:
                    if c:
                        pe.matmul(wide(1)[rows[h], j], ST[rows[h], j], hall[rows[h], RR, j, cs], start=True, stop=False)
                    pe.matmul(wide(1)[rows[h], j], VTOK[rows[h], j], ARK[rows[h], j], start=(c == 0), stop=False)
                    mm = pe.matmul(wide(1)[rows[h], j], U[rows[h], j], ARB[rows[h], j], start=False, stop=True)
                mm.then_inc(y_done, 1)
                for j, h in HEADS:
                    pe.matmul(wide(2)[rows[h], j], BTOK[rows[h], j], U[rows[h], j], start=True, stop=False)
                    mm = pe.matmul(wide(2)[rows[h], j], KTOK[rows[h], j], VTOK[rows[h], j], start=False, stop=True)
                mm.then_inc(state_done, 1)
                head_sums(0, BON, 3 * c + 1)
                head_sums(3, YC, 3 * c + 2)
                head_sums(1, SQ, 3 * c + 3)
            pe.wait_ge(chunk_done, NCH)
            product("out0", 4, "X", hall[:, RR])
            pe.wait_ge(tok_ready, 2)
            turn_rows(0, token_rows(X_TOK))
            product("dk", 4, "W", hall[:, X_T], ready=lambda q: turned_tiles(0, q))
            product("dq", 4, "W", hall[:, X_T])
            product("dv", 4, "X", hall[:, X_T])

            def diff_scores(i):
                h, t = divmod(i, TT)
                if i >= 2:
                    pe.wait_ge(score_read, i - 1)
                for m in range(2):
                    mm = pe.matmul(ps[:, 4 + i % 2, m * T:m * T + P * (t + 1)], hall[:, DQ, 2 * h + m, t * P:(t + 1) * P],
                                   hall[:, DK, 2 * h + m, 0:P * (t + 1)], start=True, stop=True)
                mm.then_inc(score_done, 1)

            def diff_turn(i):
                pe.wait_ge(attn_ready, i + 1)
                if i:
                    pe.wait_ge(attn_copied, i)
                for k in range(i % TT + 1):
                    mm = pe.transpose(ps[:, 6, k * P:(k + 1) * P], prob[i % 2][:, k * P:(k + 1) * P], ident)
                mm.then_inc(attn_turned, 1)

            def diff_values(i):
                h, t = divmod(i, TT)
                pe.wait_ge(attn_copied, i + 1)
                if i:
                    pe.wait_ge(o_copied, i)
                for k in range(t + 1):
                    mm = pe.matmul(ps[:, 7, 0:T], prob_t[i % 2][:, k * P:(k + 1) * P], token_rows(DV)[:, k, h * T:(h + 1) * T],
                                   start=(k == 0), stop=(k == t))
                mm.then_inc(o_done, 1)

            def diff_hook(s):
                diff_scores(s)
                if s >= 1:
                    diff_turn(s - 1)
                if s >= 2:
                    diff_values(s - 2)

            evacuated(pe, PANELS["dq"] + 3)
            pe.wait_ge(tr_copied_v, 4)
            for p in range(4):
                panel(PANELS["dg"] + p, "X", hall[:, X_T], hook=lambda q, p=p: diff_hook(4 * p + q))
            diff_turn(15)
            diff_values(14)
            diff_values(15)
            pe.wait_ge(act_rows_ready, 1)
            turn_rows(1, token_rows(O_TOK))
            product("out1", 4, "X", hall[:, DK], ready=lambda q: turned_tiles(1, q))

            pe.wait_ge(act_rows_ready, 3)
            turn_rows(2, token_rows(H_TOK))
            panel(PANELS["cmp"], "W", hall[:, H_T], ready=lambda q: turned_tiles(2, q))
            panel(PANELS["kk"], "W", hall[:, H_T])

            def compress_hook(s):
                if s == 0:
                    pe.wait_ge(nsa_in, 96)
                    for a in range(DT):
                        mm = pe.matmul(ps[0:24, 6, 0:T], gate_w[:, a, :], hall[:, H_T, a, :], start=(a == 0), stop=(a == DT - 1))
                    mm.then_inc(gate_sum_done, 1)
                if s in (1, 2):
                    pe.wait_ge(blocks_ready, s)
                    for l in range(32):
                        mm = pe.matmul(ps[0:2 * NCMP, 3 + s, 0:P], windows[s - 1][:, l].rearrange("p g n -> p (g n)"),
                                       cmp_w1[s - 1][:, l, :], start=(l == 0), stop=(l == 31))
                    mm.then_inc(cmp_hid_done, 1)
                if s == 3:
                    pe.wait_ge(gate_sum_copied, 1)
                    for t in range(TT):
                        mm = pe.transpose(ps[:, 7, 24 * t:24 * t + 24], gate_sum[:, t * P:(t + 1) * P], ident[0:24, 0:24])
                    mm.then_inc(gate_turned, 1)
                if s == 4:
                    pe.wait_ge(cmp_hid_ready, 2)
                    for i in range(2):
                        mm = pe.transpose(ps[:, 6, 32 * i:32 * i + 30], cmp_hid[:, i, :], ident[0:30, 0:30])
                    mm.then_inc(cmp_hid_turned, 1)
                if s == 5:
                    pe.wait_ge(cmp_hid_copied, 1)
                    pe.matmul(ps[:, 4, 0:30], cmp_w2[:, 0, :], cmp_hid_t[:, 0, :], start=True, stop=True)
                    for g in range(2):
                        mm = pe.matmul(ps[0:NCMP, 5, g * P:(g + 1) * P], cmp_hid_t[:, 1, NCMP * g:NCMP * g + NCMP], cmp_w2[:, 1, :],
                                       start=True, stop=True)
                    mm.then_inc(cmp_made, 1)

            for p in range(2):
                panel(PANELS["kr"] + p, "W", hall[:, H_T], hook=lambda q, p=p: compress_hook(4 * p + q))
            for name in ("qr", "qa"):
                for p in range(2):
                    panel(PANELS[name] + p, "W", hall[:, H_T])

            def cmp_hook(s):
                if s == 1:
                    evacuated(pe, PANELS["qa"] + 1)
                    pe.wait_ge(cmp_copied, 2)
                    for i in range(SCORES):
                        h, t = divmod(i, TT)
                        mm = pe.matmul(ps[:, 4, NCMP * i:NCMP * i + NCMP], qa[:, h, t * P:(t + 1) * P],
                                       cmp_k[:, NCMP * (h // 4):NCMP * (h // 4) + NCMP], start=True, stop=True)
                    mm.then_inc(cmp_scored, 1)
                if s == 3:
                    pe.wait_ge(cmp_probs_ready, 1)
                    for i in range(SCORES):
                        mm = pe.transpose(ps[0:NCMP, 4 + i // 4, (i % 4) * P:(i % 4 + 1) * P],
                                          cmp_p[:, NCMP * i:NCMP * i + NCMP], ident)
                        if i % 4 == 3:
                            mm.then_inc(cmp_turned, 1)

            panel(PANELS["vv"], "X", hall[:, H_T], hook=cmp_hook)

            def nsa_scores(i):
                h, t = divmod(i, TT)
                if i >= 2:
                    pe.wait_ge(score_read, SCORES + i - 1)
                for b in range(2):
                    mm = pe.matmul(ps[:, 4 + i % 2, b * T:b * T + P * (t + 1)], qa[:, h, t * P:(t + 1) * P],
                                   k4[:, 2 * b + h // 4, 0:P * (t + 1)], start=True, stop=True)
                mm.then_inc(score_done, 1)

            def nsa_turn(i):
                pe.wait_ge(attn_ready, SCORES + i + 1)
                pe.wait_ge(attn_copied, SCORES + i)
                for b in range(2):
                    for k in range(i % TT + 1):
                        mm = pe.transpose(ps[:, 6, b * T + k * P:b * T + (k + 1) * P],
                                          a_prob[i % 2][:, b * T + k * P:b * T + (k + 1) * P], ident)
                mm.then_inc(attn_turned, 1)

            def nsa_values(i):
                h, t = divmod(i, TT)
                g = h // 4
                pe.wait_ge(attn_copied, SCORES + i + 1)
                pe.wait_ge(o_copied, SCORES + i)
                pe.matmul(ps[:, 7, 0:P], cmp_v[:, g, :], cmp_prob_t[:, i, :], start=True, stop=False)
                for b in range(2):
                    for k in range(t + 1):
                        mm = pe.matmul(ps[:, 7, 0:P], vv[:, k, (2 * b + g) * P:(2 * b + g + 1) * P],
                                       a_prob_t[i % 2][:, b * T + k * P:b * T + (k + 1) * P], start=False,
                                       stop=(b == 1 and k == t))
                mm.then_inc(o_done, 1)

            def nsa_hook(s):
                if s == 0:
                    pe.wait_ge(cmp_turned_copied, 4)
                    evacuated(pe, PANELS["vv"])
                nsa_scores(s)
                if s >= 1:
                    nsa_turn(s - 1)
                if s >= 2:
                    nsa_values(s - 2)

            for m, name in enumerate(("vr", "gr")):
                for p in range(2):
                    panel(PANELS[name] + p, "X", hall[:, H_T], hook=lambda q, p=p, m=m: nsa_hook(8 * m + 4 * p + q))
            nsa_turn(15)
            nsa_values(14)
            nsa_values(15)

            def ret_scores(h):
                if h >= 2:
                    pe.wait_ge(ret_score_ready, h - 1)
                for k, lo, at in ((0, 0, 0), (1, P, T)):
                    for a in range(2):
                        mm = pe.matmul(ps[:, 4 + h % 2, at:at + T - lo], kr[:, 2 * h + a, k * P:(k + 1) * P],
                                       qr[:, 2 * h + a, lo:T], start=(a == 0), stop=(a == 1))
                mm.then_inc(ret_score_done, 1)

            def ret_values(h):
                pe.wait_ge(ret_score_ready, h + 1)
                if h >= 2:
                    pe.wait_ge(ret_o_ready, h - 1)
                for t, k, at in ((0, 0, 0), (1, 0, P), (1, 1, T)):
                    mm = pe.matmul(ps[:, 6 + h % 2, t * T:(t + 1) * T], ret_p[h % 2][:, at:at + P], vr[:, k, h * T:(h + 1) * T],
                                   start=(k == 0), stop=(k == t))
                mm.then_inc(ret_o_done, 1)

            pe.wait_ge(score_read, 2 * SCORES)
            pe.wait_ge(attn_copied, 2 * SCORES)
            pe.wait_ge(o_copied, 2 * SCORES)
            pe.wait_ge(rope_ready, 2)
            evacuated(pe, PANELS["gr"])
            evacuated(pe, PANELS["gr"] + 1)
            ret_scores(0)
            ret_scores(1)
            ret_values(0)
            ret_scores(2)
            ret_values(1)
            ret_scores(3)
            ret_values(2)
            ret_values(3)
            for h in range(4):
                pe.wait_ge(ret_o_ready, h + 1)
                for a in range(2):
                    for t in range(TT):
                        mm = pe.transpose(ps[:, h, a * T + t * P:a * T + (t + 1) * P], ret_o[h][:, t, a * P:(a + 1) * P], ident)
                mm.then_inc(ret_turned, 1)
            pe.wait_ge(ret_turned_copied, 4)
            product("out2", 4, "X", hall[:, CAT_T])

            pe.wait_ge(act_rows_ready, 5)
            turn_rows(3, token_rows(H_TOK))
            product("up", 16, "W", hall[:, H_T], ready=lambda q: turned_tiles(3, q))
            pe.wait_ge(up_squared, 16)
            with pe.Fori(0, 2) as i:
                for p in range(2):
                    panel(PANELS["down"] + p, "X", up, i=i, slots=16, slot=4 * PANELS["down"] + 16 * p)

        @block.vector
        def _(dve):
            steps = [0]

            def then(ins):
                steps[0] += 1
                ins.then_inc(dve_step, 1)
                dve.wait_ge(dve_step, steps[0])

            for col, value in ((EPS_GN, GN_EPS), (EPS_LN, LN_EPS), (EPS_SUB, SUBLN_EPS), (EPS_6, EPS6)):
                ins = dve.memset(col, value)
            ins.then_inc(eps_ready, 1)

            def token_mix(m):
                for q in range(4):
                    s = slice(4 * q, 4 * q + 4)
                    if 1 <= m <= 2:
                        dve.wait_ge(lora_read, 4 * (m - 1) + q + 1)
                    elif m > 2:
                        computed(dve, 4 * (m - 3) + 3, q)
                    x, y = hall[:, XT, s], hall[:, MIX, s]
                    dve.tensor_tensor(y[:, :, 1:], x[:, :, 0:T - 1], x[:, :, 1:], ALU.subtract)
                    then(dve.tensor_scalar(y[:, :, 0:1], x[:, :, 0:1], -1.0, None, ALU.mult))
                    then(dve.tensor_tensor(y, y, over(pv(MIXES[m])[:, s], [P, 4, T]), ALU.mult))
                    dve.tensor_tensor(y, y, x, ALU.add).then_inc(mix_ready, 1)

            dve.wait_ge(x_in, 48)
            for m in range(3):
                token_mix(m)
            dve.wait_ge(lora_in, 48)
            for j in range(DT):
                if j % 4 == 0:
                    dve.wait_ge(lora_up_copied, j // 4 + 1)
                ins = dve.tensor_tensor_scan(hall[:, LD, j], restart, hall[:, LD, j], 0.0, ALU.mult, ALU.add)
                if j % 4 == 3:
                    ins.then_inc(decay_summed, 1)

            def key_raw(g):
                s = slice(4 * g, 4 * g + 4)
                evacuated(dve, PANELS["k"] + g)
                if g == 0:
                    dve.wait_ge(lora_up_copied, 8)
                dve.tensor_tensor(hall[:, KN, s], hall[:, KK, s], over(pv("k_k")[:, s], [P, 4, T]), ALU.mult)\
                   .then_inc(key_raw_ready, 1)

            def key_group(g):
                s = slice(4 * g, 4 * g + 4)
                sq, kn, a, k, ld = key_sq[g % 2], hall[:, KN, s], hall[:, AA, s], hall[:, KK, s], hall[:, LD, s]
                dve.wait_ge(key_norm_ready, g + 1)
                then(dve.tensor_scalar(sq, sq, 1e-12, None, ALU.max))
                then(dve.reciprocal(sq, sq))
                then(dve.tensor_tensor(kn, kn, sq, ALU.mult))
                then(dve.scalar_tensor_tensor(key_tmp, a, -1.0, over(pv("k_a")[:, s], [P, 4, T]), ALU.add, ALU.mult))
                then(dve.scalar_tensor_tensor(k, key_tmp, 1.0, k, ALU.add, ALU.mult))
                then(dve.tensor_tensor(a, a, kn, ALU.mult))
                dve.wait_ge(decay_exp_ready, g + 1)
                dve.tensor_tensor(a, a, key_exp, ALU.mult)
                dve.tensor_tensor(k, k, key_exp, ALU.mult)
                chunks = lambda ap: ap.rearrange("p a (c t) -> p (a c) t", t=N)
                dve.tensor_tensor(chunks(kn)[:, :, 1:], chunks(kn)[:, :, 1:], chunks(ld)[:, :, 0:N - 1], ALU.mult)
                dve.tensor_copy(wl[:, s], ld.rearrange("p a (c t) -> p a c t", t=N)[:, :, :, N - 1])\
                   .then_inc(key_group_done, 1)

            for g in range(3):
                key_raw(g)
            token_mix(3)
            key_raw(3)
            for g in range(4):
                key_group(g)
            token_mix(4)
            dve.wait_ge(key_group_done, 4)
            for g in range(4):
                s = slice(4 * g, 4 * g + 4)
                evacuated(dve, PANELS["r"] + g)
                dve.tensor_tensor(hall[:, RR, s], hall[:, RR, s], hall[:, LD, s], ALU.mult).then_inc(receptance_done, 1)
            token_mix(5)

            computed(dve, PANELS["g"] + 3)
            for c in range(NCH):
                cs = slice(c * N, (c + 1) * N)
                if c:
                    dve.wait_ge(chunk_done, c)
                dve.wait_ge(gram_done, 3 * c + 1)
                then(dve.tensor_tensor(X, gram(0)[:, :, 0], mask(C_NM1), ALU.mult))
                dve.tensor_tensor(X, X, mask(C_ID64), ALU.add)
                dve.tensor_tensor(ARB, gram(0)[:, :, 1], mask(C_UI), ALU.mult).then_inc(gram_masked, 1)
                dve.wait_ge(gram_done, 3 * c + 2)
                dve.tensor_tensor(AAK, gram(1)[:, :, 0], mask(C_U), ALU.mult)
                dve.tensor_tensor(ARK, gram(1)[:, :, 1], mask(C_UI), ALU.mult).then_inc(gram_masked, 1)
                dve.wait_ge(gram_done, 3 * c + 3)
                then(dve.tensor_tensor(AT, wide(0), mask(C_L), ALU.mult))
                then(dve.tensor_tensor(XTR, AT, mask(C_NM1T), ALU.mult))
                dve.tensor_tensor(XTR, XTR, mask(C_ID64), ALU.add).then_inc(gram_masked, 1)
                dve.wait_ge(gram_masked, 3 * c + 3)
                for i in range(5):
                    dve.wait_ge(z_done, 5 * c + i + 1)
                    dve.tensor_tensor(Z, wide(1), mask(C_MB + 64 * i), ALU.mult).then_inc(z_masked, 1)
                    if i:
                        dve.wait_ge(merged, 9 * c + 2 * i)
                    dve.wait_ge(merge_done, 9 * c + 2 * i + 1)
                    dve.tensor_tensor(X, X, wide(2), ALU.subtract).then_inc(merged, 1)
                    if i < 4:
                        dve.wait_ge(merge_done, 9 * c + 2 * i + 2)
                        dve.tensor_tensor(XTR, XTR, wide(3), ALU.subtract).then_inc(merged, 1)
                dve.wait_ge(rhs_done, c + 1)
                then(dve.tensor_tensor(BON, hall[:, RR, :, cs], hall[:, KK, :, cs], ALU.mult))
                dve.tensor_tensor(BON, BON, over(pv("r_k"), [P, DT, N]), ALU.mult).then_inc(head_in_ready, 1)
                dve.wait_ge(state_done, c + 1)
                decay = over(wl[:, :, c], [P, DT, N])
                if c == 0:
                    dve.tensor_tensor(ST, wide(2), decay, ALU.mult).then_inc(state_ready, 1)
                else:
                    then(dve.tensor_tensor(ST, wide(2), ST, ALU.add))
                    dve.tensor_tensor(ST, ST, decay, ALU.mult).then_inc(state_ready, 1)
                dve.wait_ge(state_ready, c + 1)
                dve.wait_ge(head_sum_done, 3 * c + 1)
                then(dve.tensor_tensor(BON, wide(0), hall[:, VV, :, cs], ALU.mult))
                dve.wait_ge(head_sum_done, 3 * c + 2)
                dve.scalar_tensor_tensor(YC, wide(3), -1.0 / N, YC, ALU.mult, ALU.add).then_inc(y_centred, 1)
                dve.wait_ge(y_centred, c + 1)
                dve.wait_ge(head_root_ready, c + 1)
                then(dve.reciprocal(SQ, SQ))
                then(dve.tensor_tensor(YC, YC, SQ, ALU.mult))
                then(dve.tensor_tensor(YC, YC, over(pv("gn_g"), [P, DT, N]), ALU.mult))
                then(dve.tensor_tensor(YC, YC, over(pv("gn_b"), [P, DT, N]), ALU.add))
                then(dve.tensor_tensor(YC, YC, BON, ALU.add))
                dve.tensor_tensor(hall[:, RR, :, cs], YC, hall[:, LD, :, cs], ALU.mult).then_inc(chunk_done, 1)

            def out_rows(name, m):
                z = token_rows(X_TOK)
                dve.wait_ge(rows_in, 48 if m == 0 else 80)
                for p in range(4):
                    n, c = PANELS[name] + p, slice(512 * p, 512 * p + 512)
                    computed(dve, n)
                    for t in range(TT):
                        ins = dve.scalar_tensor_tensor(z[:, t, c], z[:, t, c], ALPHA, ps[:, 2 * (n % 2) + t, :], ALU.mult, ALU.add)
                    ins.then_inc(panel_evacuated[n % 2], 1)
                    evacuated(dve, n)
                    for t in range(TT):
                        ins = dve.bn_stats(stats[:, t, p, :], z[:, t, c])
                then(ins)
                for t in range(TT):
                    ins = dve.bn_aggr(mean_var[:, t, :], stats[:, t])
                ins.then_inc(ln_var_ready, 1)
                dve.wait_ge(ln_root_ready, m + 1)
                then(dve.reciprocal(root, root))
                for t in range(TT):
                    then(dve.tensor_scalar(z[:, t], z[:, t], mean_var[:, t, 0:1], root[:, t:t + 1], ALU.subtract, ALU.mult))
                    then(dve.tensor_tensor(z[:, t], z[:, t], token_rows(ROWS)[:, 0], ALU.mult))
                    dve.tensor_tensor(z[:, t], z[:, t], token_rows(ROWS)[:, 1], ALU.add).then_inc(tok_ready, 1)

            def copy_turned(v, dst, scale=None):
                for u in range(0, 8, 2):
                    dve.wait_ge(tr_done, 8 * v + u + 1)
                    src = ps[:, 4 + u % 4, :].rearrange("p (a t) -> p a t", a=2)
                    if scale is None:
                        dve.tensor_copy(dst[:, 2 * u:2 * u + 2, :], src).then_inc(tr_copied_v, 1)
                    else:
                        dve.tensor_tensor(dst[:, 2 * u:2 * u + 2, :], src, over(pv(scale)[:, 2 * u:2 * u + 2], [P, 2, T]), ALU.mult)\
                           .then_inc(tr_copied_v, 1)

            out_rows("out0", 0)
            copy_turned(0, hall[:, X_T])

            dve.wait_ge(diff_in, 32)
            then(dve.tensor_tensor(lam_tmp, lam_rows[:, 0:4:2, :], lam_rows[:, 1:4:2, :], ALU.mult))
            dve.tensor_reduce(lam_sum, lam_tmp, AX.X, ALU.add).then_inc(lam_parts, 1)
            dve.wait_ge(lam_exp, 1)
            then(dve.tensor_tensor(lam, lam_sum[:, 1:2], lam_sum[:, 0:1], ALU.subtract))
            then(dve.tensor_scalar(neg_lam, lam, -LAM_INIT, None, ALU.add))

            def diff_logits(i):
                h, t = divmod(i, TT)
                w = P * (t + 1)
                pr = prob[i % 2].rearrange("p (m k) -> p m k", m=2)[:, :, 0:w]
                slope = 2.0 ** (-(8.0 / DH) * (h + 1))
                dve.wait_ge(score_done, i + 1)
                if i >= 2:
                    dve.wait_ge(attn_turned, i - 1)
                dd = dist[:, T - w:T].unsqueeze(1).broadcast_to([P, 2, w])
                dve.scalar_tensor_tensor(pr, dd, -slope / D_SCALE, ps[:, 4 + i % 2, :].rearrange("p (m k) -> p m k", m=2)[:, :, 0:w],
                                         ALU.mult, ALU.add).then_inc(score_read, 1)
                dve.wait_ge(score_read, i + 1)
                then(dve.tensor_reduce(top[i % 2], pr, AX.X, ALU.max))
                dve.tensor_scalar(top[i % 2], top[i % 2], -D_SCALE, None, ALU.mult).then_inc(score_max, 1)

            def diff_weights(i):
                t = i % TT
                w = P * (t + 1)
                pr, r = prob[i % 2], share[i % 2]
                dve.wait_ge(score_exp, i + 1)
                then(dve.reciprocal(r, total[i % 2]))
                then(dve.tensor_tensor(r[:, 1:2], r[:, 1:2], neg_lam, ALU.mult))
                then(dve.tensor_scalar(pr[:, T:T + w], pr[:, T:T + w], r[:, 1:2], None, ALU.mult))
                dve.scalar_tensor_tensor(pr[:, 0:w], pr[:, 0:w], r[:, 0:1], pr[:, T:T + w], ALU.mult, ALU.add)\
                   .then_inc(attn_ready, 1)

            for i in range(SCORES + 1):
                if i < SCORES:
                    diff_logits(i)
                if i:
                    diff_weights(i - 1)
            dve.wait_ge(squares_summed, 1)
            then(dve.reciprocal(o_squares, o_squares))
            then(dve.tensor_scalar(o_squares, o_squares, 1.0 - LAM_INIT, None, ALU.mult))
            evacuated(dve, PANELS["dg"] + 2)
            evacuated(dve, PANELS["dg"] + 3)
            for i in range(SCORES):
                h, t = divmod(i, TT)
                o, g = (token_rows(r)[:, t, h * T:(h + 1) * T] for r in (O_TOK, DG))
                ins = dve.scalar_tensor_tensor(o, o, o_squares[:, i:i + 1], g, ALU.mult, ALU.mult)
            ins.then_inc(act_rows_ready, 1)
            copy_turned(1, hall[:, DK], "subln")
            out_rows("out1", 1)

            def unit_rows(k, src, dst):
                dve.wait_ge(post_root_ready, k)
                then(dve.reciprocal(row_root, row_root))
                for t in range(TT):
                    dve.tensor_scalar(token_rows(dst)[:, t], token_rows(src)[:, t], row_root[:, t:t + 1], None, ALU.mult)\
                       .then_inc(act_rows_ready, 1)

            dve.wait_ge(tok_ready, 4)
            unit_rows(1, X_TOK, H_TOK)
            copy_turned(2, hall[:, H_T], "mix_pre")

            evacuated(dve, PANELS["cmp"])
            dve.wait_ge(nsa_in, 96)
            for i in range(2):
                for g in range(2):
                    tile = cm[:, 2 * i + g, :]
                    view = bass.AP(tile.tensor, tile.offset, [tile.ap[0], [1, 32], [16, NCMP]])
                    ins = dve.tensor_tensor(windows[i][:, :, g, :], view, over(block_pe[:, 32 * i:32 * i + 32], [P, 32, NCMP]), ALU.add)
                ins.then_inc(blocks_ready, 1)
            for i in range(2):
                dve.wait_ge(cmp_hid_done, i + 1)
                dve.tensor_tensor(cmp_hid[:, i, :], ps[0:2 * NCMP, 4 + i, 0:P], cmp_b1[:, i, :], ALU.add).then_inc(cmp_step, 1)
            dve.wait_ge(cmp_hid_turned, 1)
            dve.tensor_copy(cmp_hid_t, ps[:, 6, 0:64].rearrange("p (a b) -> p a b", a=2)[:, :, 0:30]).then_inc(cmp_hid_copied, 1)
            dve.wait_ge(cmp_made, 1)
            dve.tensor_copy(cmp_k, ps[:, 4, 0:30]).then_inc(cmp_copied, 1)
            dve.tensor_copy(cmp_v, ps[0:NCMP, 5, 0:2 * P].rearrange("p (g c) -> p g c", g=2)).then_inc(cmp_copied, 1)

            dve.wait_ge(rope_in, 32)
            for x, name in ((kr, "kr"), (qr, "qr")):
                evacuated(dve, PANELS[name])
                evacuated(dve, PANELS[name] + 1)
                x1, x2 = x[:, 0:8:2, :], x[:, 1:8:2, :]
                cos, sin = (rope[:, i, :].unsqueeze(1).broadcast_to([P, 4, T]) for i in range(2))
                dve.tensor_tensor(rope_tmp[0], x1, sin, ALU.mult)
                then(dve.tensor_tensor(rope_tmp[1], x2, sin, ALU.mult))
                dve.tensor_tensor(x1, x1, cos, ALU.mult)
                then(dve.tensor_tensor(x2, x2, cos, ALU.mult))
                dve.tensor_tensor(x1, x1, rope_tmp[1], ALU.subtract)
                dve.tensor_tensor(x2, x2, rope_tmp[0], ALU.add).then_inc(rope_ready, 1)
                dve.wait_ge(rope_ready, 1 if name == "kr" else 2)

            dve.wait_ge(t5_copied, 9)
            dve.wait_ge(cmp_scored, 1)
            cmp_view = cmp_p.rearrange("p (i n) -> p i n", n=NCMP)
            then(dve.scalar_tensor_tensor(cmp_p, ps[:, 4, 0:SCORES * NCMP], A_SCALE, cmp_bias, ALU.mult, ALU.add))
            then(dve.tensor_reduce(cmp_top, cmp_view, AX.X, ALU.max))
            dve.tensor_tensor(cmp_view, cmp_view, over(cmp_top, [P, SCORES, NCMP]), ALU.subtract).then_inc(cmp_centred, 1)
            dve.wait_ge(cmp_exp, 1)
            then(dve.tensor_reduce(cmp_total, cmp_view, AX.X, ALU.add))
            then(dve.reciprocal(cmp_total, cmp_total))
            dve.wait_ge(gates_ready, 1)
            gate = gates.rearrange("p t (h b) -> p h t b", b=3)
            then(dve.tensor_tensor(cmp_total.rearrange("p (h t) -> p h t", t=TT), cmp_total.rearrange("p (h t) -> p h t", t=TT),
                                   gate[:, :, :, 0], ALU.mult))
            then(dve.tensor_tensor(cmp_p, cmp_p, cmp_valid, ALU.mult))
            dve.tensor_tensor(cmp_view, cmp_view, over(cmp_total, [P, SCORES, NCMP]), ALU.mult).then_inc(cmp_probs_ready, 1)

            def nsa_logits(i):
                h, t = divmod(i, TT)
                w = P * (t + 1)
                pr = a_prob[i % 2].rearrange("p (m k) -> p m k", m=2)[:, :, 0:w]
                dve.wait_ge(score_done, SCORES + i + 1)
                if i >= 2:
                    dve.wait_ge(attn_turned, SCORES + i - 1)
                bb = bias[:, h, T - w:T].unsqueeze(1).broadcast_to([P, 2, w])
                dve.scalar_tensor_tensor(pr, ps[:, 4 + i % 2, :].rearrange("p (m k) -> p m k", m=2)[:, :, 0:w], A_SCALE, bb,
                                         ALU.mult, ALU.add).then_inc(score_read, 1)
                dve.wait_ge(score_read, SCORES + i + 1)
                then(dve.tensor_reduce(top[i % 2], pr, AX.X, ALU.max))
                dve.tensor_scalar(top[i % 2], top[i % 2], -1.0, None, ALU.mult).then_inc(score_max, 1)

            def nsa_weights(i):
                h, t = divmod(i, TT)
                w = P * (t + 1)
                r = share[i % 2]
                dve.wait_ge(score_exp, SCORES + i + 1)
                then(dve.reciprocal(r, total[i % 2]))
                then(dve.tensor_tensor(r, r, gates[:, t, 3 * h + 1:3 * h + 3], ALU.mult))
                for b in range(2):
                    pr = a_prob[i % 2][:, b * T:b * T + w]
                    ins = dve.tensor_scalar(pr, pr, r[:, b:b + 1], None, ALU.mult)
                ins.then_inc(attn_ready, 1)

            for i in range(SCORES + 1):
                if i < SCORES:
                    nsa_logits(i)
                if i:
                    nsa_weights(i - 1)

            dve.wait_ge(ret_in, 64)
            evacuated(dve, PANELS["gr"])
            evacuated(dve, PANELS["gr"] + 1)

            def ret_weights(h):
                dve.wait_ge(ret_score_done, h + 1)
                if h >= 2:
                    dve.wait_ge(ret_o_done, h - 1)
                dve.tensor_tensor(ret_p[h % 2], ps[:, 4 + h % 2, 0:384], decay_table[h], ALU.mult).then_inc(ret_score_ready, 1)

            def ret_norm(h):
                dve.wait_ge(ret_o_done, h + 1)
                o = ps[:, 6 + h % 2, :].rearrange("p (t c) -> p t c", t=TT)
                st, mv, rt = ret_stats[h % 2], ret_mv[h % 2], ret_root[h % 2]
                for t in range(TT):
                    ins = dve.bn_stats(st[:, t, :], o[:, t, :])
                then(ins)
                for t in range(TT):
                    ins = dve.bn_aggr(mv[:, t, :], st[:, t, :])
                ins.then_inc(ret_var_ready, 1)
                dve.wait_ge(ret_root_ready, h + 1)
                then(dve.reciprocal(rt, rt))
                for t in range(TT):
                    ins = dve.tensor_scalar(ret_o[h][:, t, :], o[:, t, :], mv[:, t, 0:1], rt[:, t:t + 1], ALU.subtract, ALU.mult)
                then(ins)
                dve.tensor_tensor(ret_o[h], ret_o[h], gr[:, :, h * T:(h + 1) * T], ALU.mult).then_inc(ret_o_ready, 1)

            ret_weights(0)
            ret_weights(1)
            ret_norm(0)
            ret_weights(2)
            ret_norm(1)
            ret_weights(3)
            ret_norm(2)
            ret_norm(3)

            def add_rows(k, src, row, dst, done):
                dve.wait_ge(post_root_ready, k)
                dve.wait_ge(post_in, 32)
                then(dve.reciprocal(row_root, row_root))
                for t in range(TT):
                    y = token_rows(src)[:, t]
                    then(dve.scalar_tensor_tensor(y, y, row_root[:, t:t + 1], token_rows(POST)[:, row], ALU.mult, ALU.mult))
                    dve.tensor_tensor(token_rows(dst)[:, t], y, token_rows(X_TOK)[:, t], ALU.add).then_inc(done, 1)

            add_rows(2, MIX_TOK, 0, X_TOK, post_rows_ready)
            dve.wait_ge(post_rows_ready, 2)
            unit_rows(3, X_TOK, H_TOK)
            copy_turned(3, hall[:, H_T], "mlp_pre")
            with dve.Fori(0, 8) as i:
                for p in range(2):
                    n = PANELS["up"] + p
                    dve.wait_ge(slots_used, i * 8 + 4 * (n + 1))
                    four = up[:, bass.ds(i * 8 + 4 * p, 4), :]
                    dve.tensor_scalar(four, ps[:, 2 * (n % 2):2 * (n % 2) + 2, :].rearrange("p b (a t) -> p (b a) t", a=2),
                                      0.0, None, ALU.max).then_inc(panel_evacuated[n % 2], 1)
                    dve.wait_ge(panel_evacuated[n % 2], i + (n // 2 + 1))
                    dve.tensor_tensor(four, four, four, ALU.mult).then_inc(up_squared, 1)
            add_rows(4, H_TOK, 1, H_TOK, out_rows_ready)

        @block.scalar
        def _(act):
            steps = [0]

            def then(ins):
                steps[0] += 1
                ins.then_inc(act_step, 1)
                act.wait_ge(act_step, steps[0])

            def evacuate(n, dst, func=ACT.Copy):
                computed(act, n)
                for b in range(2):
                    ins = act.activation(dst[:, 2 * b:2 * b + 2, :], ps[:, 2 * (n % 2) + b, :].rearrange("p (a t) -> p a t", a=2), func)
                ins.then_inc(panel_evacuated[n % 2], 1)

            for h in range(8):
                act.wait_ge(t5_done, h + 1)
                act.activation(t5_rows[:, h, :], ps[:, 4 + h % 2, 0:384], ACT.Copy).then_inc(t5_copied, 1)
            act.wait_ge(t5_done, 9)
            act.activation(cmp_bias, ps[:, 6, 0:240], ACT.Copy).then_inc(t5_copied, 1)
            act.wait_ge(lora_read, 4)
            act.activation(lora_hid[:, 0], ps[0:LORA, 4, 0:T], ACT.Tanh).then_inc(lora_hid_copied, 1)
            act.wait_ge(lora_read, 8)
            act.activation(lora_hid[:, 1], ps[0:LORA, 5, 0:T], ACT.Copy).then_inc(lora_hid_copied, 1)
            for u in range(8):
                act.wait_ge(lora_up_done, u + 1)
                for c in range(4):
                    j = 4 * (u % 4) + c
                    ins = act.activation(hall[:, (LD, AA)[u // 4], j], ps[:, 4 + 2 * (u % 2) + c // 2, (c % 2) * T:(c % 2 + 1) * T],
                                         ACT.Sigmoid, bias=pv(("w0", "a0")[u // 4])[:, j:j + 1])
                ins.then_inc(lora_up_copied, 1)
            for p in range(4):
                evacuate(PANELS["k"] + p, hall[:, KK, 4 * p:4 * p + 4])

            def square_keys(g):
                act.wait_ge(key_raw_ready, g + 1)
                if g >= 2:
                    act.wait_ge(key_group_done, g - 1)
                act.activation(key_sq[g % 2], hall[:, KN, 4 * g:4 * g + 4], ACT.Square).then_inc(key_squared, 1)

            def key_roots(g):
                act.wait_ge(key_norm_summed, g + 1)
                act.activation(key_sq[g % 2], ps[:, 4 + 2 * (g % 2):6 + 2 * (g % 2), :].rearrange("p b (a t) -> p (b a) t", a=2),
                               ACT.Sqrt).then_inc(key_norm_ready, 1)
                act.wait_ge(decay_summed, g + 1)
                if g >= 1:
                    act.wait_ge(key_group_done, g)
                ld = hall[:, LD, 4 * g:4 * g + 4]
                then(act.activation(key_exp, ld, ACT.Exp, scale=-DECAY))
                act.activation(ld, ld, ACT.Exp, scale=DECAY).then_inc(decay_exp_ready, 1)

            square_keys(0)
            square_keys(1)
            key_roots(0)
            key_roots(1)
            act.wait_ge(t5_stored, 16)
            evacuate(PANELS["r"], hall[:, RR, 0:4])
            square_keys(2)
            square_keys(3)
            key_roots(2)
            key_roots(3)
            for p in range(1, 4):
                evacuate(PANELS["r"] + p, hall[:, RR, 4 * p:4 * p + 4])
            act.wait_ge(key_group_done, 4)
            for p in range(4):
                evacuate(PANELS["v"] + p, hall[:, VV, 4 * p:4 * p + 4])
            act.wait_ge(receptance_done, 4)
            for p in range(4):
                evacuate(PANELS["g"] + p, hall[:, LD, 4 * p:4 * p + 4], ACT.Silu)
            act.wait_ge(eps_ready, 1)
            for c in range(NCH):
                for w, dst in enumerate((BTOK, KTOK, VTOK)):
                    act.wait_ge(turned, 3 * c + w + 1)
                    act.activation(dst, wide(w), ACT.Copy).then_inc(turned_copied, 1)
                act.wait_ge(rhs_done, c + 1)
                act.activation(RHS, wide(3), ACT.Copy, scale=-1.0).then_inc(rhs_ready, 1)
                act.wait_ge(u_done, c + 1)
                act.activation(U, wide(0), ACT.Copy).then_inc(u_ready, 1)
                act.wait_ge(y_done, c + 1)
                act.wait_ge(head_in_ready, 3 * c + 1)
                act.activation(YC, wide(1), ACT.Copy).then_inc(head_in_ready, 1)
                act.wait_ge(y_centred, c + 1)
                act.activation(SQ, YC, ACT.Square).then_inc(head_in_ready, 1)
                act.wait_ge(head_sum_done, 3 * c + 3)
                act.activation(SQ, wide(1), ACT.Sqrt, scale=1.0 / N, bias=EPS_GN).then_inc(head_root_ready, 1)

            def copy_turned(v, dst, scale=None):
                for u in range(1, 8, 2):
                    act.wait_ge(tr_done, 8 * v + u + 1)
                    src = ps[:, 4 + u % 4, :].rearrange("p (a t) -> p a t", a=2)
                    if scale is None:
                        ins = act.activation(dst[:, 2 * u:2 * u + 2, :], src, ACT.Copy)
                    else:
                        for a in range(2):
                            ins = act.activation(dst[:, 2 * u + a, :], src[:, a, :], ACT.Copy, scale=pv(scale)[:, 2 * u + a:2 * u + a + 1])
                    ins.then_inc(tr_copied_a, 1)

            def evacuate_rows(n, dst, func=ACT.Copy):
                computed(act, n)
                for t in range(TT):
                    ins = act.activation(dst[:, t, :], ps[:, 2 * (n % 2) + t, :], func)
                ins.then_inc(panel_evacuated[n % 2], 1)

            def norm_root(m):
                act.wait_ge(ln_var_ready, m + 1)
                act.activation(root, mean_var[:, :, 1], ACT.Sqrt, bias=EPS_LN).then_inc(ln_root_ready, 1)

            norm_root(0)
            copy_turned(0, hall[:, X_T])
            for p in range(4):
                evacuate(PANELS["dk"] + p, hall[:, DK, 4 * p:4 * p + 4])
            for p in range(4):
                evacuate(PANELS["dq"] + p, hall[:, DQ, 4 * p:4 * p + 4])
            for p in range(4):
                evacuate_rows(PANELS["dv"] + p, token_rows(DV)[:, :, 512 * p:512 * p + 512])
            act.wait_ge(lam_parts, 1)
            act.activation(lam_sum, lam_sum, ACT.Exp).then_inc(lam_exp, 1)

            def diff_exp(i):
                w = P * (i % TT + 1)
                act.wait_ge(score_max, i + 1)
                for m in range(2):
                    pr = prob[i % 2][:, m * T:m * T + w]
                    ins = act.activation(pr, pr, ACT.Exp, bias=top[i % 2][:, m:m + 1], scale=D_SCALE, accum_out=total[i % 2][:, m:m + 1])
                ins.then_inc(score_exp, 1)

            def diff_copy_attn(i):
                w = P * (i % TT + 1)
                act.wait_ge(attn_turned, i + 1)
                if i >= 2:
                    act.wait_ge(o_done, i - 1)
                act.activation(prob_t[i % 2][:, 0:w], ps[:, 6, 0:w], ACT.Copy).then_inc(attn_copied, 1)

            def diff_copy_o(i):
                h, t = divmod(i, TT)
                act.wait_ge(o_done, i + 1)
                act.activation(junk, ps[:, 7, 0:T], ACT.Square, accum_out=o_squares[:, i:i + 1])
                act.activation(token_rows(O_TOK)[:, t, h * T:(h + 1) * T], ps[:, 7, 0:T], ACT.Copy).then_inc(o_copied, 1)

            for s in range(SCORES + 2):
                if s % 4 == 3 and s < SCORES:
                    p = s // 4
                    evacuate_rows(PANELS["dg"] + p, token_rows(DG)[:, :, 512 * p:512 * p + 512], ACT.Silu)
                if s < SCORES:
                    diff_exp(s)
                if 1 <= s <= SCORES:
                    diff_copy_attn(s - 1)
                if s >= 2:
                    diff_copy_o(s - 2)
            act.wait_ge(o_copied, SCORES)
            act.activation(o_squares, o_squares, ACT.Sqrt, scale=1.0 / T, bias=EPS_SUB).then_inc(squares_summed, 1)
            copy_turned(1, hall[:, DK], "subln")
            norm_root(1)

            def row_rms(src, ready, dump):
                for t in range(TT):
                    act.wait_ge(ready[0], ready[1] + t)
                    ins = act.activation(token_rows(dump)[:, t], token_rows(src)[:, t], ACT.Square, accum_out=row_squares[:, t, 0:1])
                then(ins)
                act.activation(row_root, row_squares[:, :, 0], ACT.Sqrt, scale=1.0 / D, bias=EPS_6).then_inc(post_root_ready, 1)

            row_rms(X_TOK, (tok_ready, 3), DG)
            copy_turned(2, hall[:, H_T], "mix_pre")
            evacuate(PANELS["cmp"], cm)
            evacuate(PANELS["kk"], k4)
            act.wait_ge(gate_sum_done, 1)
            act.activation(gate_sum, ps[0:24, 6, 0:T], ACT.Copy).then_inc(gate_sum_copied, 1)
            for i in range(2):
                act.wait_ge(cmp_step, i + 1)
                act.activation(cmp_hid[:, i, :], cmp_hid[:, i, :], ACT.Gelu_apprx_tanh).then_inc(cmp_hid_ready, 1)
            act.wait_ge(gate_turned, 1)
            act.activation(gates, ps[:, 7, 0:48].rearrange("p (t b) -> p t b", t=TT), ACT.Sigmoid).then_inc(gates_ready, 1)
            for name, dst in (("kr", kr), ("qr", qr), ("qa", qa)):
                for p in range(2):
                    evacuate(PANELS[name] + p, dst[:, 4 * p:4 * p + 4])
            act.wait_ge(cmp_centred, 1)
            act.activation(cmp_p, cmp_p, ACT.Exp).then_inc(cmp_exp, 1)
            for i in range(4):
                act.wait_ge(cmp_turned, i + 1)
                act.activation(cmp_prob_t[:, 4 * i:4 * i + 4, :], ps[0:NCMP, 4 + i, :].rearrange("p (i q) -> p i q", i=4), ACT.Copy)\
                   .then_inc(cmp_turned_copied, 1)
            evacuate_rows(PANELS["vv"], vv)

            def nsa_exp(i):
                w = P * (i % TT + 1)
                act.wait_ge(score_max, SCORES + i + 1)
                for m in range(2):
                    pr = a_prob[i % 2][:, m * T:m * T + w]
                    ins = act.activation(pr, pr, ACT.Exp, bias=top[i % 2][:, m:m + 1], accum_out=total[i % 2][:, m:m + 1])
                ins.then_inc(score_exp, 1)

            def nsa_copy_attn(i):
                w = P * (i % TT + 1)
                act.wait_ge(attn_turned, SCORES + i + 1)
                if i >= 2:
                    act.wait_ge(o_done, SCORES + i - 1)
                view = lambda ap: ap.rearrange("p (m k) -> p m k", m=2)[:, :, 0:w]
                act.activation(view(a_prob_t[i % 2]), view(ps[:, 6, :]), ACT.Copy).then_inc(attn_copied, 1)

            def nsa_copy_o(i):
                h, t = divmod(i, TT)
                act.wait_ge(o_done, SCORES + i + 1)
                act.activation(hall[:, CAT_T, h, t * P:(t + 1) * P], ps[:, 7, 0:P], ACT.Copy).then_inc(o_copied, 1)

            act.wait_ge(rope_ready, 2)
            for s in range(SCORES + 2):
                if s % 4 == 3 and s < SCORES:
                    p = (s // 4) % 2
                    evacuate_rows(PANELS[("vr", "gr")[s // 8]] + p, (vr, gr)[s // 8][:, :, 512 * p:512 * p + 512],
                                  (ACT.Copy, ACT.Silu)[s // 8])
                if s < SCORES:
                    nsa_exp(s)
                if 1 <= s <= SCORES:
                    nsa_copy_attn(s - 1)
                if s >= 2:
                    nsa_copy_o(s - 2)
            for h in range(4):
                act.wait_ge(ret_var_ready, h + 1)
                act.activation(ret_root[h % 2], ret_mv[h % 2][:, :, 1], ACT.Sqrt, bias=EPS_6).then_inc(ret_root_ready, 1)
            for h in range(4):
                act.wait_ge(ret_turned, h + 1)
                act.activation(hall[:, CAT_T, 8 + 2 * h:10 + 2 * h, :], ps[:, h, :].rearrange("p (a t) -> p a t", a=2), ACT.Copy)\
                   .then_inc(ret_turned_copied, 1)

            def summed_rows(name, dst, dump, slot, slots, k):
                for p in range(4):
                    n = PANELS[name] + p
                    act.wait_ge(slots_used, slot + slots * (p + 1))
                    for t in range(TT):
                        act.activation(token_rows(dump)[:, t, 512 * p:512 * p + 512], ps[:, 2 * (n % 2) + t, :], ACT.Square, accum_out=row_squares[:, t, p:p + 1])
                    for t in range(TT):
                        ins = act.activation(token_rows(dst)[:, t, 512 * p:512 * p + 512], ps[:, 2 * (n % 2) + t, :], ACT.Copy)
                    ins.then_inc(panel_evacuated[n % 2], 1)
                evacuated(act, PANELS[name] + 3)
                for t in range(TT):
                    ins = act.activation(token_rows(dump)[:, t, 0:4], row_squares[:, t, :], ACT.Copy, accum_out=row_root[:, t:t + 1])
                then(ins)
                act.activation(row_root, row_root, ACT.Sqrt, scale=1.0 / D, bias=EPS_6).then_inc(post_root_ready, 1)

            summed_rows("out2", MIX_TOK, VR_GR, 4 * PANELS["out2"], 4, 2)
            row_rms(X_TOK, (post_rows_ready, 1), VR_GR)
            copy_turned(3, hall[:, H_T], "mlp_pre")
            summed_rows("down", H_TOK, H_T, 4 * PANELS["down"], 16, 4)


def kernel(**inputs):
    import concourse.bacc as bacc
    from concourse.bass_utils import run_bass_kernel_spmd as run

    a = {k: np.asarray(v) for k, v in inputs.items()}
    nc = bacc.Bacc("TRN2", target_bir_lowering=False, num_devices=1)
    arrays, d = {}, {}

    def give(name, value):
        value = np.ascontiguousarray(value)
        arrays[name] = value
        d[name] = nc.dram_tensor(name, value.shape, mybir.dt.from_np(value.dtype), kind="ExternalInput").ap()

    def tiles(w):
        return w.reshape(DT, P, -1).transpose(1, 0, 2).reshape(P, -1)

    def rows_of(w):
        return w.reshape(TT, P, -1).transpose(1, 0, 2).reshape(P, -1)

    x = a["x"][0]
    slots = []

    def stream(w, columns=None):
        columns = np.arange(w.shape[1]) if columns is None else columns
        for c in range(0, len(columns), 512):
            slots.append(slot_panels(w, columns[c:c + 512]))

    stream(a["a_w_in"][0, 1])
    stream(a["a_w_in"][0, 0])
    stream(a["a_w_in"][0, 2])
    stream(a["a_w_in"][0, 3])
    stream(a["a_w_out"][0])
    stream(a["w_k_shared"])
    stream(a["b_w_qg"][0], np.arange(D))
    stream(a["w_v_shared"])
    stream(a["b_w_qg"][0], np.arange(D, 2 * D))
    stream(a["b_w_out"][0])
    w_in, kv = a["w_in_2"][0], [np.arange(1024 + 256 * i, 1280 + 256 * i) for i in range(6)]
    ret = [np.arange(2584 + 1024 * i, 3608 + 1024 * i) for i in range(4)]
    for columns in ((kv[0], kv[1]), (kv[2], kv[4]), (ret[1],), (ret[0],), (np.arange(1024),), (kv[3], kv[5]), (ret[2],), (ret[3],)):
        stream(w_in, np.concatenate(columns))
    stream(a["w_out_2"][0])
    stream(a["w_up_2"][0])
    stream(a["w_down_2"][0])
    give("stream", np.concatenate(slots))
    d["slots"] = arrays["stream"].shape[0]
    give("x_channels", tiles(x.T))
    give("resident", resident_constants())
    vectors = {
        "mu_r": a["a_mu_proj"][0, 0], "mu_k": a["a_mu_proj"][0, 1], "mu_v": a["a_mu_proj"][0, 2],
        "mu_g": a["a_mu_proj"][0, 3], "mu_w": a["a_mu_lora"][0, 0], "mu_a": a["a_mu_lora"][0, 1],
        "w0": a["a_w0"][0], "a0": a["a_a0"][0], "k_k": a["a_k_k"][0], "k_a": a["a_k_a"][0],
        "r_k": a["a_r_k"][0].reshape(-1), "gn_g": a["a_gn_g"][0], "gn_b": a["a_gn_b"][0],
        "mix_pre": a["norm_mix_pre_2"][0], "mlp_pre": a["norm_mlp_pre_2"][0],
        "subln": np.tile(a["b_subln_g"][0], DH),
    }
    give("params", np.stack([vectors[name].reshape(DT, P).T for name in PV], 1).reshape(P, -1))
    give("lora1", np.concatenate([tiles(a["a_w1"][0]), tiles(a["a_a1"][0])], 1))
    give("lora2", np.concatenate([a["a_w2"][0], a["a_a2"][0]], 1))
    give("restart", np.broadcast_to((np.arange(T) % N != 0).astype(np.float32), (P, T)))
    give("x_tokens", rows_of(x))
    give("rows", np.stack([a["ln_g"][0], a["ln_b"][0], a["ln_g"][1], a["ln_b"][1], a["norm_mix_post_2"][0],
                           a["norm_mlp_post_2"][0]]))
    give("dist", diff_constants())
    give("lambda", a["b_lambda"][0].reshape(-1))
    give("t5_table", np.broadcast_to(np.concatenate([a["t5_bias_2"], np.full((1, 8), NEG, np.float32)])[:, :, None],
                                     (33, 8, P)).reshape(33, -1))
    give("t5_one", t5_constants())
    give("cmp_small", np.concatenate([a["cmp_pe_k_2"][0].T, a["cmp_pe_v_2"][0].T, a["cmp_w2_k_2"][0], a["cmp_w2_v_2"][0]], 1))
    give("cmp_b1", np.concatenate([a["cmp_b1_k_2"][0], a["cmp_b1_v_2"][0]]))
    give("cmp_w1", np.stack([a[k][0].reshape(32, P, P).transpose(1, 0, 2).reshape(P, -1) for k in ("cmp_w1_k_2", "cmp_w1_v_2")]))
    give("gate_w", tiles(w_in[:, 2560:2584]))
    give("rope", rope_constants().reshape(P, -1))
    give("valid", np.broadcast_to(valid_constants()[:, None], (P, 8, TT, NCMP)).reshape(P, -1))
    give("decay", decay_constants().reshape(P, -1))
    d["t5_scratch"] = nc.dram_tensor("t5_scratch", (8, P, 384), F32, kind="Internal").ap()
    d["out"] = nc.dram_tensor("out", (T, D), F32, kind="ExternalOutput").ap()
    build(nc, d)
    r = run(nc, [arrays], core_ids=[0])
    return r.results[0]["out"].reshape(1, T, D)
```

```python
from contextlib import ExitStack
import math

import numpy as np

import concourse.bass as bass
from concourse import mybir

F32 = mybir.dt.float32
F32R = mybir.dt.float32r
ALU = mybir.AluOpType
ACT = mybir.ActivationFunctionType
AX = mybir.AxisListType

P = 128
D = 2048
T = 256
DT = D // P
TT = T // P
N = 64
NCH = T // N
LORA = 96
ALPHA = (2.0 * 2) ** 0.25
LN_EPS = 1e-5
RING = 4
TURN = 2 * RING
DECAY = -math.exp(-0.5)
GN_EPS = 64e-5

DH = 8
D_SCALE = 128 ** -0.5
LAM_INIT = 0.8 - 0.6 * math.exp(-0.3 * 1)
SUBLN_EPS = 1e-5
A_SCALE = 128 ** -0.5
NCMP = 15
NEG = -1e30
EPS6 = 1e-6

PANELS = {}
_n = 0
for _name, _count in (("k", 4), ("r", 4), ("v", 4), ("g", 4), ("out0", 4), ("dk", 4), ("dq", 4), ("dv", 4), ("dg", 4),
                      ("out1", 4), ("cmp", 1), ("kk", 1), ("kr", 2), ("qr", 2), ("qa", 2), ("vv", 1), ("vr", 2),
                      ("gr", 2), ("out2", 4), ("up", 16), ("down", 4)):
    PANELS[_name] = _n
    _n += _count
SLOTS = 4 * PANELS["down"] + 4 * 16
HALF = {name: 8 * first for name, first in PANELS.items()}
GROUP_ENDS = [HALF[name] for name in ("out0", "dk", "out1", "cmp", "out2", "up", "down")] + [2 * SLOTS]

PV = {name: i for i, name in enumerate(
    ("mu_w", "mu_a", "mu_k", "mu_r", "mu_v", "mu_g", "w0", "a0", "k_k", "k_a", "r_k", "gn_g", "gn_b", "mix_pre",
     "mlp_pre", "subln"))}
MIXES = ("mu_w", "mu_a", "mu_k", "mu_r", "mu_v", "mu_g")

C_ID, C_ONES64, C_ID64, C_NM1, C_NM1T, C_MB, C_U, C_UI, C_L = 0, 128, 256, 320, 384, 448, 768, 832, 896
C_COLS = 960


def resident_constants():
    c = np.zeros((P, C_COLS), np.float32)
    c[:, C_ID:C_ID + P] = np.eye(P)
    c[:64, C_ONES64:C_ONES64 + 64] = 1
    c[64:, C_ONES64 + 64:C_ONES64 + 128] = 1
    r, s = np.arange(P)[:, None] % 64, np.arange(64)[None, :]
    c[:, C_ID64:C_ID64 + 64] = r == s

    def merge(b, lo, hi):
        return (lo // (2 * b) == hi // (2 * b)) & (lo % (2 * b) < b) & (hi % (2 * b) >= b)

    c[:, C_NM1:C_NM1 + 64] = -1.0 * merge(1, r, s)
    c[:, C_NM1T:C_NM1T + 64] = -1.0 * merge(1, s, r)
    for i, b in enumerate((2, 4, 8, 16, 32)):
        c[:, C_MB + 64 * i:C_MB + 64 * i + 64] = merge(b, r, s)
    c[:, C_U:C_U + 64] = r < s
    c[:, C_UI:C_UI + 64] = r <= s
    c[:, C_L:C_L + 64] = r > s
    return c


def diff_constants():
    q, k = 128 + np.arange(P)[:, None], np.arange(T)[None, :]
    return np.where(k // 64 <= q // 64, np.abs(q - k), 1e30).astype(np.float32)


def t5_buckets(rel):
    n = np.maximum(rel, 0)
    nf = np.maximum(n, 1).astype(np.float32)
    large = 16 + (np.log(nf / np.float32(16)) / np.float32(np.log(128 / 16)) * np.float32(16)).astype(np.int32)
    return np.where(n < 16, n, np.minimum(large, 31))


def t5_constants():
    rel = np.concatenate([255 - np.arange(384), np.arange(512) - 255])
    one = np.zeros((33, 896), np.float32)
    one[np.where(rel < 0, 32, t5_buckets(rel)), np.arange(896)] = 1
    return one


def valid_constants():
    t = np.arange(T).reshape(TT, P).T[:, :, None]
    return (t >= 16 * np.arange(NCMP) + 31).astype(np.float32)


def rope_constants():
    inv = (np.float32(10000.0) ** (-np.arange(0, 256, 2, dtype=np.float32) / np.float32(256))).astype(np.float32)
    ang = (np.arange(T, dtype=np.float32)[:, None] * inv[None, :]).astype(np.float32)
    return np.stack([np.cos(ang).T, np.sin(ang).T], 1).astype(np.float32)


def decay_constants():
    lg = np.log(1.0 - np.exp2(-5.0 - np.arange(4)))
    m = np.arange(P)[:, None]
    out = np.zeros((P, 4, 384))
    for h in range(4):
        d0 = np.arange(T)[None, :] - m
        d1 = np.arange(P)[None, :] - m
        out[:, h, :256] = np.where(d0 >= 0, np.exp(np.maximum(d0, 0) * lg[h]), 0)
        out[:, h, 256:] = np.where(d1 >= 0, np.exp(np.maximum(d1, 0) * lg[h]), 0)
    return (out / 16.0).astype(np.float32)


def slot_panels(w, columns):
    part = w[:, columns]
    return part.reshape(-1, 4, P, 512).transpose(0, 2, 1, 3).reshape(-1, P, 2048)


def build(nc, d):
    ctx = ExitStack()
    with ctx:
        def sb(name, shape, kind=F32):
            return ctx.enter_context(nc.sbuf_tensor(name, shape, kind))

        def sem(name):
            return ctx.enter_context(nc.semaphore(name))

        ring = sb("ring", [P, RING, 4, 512])
        w_hi, w_lo = sb("w_hi", [P, 2, 2, 512], F32R), sb("w_lo", [P, 2, 2, 512], F32R)
        a_hi, a_lo = sb("a_hi", [P, 2, 2, T], F32R), sb("a_lo", [P, 2, 2, T], F32R)
        key_work = sb("key_work", [P, 2, 4, T])
        hall = sb("hall", [P, 8, DT, T])
        work = sb("work", [P, 2, DT, N])
        con = sb("con", [P, C_COLS])
        par = sb("par", [P, 16, DT])
        wl = sb("wl", [P, DT, NCH])
        small = sb("small", [P, 464])
        ps = ctx.enter_context(nc.psum_tensor("ps", [P, 8, 512], F32))

        XT, MIX, LD, AA, KK, KN, RR, VV = range(8)
        flat = [hall[:, i].rearrange("p a b -> p (a b)") for i in range(8)]
        ident = con[:, C_ID:C_ID + P]
        ones64 = con[:, C_ONES64:C_ONES64 + P]
        id64 = con[:, C_ID64:C_ID64 + 64]

        def pv(name):
            return par[:, PV[name], :]

        def over(ap, shape):
            return ap.unsqueeze(2).broadcast_to(shape)

        def mask(column, width=DT):
            return con[:, column:column + 64].unsqueeze(1).broadcast_to([P, width, 64])

        slot_landed = [sem(f"slot_landed{i}") for i in range(RING)]
        weights_hi = sem("weights_hi")
        activation_hi = sem("activation_hi")
        weights_split = sem("weights_split")
        activation_split = sem("activation_split")
        halves_used = sem("halves_used")
        panel_evacuated = [sem("even_panel_evacuated"), sem("odd_panel_evacuated")]
        const_in = sem("const_in")
        x_in = sem("x_in")
        lora_in = sem("lora_in")
        mix_ready = sem("mix_ready")
        lora_read = sem("lora_read")
        lora_hid_done = sem("lora_hid_done")
        lora_hid_copied = sem("lora_hid_copied")
        lora_up_done = sem("lora_up_done")
        lora_up_copied = sem("lora_up_copied")
        key_raw_ready = sem("key_raw_ready")
        key_squared = sem("key_squared")
        key_norm_summed = sem("key_norm_summed")
        key_norm_ready = sem("key_norm_ready")
        decay_summed = sem("decay_summed")
        decay_exp_ready = sem("decay_exp_ready")
        key_group_done = sem("key_group_done")
        receptance_done = sem("receptance_done")
        gram_done = sem("gram_done")
        dve_step = sem("dve_step")
        act_step = sem("act_step")
        gram_masked = sem("gram_masked")
        z_done = sem("z_done")
        z_masked = sem("z_masked")
        merge_done = sem("merge_done")
        merged = sem("merged")
        turned = sem("turned")
        turned_copied = sem("turned_copied")
        rhs_done = sem("rhs_done")
        rhs_ready = sem("rhs_ready")
        u_done = sem("u_done")
        u_ready = sem("u_ready")
        y_done = sem("y_done")
        y_copied = sem("y_copied")
        state_done = sem("state_done")
        state_ready = sem("state_ready")
        head_sum_done = sem("head_sum_done")
        head_in_ready = sem("head_in_ready")
        head_root_ready = sem("head_root_ready")
        out_rows_ready = sem("out_rows_ready")
        rows_in = sem("rows_in")
        ln_var_ready = sem("ln_var_ready")
        ln_root_ready = sem("ln_root_ready")
        act_rows_ready = sem("act_rows_ready")
        tok_ready = sem("tok_ready")
        tr_done = sem("tr_done")
        tr_copied_v = sem("tr_copied_v")
        tr_copied_a = sem("tr_copied_a")
        region_free = sem("region_free")
        diff_in = sem("diff_in")
        lam_parts = sem("lam_parts")
        lam_exp = sem("lam_exp")
        score_done = sem("score_done")
        score_max = sem("score_max")
        score_exp = sem("score_exp")
        attn_ready = sem("attn_ready")
        attn_turned = sem("attn_turned")
        attn_copied = sem("attn_copied")
        o_done = sem("o_done")
        o_copied = sem("o_copied")
        nsa_in = sem("nsa_in")
        t5_in = sem("t5_in")
        t5_done = sem("t5_done")
        t5_copied = sem("t5_copied")
        t5_stored = sem("t5_stored")
        blocks_ready = sem("blocks_ready")
        cmp_done = sem("cmp_done")
        cmp_step = sem("cmp_step")
        gate_done = sem("gate_done")
        gate_copied = sem("gate_copied")
        rope_ready = sem("rope_ready")
        ret_score_done = sem("ret_score_done")
        ret_score_ready = sem("ret_score_ready")
        ret_o_done = sem("ret_o_done")
        ret_o_ready = sem("ret_o_ready")
        ret_var_ready = sem("ret_var_ready")
        ret_root_ready = sem("ret_root_ready")
        out_stored = sem("out_stored")
        chunk_done = sem("chunk_done")
        eps_ready = sem("eps_ready")
        y_centred = sem("y_centred")
        finished = sem("finished")
        ret_in = sem("ret_in")


        more = ("squares_summed score_read post_in nsa_parts_in cmp_hid_done cmp_hid_ready cmp_hid_turned cmp_hid_copied "
                "cmp_made cmp_copied cmp_scored cmp_centred cmp_exp cmp_probs_ready cmp_turned cmp_turned_copied "
                "gate_sum_done gate_sum_copied gate_turned gates_ready rope_in mix_copied post_root_ready post_rows_ready "
                "up_squared down_copied ret_turned ret_turned_copied t5_table_in").split()
        (squares_summed, score_read, post_in, nsa_parts_in, cmp_hid_done, cmp_hid_ready, cmp_hid_turned, cmp_hid_copied,
         cmp_made, cmp_copied, cmp_scored, cmp_centred, cmp_exp, cmp_probs_ready, cmp_turned, cmp_turned_copied,
         gate_sum_done, gate_sum_copied, gate_turned, gates_ready, rope_in, mix_copied, post_root_ready, post_rows_ready,
         up_squared, down_copied, ret_turned, ret_turned_copied, t5_table_in) = (sem(x) for x in more)
        block = ctx.enter_context(nc.Block())

        def evacuated(eng, n):
            eng.wait_ge(panel_evacuated[n % 2], n // 2 + 1)

        def computed(eng, n, quarter=3):
            eng.wait_ge(halves_used, 8 * n + 2 * (quarter + 1))

        def wide(w):
            return ps[:, 2 * w:2 * w + 2, :].rearrange("p b (j s) -> p (b j) s", s=N)

        def gram(w):
            return ps[:, 4 * w:4 * w + 4, :].rearrange("p b (j x s) -> p (b j) x s", x=2, s=N)

        bufs = [flat[i].rearrange("p (k j s) -> p k j s", k=4, s=N) for i in (XT, MIX)]
        X, XTR, AT, Z = (bufs[0][:, k] for k in range(4))
        ARB, AAK, ARK, VTOK = (bufs[1][:, k] for k in range(4))
        ST, KTOK = work[:, 0], work[:, 1]
        BTOK, RHS, U, YC, BON, SQ = AT, Z, XTR, ARB, AAK, ARK
        HEADS = [x for j in range(DT) for x in ((j, 0), ((j + DT // 2) % DT, 1))]
        rows = (slice(0, N), slice(N, P))
        lora_w1 = flat[VV][:, 0:2 * DT * LORA].rearrange("p (m a r) -> p m a r", m=2, r=LORA)
        lora_w2 = flat[KN][0:LORA, :].rearrange("p (m c) -> p m c", m=2)
        restart = work[:, 0].rearrange("p j s -> p (j s)")[:, 0:T]
        lora_hid = work[0:LORA, 1].rearrange("p j s -> p (j s)")[:, 0:2 * T].rearrange("p (m t) -> p m t", m=2)
        key_sq = [work[:, i].rearrange("p j s -> p (j s)").rearrange("p (a t) -> p a t", a=4) for i in range(2)]
        key_tmp, key_exp = key_work[:, 0], key_work[:, 1]
        EPS_GN, EPS_LN, EPS_SUB, EPS_6 = (small[:, i:i + 1] for i in range(4))

        def token_rows(region, width=D):
            return flat[region][:, 0:TT * width].rearrange("p (a c) -> p a c", a=TT)

        X_TOK, ROWS, X_T, DK, DQ, DV, DG, O_TOK = range(8)
        prob = [flat[ROWS][:, 512 * i:512 * i + 512] for i in range(2)]
        prob_t = [flat[ROWS][:, 1024 + 512 * i:1536 + 512 * i] for i in range(2)]
        dist = flat[ROWS][:, 2048:2304]
        lam_rows = flat[ROWS][:, 2304:2816].rearrange("p (a b) -> p a b", a=4)
        lam_tmp = flat[ROWS][:, 2816:3072].rearrange("p (a b) -> p a b", a=2)
        junk = flat[ROWS][:, 3072:3328]
        stats = small[:, 8:56].rearrange("p (t k s) -> p t k s", t=TT, k=4)
        mean_var = small[:, 56:60].rearrange("p (t k) -> p t k", t=TT)
        root = small[:, 60:62]
        top = [small[:, 64 + 4 * i:66 + 4 * i] for i in range(2)]
        total = [small[:, 72 + 4 * i:74 + 4 * i] for i in range(2)]
        share = [small[:, 80 + 4 * i:82 + 4 * i] for i in range(2)]
        lam_sum, lam, neg_lam = small[:, 88:90], small[:, 90:91], small[:, 91:92]
        o_squares = small[:, 96:112]
        row_squares = small[:, 112:120].rearrange("p (t k) -> p t k", t=TT)
        row_root = small[:, 120:122]

        H_TOK, H_T, QA_CM_K4, QR_KR, VR_GR, CAT_T, BIAS_VV = 1, 2, 3, 4, 5, 6, 7
        qa, cm, k4 = hall[:, QA_CM_K4, 0:8], hall[:, QA_CM_K4, 8:12], hall[:, QA_CM_K4, 12:16]
        qr, kr = hall[:, QR_KR, 0:8], hall[:, QR_KR, 8:16]
        vr = flat[VR_GR][:, 0:2048].rearrange("p (t c) -> p t c", t=TT)
        gr = flat[VR_GR][:, 2048:4096].rearrange("p (t c) -> p t c", t=TT)
        bias = flat[BIAS_VV][:, 0:2048].rearrange("p (h k) -> p h k", h=8)
        vv = flat[BIAS_VV][:, 2048:3072].rearrange("p (t c) -> p t c", t=TT)
        misc = flat[BIAS_VV][:, 3072:4096]
        block_pe = misc[:, 0:64]
        cmp_w2 = misc[:, 64:320].rearrange("p (a b) -> p a b", a=2)
        cmp_b1 = misc[0:2 * NCMP, 320:576].rearrange("p (a b) -> p a b", a=2)
        cmp_hid = misc[0:2 * NCMP, 576:832].rearrange("p (a b) -> p a b", a=2)
        cmp_hid_t = misc[:, 832:892].rearrange("p (a b) -> p a b", a=2)
        gates = misc[:, 892:940].rearrange("p (t b) -> p t b", t=TT)
        gate_sum = flat[CAT_T][0:24, 0:T]
        work_flat = work[:].rearrange("p a j s -> p (a j s)")
        windows = [work_flat[:, 960 * i:960 * i + 960].rearrange("p (l g n) -> p l g n", l=32, g=2) for i in range(2)]
        cmp_prob_t = work_flat[0:NCMP, :].rearrange("p (i q) -> p i q", q=P)
        cmp_w1 = [flat[r].rearrange("p (l c) -> p l c", l=32) for r in (H_TOK, VR_GR)]
        gate_w = con[:, 256:640].rearrange("p (a b) -> p a b", a=DT)
        cmp_k = con[:, 640:670]
        cmp_v = con[0:NCMP, 670:926].rearrange("p (g c) -> p g c", g=2)
        cmp_bias = small[:, 224:464]
        cmp_p, cmp_valid = flat[H_TOK][:, 3072 - 512:3072 - 272], flat[H_TOK][:, 3072 - 256:3072 - 16]
        cmp_top, cmp_total = small[:, 128:144], small[:, 144:160]
        a_prob = [flat[H_TOK][:, 512 * i:512 * i + 512] for i in range(2)]
        a_prob_t = [flat[H_TOK][:, 1024 + 512 * i:1536 + 512 * i] for i in range(2)]
        cmp_p = flat[H_TOK][:, 2048:2288]
        cmp_valid = flat[H_TOK][:, 2304:2544]
        rope = flat[H_TOK][:, 2560:3072].rearrange("p (a t) -> p a t", a=2)
        decay_table = [flat[r][:, at + 384 * i:at + 384 * i + 384] for r, at in ((H_TOK, 3072), (QA_CM_K4, 2048)) for i in range(2)]
        rope_tmp = [hall[:, CAT_T, 8:12], hall[:, CAT_T, 12:16]]
        ret_p = [flat[H_TOK][:, 512 * i:512 * i + 384] for i in range(2)]
        ret_o = [flat[H_TOK][:, 1024 + 512 * i:1536 + 512 * i].rearrange("p (t c) -> p t c", t=TT) for i in range(4)]
        ret_stats = [small[:, 160 + 12 * i:172 + 12 * i].rearrange("p (t s) -> p t s", t=TT) for i in range(2)]
        ret_mv = [small[:, 184 + 4 * i:188 + 4 * i].rearrange("p (t s) -> p t s", t=TT) for i in range(2)]
        ret_root = [small[:, 192 + 2 * i:194 + 2 * i] for i in range(2)]
        up = hall[:, 4:8].rearrange("p r a t -> p (r a) t")
        MIX_TOK, POST = 4, 3
        t5_table, t5_one = flat[KK][0:33, 0:1024].rearrange("p (h q) -> p h q", h=8), flat[KK][0:33, 1024:1920]
        t5_rows = flat[RR][:, 0:3072].rearrange("p (h m) -> p h m", h=8)
        SCORES = 16
        operand = {name: hall[:, region] for name, region in
                   (("k", MIX), ("r", MIX), ("v", MIX), ("g", MIX), ("out0", RR), ("dk", X_T), ("dq", X_T), ("dv", X_T),
                    ("dg", X_T), ("out1", DK), ("cmp", H_T), ("kk", H_T), ("kr", H_T), ("qr", H_T), ("qa", H_T),
                    ("vv", H_T), ("vr", H_T), ("gr", H_T), ("out2", CAT_T), ("up", H_T))}
        operand["down"] = up

        def product_of(h):
            name = [n for n in HALF if HALF[n] <= h][-1]
            return name, 2 * (h - HALF[name]) % (64 if name == "down" else DT)

        def ahead(n):
            return min(8 * n + 10, min(e for e in GROUP_ENDS if e > 8 * n))

        def ring_half(h):
            return ring[:, h // 2 % RING, 2 * (h % 2):2 * (h % 2) + 2]

        @block.sync
        def _(sp):
            stream = d["stream"]
            turns = d["slots"] // RING
            for j in range(RING):
                sp.dma_start(ring[:, j].rearrange("p a b -> p (a b)"), stream[j]).then_inc(slot_landed[j], 16)
            with sp.Fori(1, turns) as i:
                for j in range(RING):
                    sp.wait_ge(weights_split, i * TURN + 2 * (j + 1 - RING))
                    sp.dma_start(ring[:, j].rearrange("p a b -> p (a b)"),
                                 stream[bass.ds(i * RING + j, 1)].rearrange("o p c -> (o p) c")).then_inc(slot_landed[j], 16)
            for s in range(turns * RING, d["slots"]):
                sp.wait_ge(weights_split, 2 * (s + 1 - RING))
                sp.dma_start(ring[:, s % RING].rearrange("p a b -> p (a b)"), stream[s])\
                  .then_inc(slot_landed[s % RING], 16)

        @block.gpsimd
        def _(pool):
            def split(name, panels=4, first=0, halves=8):
                h0 = HALF[name] + halves * first
                with pool.Fori(0, panels) as i:
                    for h in range(h0, h0 + halves):
                        tile = product_of(h)[1]
                        pool.wait_ge(activation_hi, i * halves + (h + 1))
                        if h >= 2:
                            pool.wait_ge(halves_used, i * halves + (h - 1))
                        pool.tensor_tensor(a_lo[:, h % 2], operand[name][:, tile:tile + 2], a_hi[:, h % 2].bitcast(F32), ALU.subtract)\
                            .then_inc(activation_split, 1)

            for dst, src in ((flat[KK][0:33, 0:1024], d["t5_table"]), (t5_one, d["t5_one"])):
                pool.dma_start(dst, src).then_inc(t5_table_in, 16)
            for dst, src in ((flat[XT], d["x_channels"]), (con[:], d["resident"]),
                             (par[:].rearrange("p a b -> p (a b)"), d["params"])):
                pool.dma_start(dst, src).then_inc(x_in, 16)
            for dst, src in ((flat[VV][:, 0:2 * DT * LORA], d["lora1"]), (flat[KN][0:LORA, :], d["lora2"]),
                             (restart, d["restart"])):
                pool.dma_start(dst, src).then_inc(lora_in, 16)
            pool.wait_ge(t5_copied, 8)
            pool.dma_start(d["t5_scratch"].rearrange("h p m -> p h m"), t5_rows).then_inc(t5_stored, 16)
            for h in range(2):
                pool.wait_ge(activation_hi, h + 1)
                pool.tensor_tensor(a_lo[:, h], hall[:, MIX, 2 * h:2 * h + 2], a_hi[:, h].bitcast(F32), ALU.subtract)\
                    .then_inc(activation_split, 1)
            for h in range(2, 8):
                pool.wait_ge(activation_hi, h + 1)
                pool.wait_ge(halves_used, h - 1)
                pool.tensor_tensor(a_lo[:, h % 2], hall[:, MIX, 2 * h:2 * h + 2], a_hi[:, h % 2].bitcast(F32), ALU.subtract)\
                    .then_inc(activation_split, 1)
            split("k", 3, first=1)
            for name in ("r", "v", "g"):
                split(name)
            pool.wait_ge(chunk_done, NCH)
            pool.dma_start(flat[X_TOK], d["x_tokens"]).then_inc(rows_in, 16)
            for i in range(2):
                pool.dma_start(token_rows(ROWS)[:, i], d["rows"][i].partition_broadcast(P)).then_inc(rows_in, 16)
            split("out0")
            pool.wait_ge(tok_ready, 2)
            pool.dma_start(dist, d["dist"]).then_inc(diff_in, 16)
            pool.dma_start(flat[ROWS][:, 2304:2816], d["lambda"].partition_broadcast(P)).then_inc(diff_in, 16)
            for name in ("dk", "dq", "dv", "dg"):
                split(name)
            pool.wait_ge(o_copied, SCORES)
            for i in range(2):
                pool.dma_start(token_rows(ROWS)[:, i], d["rows"][2 + i].partition_broadcast(P)).then_inc(rows_in, 16)
            split("out1", 1)
            pool.wait_ge(tr_done, 16)
            pool.wait_ge(t5_stored, 16)
            scratch = d["t5_scratch"]
            pool.dma_start(bias, bass.AP(scratch.tensor, 127, [[383, P], [P * 384, 8], [1, T]])).then_inc(nsa_in, 16)
            for dst, src in ((misc[:, 0:320], d["cmp_small"]), (misc[0:2 * NCMP, 320:576], d["cmp_b1"].partition_broadcast(2 * NCMP)),
                             (con[:, 256:640], d["gate_w"]), (flat[VR_GR], d["cmp_w1"][1])):
                pool.dma_start(dst, src).then_inc(nsa_in, 16)
            split("out1", 3, first=1)
            pool.wait_ge(tr_done, 24)
            pool.dma_start(flat[H_TOK], d["cmp_w1"][0]).then_inc(nsa_in, 16)
            split("cmp", 1)
            split("kk", 1)
            split("kr", 1)
            pool.wait_ge(cmp_hid_done, 2)
            pool.dma_start(flat[H_TOK][:, 2560:3072], d["rope"]).then_inc(rope_in, 16)
            pool.dma_start(cmp_valid, d["valid"]).then_inc(rope_in, 16)
            for h in range(4):
                pool.dma_start(decay_table[h], d["decay"][:, 384 * h:384 * h + 384]).then_inc(ret_in, 16)
            split("kr", 1, first=1)
            split("qr", 2)
            split("qa", 2)
            split("vv", 1)
            split("vr", 2)
            split("gr", 2)
            pool.wait_ge(ret_turned, 4)
            pool.wait_ge(ret_score_ready, 4)
            for i in range(2):
                pool.dma_start(token_rows(POST)[:, i], d["rows"][4 + i].partition_broadcast(P)).then_inc(post_in, 16)
            split("out2")
            split("up", 16)
            split("down", 4, halves=32)
            for t in range(TT):
                pool.wait_ge(out_rows_ready, t + 1)
                pool.dma_start(d["out"][t * P:(t + 1) * P, :], token_rows(H_TOK)[:, t]).then_inc(out_stored, 16)
            pool.wait_ge(out_stored, 32)

        @block.tensor
        def _(pe):
            def half_products(kind, h, turns, bank, tile, last, q, pass_hook=None):
                b = h % 2
                pe.wait_ge(activation_hi, turns + (h + 1))
                for k, (w, x) in enumerate(((w_hi, a_hi), (w_lo, a_hi), (w_hi, a_lo))):
                    if pass_hook:
                        pass_hook(q, b, k)
                    if k == 1:
                        pe.wait_ge(weights_split, turns + (h + 1))
                    if k == 2:
                        pe.wait_ge(activation_split, turns + (h + 1))
                    for a in range(2):
                        first, final = tile + a == 0 and k == 0, tile + a == last and k == 2
                        if kind == "W":
                            for c in range(4):
                                mm = pe.matmul(ps[:, bank + c // 2, (c % 2) * T:(c % 2 + 1) * T],
                                               w[:, b, a, c * P:(c + 1) * P], x[:, b, a, :],
                                               start=(first and c % 2 == 0), stop=final, skip_group_check=True)
                        else:
                            for c in range(TT):
                                mm = pe.matmul(ps[:, bank + c, :], x[:, b, a, c * P:(c + 1) * P], w[:, b, a, :],
                                               start=first, stop=final)
                return mm

            def panel(n, kind, hook=None, i=0, slots=4, slot=None, pass_hook=None):
                if n >= 2:
                    pe.wait_ge(panel_evacuated[n % 2], (n - 2) // 2 + 1 + i)
                for q in range(slots):
                    for b in range(2):
                        h = 2 * ((4 * n if slot is None else slot) + q) + b
                        half_products(kind, h, i * (4 * slots), 2 * (n % 2), 4 * q + 2 * b, 4 * slots - 1, q, pass_hook)\
                            .then_inc(halves_used, 1)
                    if hook:
                        hook(q)

            def product(name, panels, kind):
                with pe.Fori(0, panels // 2) as i:
                    for p in range(2):
                        panel(PANELS[name] + p, kind, i=i)

            def turn_rows(v, src):
                for u in range(8):
                    if u >= 4:
                        pe.wait_ge((tr_copied_v, tr_copied_a)[u % 2], 4 * v + (u - 4) // 2 + 1)
                    for a in range(2):
                        for t in range(TT):
                            c = (2 * u + a) * P
                            mm = pe.transpose(ps[:, 4 + u % 4, a * T + t * P:a * T + (t + 1) * P], src[:, t, c:c + P], ident)
                    mm.then_inc(tr_done, 1)

            pe.wait_ge(t5_table_in, 32)
            for h in range(8):
                if h >= 2:
                    pe.wait_ge(t5_copied, h - 1)
                pe.matmul(ps[:, 4 + h % 2, 0:384], t5_table[:, h, :], t5_one[:, 0:384], start=True, stop=True)\
                  .then_inc(t5_done, 1)
            for t in range(TT):
                for n in range(NCMP):
                    at = 384 + 224 + P * t - 16 * n
                    mm = pe.matmul(ps[:, 6, 15 * t + n:240:30], t5_one[:, at:at + P], t5_table[:, :, 0], start=True, stop=True)
            mm.then_inc(t5_done, 1)
            pe.wait_ge(t5_copied, 9)

            pe.wait_ge(lora_in, 48)
            for m in range(2):
                for t in range(DT):
                    if t % 4 == 0:
                        pe.wait_ge(mix_ready, 4 * m + t // 4 + 1)
                    mm = pe.matmul(ps[0:LORA, 4 + m, 0:T], lora_w1[:, m, t, :], hall[:, MIX, t, :],
                                   start=(t == 0), stop=(t == DT - 1))
                    if t % 4 == 3:
                        mm.then_inc(lora_read, 1)
            pe.wait_ge(lora_hid_copied, 2)
            for u in range(8):
                if u >= 2:
                    pe.wait_ge(lora_up_copied, u - 1)
                for c in range(4):
                    j = 4 * (u % 4) + c
                    mm = pe.matmul(ps[:, 4 + 2 * (u % 2) + c // 2, (c % 2) * T:(c % 2 + 1) * T],
                                   lora_w2[:, u // 4, j * P:(j + 1) * P], lora_hid[:, u // 4, :], start=True, stop=True)
                mm.then_inc(lora_up_done, 1)

            def key_norms(g):
                pe.wait_ge(key_squared, g + 1)
                if g >= 2:
                    pe.wait_ge(key_norm_ready, g - 1)
                for b in range(2):
                    mm = pe.matmul(ps[:, 4 + 2 * (g % 2) + b, :], ones64, key_sq[g % 2][:, 2 * b:2 * b + 2, :],
                                   start=True, stop=True)
                mm.then_inc(key_norm_summed, 1)

            KEY_NORMS_AFTER = {("r", 0): {1: 0, 3: 1}, ("r", 2): {1: 2}, ("v", 0): {1: 3}}
            for name in ("k", "r", "v", "g"):
                for p in range(4):
                    hook = None
                    if (name, p) in KEY_NORMS_AFTER:
                        hook = lambda q, after=KEY_NORMS_AFTER[name, p]: key_norms(after[q]) if q in after else None
                    panel(PANELS[name] + p, "W", hook=hook)

            def head_sums(w, src, count):
                pe.wait_ge(head_in_ready, count)
                for b in range(2):
                    mm = pe.matmul(ps[:, 2 * w + b, :], ones64, src[:, 8 * b:8 * b + 8, :], start=True, stop=True)
                mm.then_inc(head_sum_done, 1)

            for c in range(NCH):
                cs = slice(c * N, (c + 1) * N)
                if c == 0:
                    pe.wait_ge(key_group_done, 4)
                    pe.wait_ge(receptance_done, 4)
                    evacuated(pe, PANELS["g"] + 2)
                    evacuated(pe, PANELS["g"] + 3)
                else:
                    pe.wait_ge(chunk_done, c)
                for w, lhs in ((0, AA), (1, KK)):
                    for j, h in HEADS:
                        mm = pe.matmul(gram(w)[rows[h], j], hall[rows[h], lhs, j, cs], hall[rows[h], KN:KN + 2, j, cs],
                                       start=True, stop=True)
                    mm.then_inc(gram_done, 1)
                pe.wait_ge(gram_masked, 3 * c + 1)
                for j, h in HEADS:
                    mm = pe.matmul(wide(0)[rows[h], j], hall[rows[h], KN, j, cs], hall[rows[h], AA, j, cs],
                                   start=True, stop=True)
                mm.then_inc(gram_done, 1)
                for i in range(5):
                    if i == 0:
                        pe.wait_ge(gram_masked, 3 * c + 3)
                    else:
                        pe.wait_ge(merged, 9 * c + 2 * i - 1)
                    for j, h in HEADS:
                        mm = pe.matmul(wide(1)[rows[h], j], AT[rows[h], j], X[rows[h], j], start=True, stop=True)
                    mm.then_inc(z_done, 1)
                    pe.wait_ge(z_masked, 5 * c + i + 1)
                    if i:
                        pe.wait_ge(merged, 9 * c + 2 * i)
                    for j, h in HEADS:
                        mm = pe.matmul(wide(2)[rows[h], j], XTR[rows[h], j], Z[rows[h], j], start=True, stop=True)
                    mm.then_inc(merge_done, 1)
                    if i < 4:
                        for j, h in HEADS:
                            mm = pe.matmul(wide(3)[rows[h], j], Z[rows[h], j], XTR[rows[h], j], start=True, stop=True)
                        mm.then_inc(merge_done, 1)
                for w, src in ((0, AA), (1, KK), (2, VV)):
                    if w == 2:
                        pe.wait_ge(merged, 9 * c + 9)
                    for j, h in HEADS:
                        mm = pe.matmul(wide(w)[rows[h], j], hall[rows[h], src, j, cs], id64[rows[h], :],
                                       start=True, stop=True)
                    mm.then_inc(turned, 1)
                pe.wait_ge(turned_copied, 3 * c + 3)
                if c:
                    pe.wait_ge(state_ready, c)
                for j, h in HEADS:
                    if c:
                        pe.matmul(wide(3)[rows[h], j], hall[rows[h], KN, j, cs], ST[rows[h], j], start=True, stop=False)
                    mm = pe.matmul(wide(3)[rows[h], j], AAK[rows[h], j], VTOK[rows[h], j], start=(c == 0), stop=True)
                mm.then_inc(rhs_done, 1)
                pe.wait_ge(rhs_ready, c + 1)
                for j, h in HEADS:
                    mm = pe.matmul(wide(0)[rows[h], j], X[rows[h], j], RHS[rows[h], j], start=True, stop=True)
                mm.then_inc(u_done, 1)
                pe.wait_ge(u_ready, c + 1)
                for j, h in HEADS:
                    if c:
                        pe.matmul(wide(1)[rows[h], j], ST[rows[h], j], hall[rows[h], RR, j, cs], start=True, stop=False)
                    pe.matmul(wide(1)[rows[h], j], VTOK[rows[h], j], ARK[rows[h], j], start=(c == 0), stop=False)
                    mm = pe.matmul(wide(1)[rows[h], j], U[rows[h], j], ARB[rows[h], j], start=False, stop=True)
                mm.then_inc(y_done, 1)
                for j, h in HEADS:
                    pe.matmul(wide(2)[rows[h], j], BTOK[rows[h], j], U[rows[h], j], start=True, stop=False)
                    mm = pe.matmul(wide(2)[rows[h], j], KTOK[rows[h], j], VTOK[rows[h], j], start=False, stop=True)
                mm.then_inc(state_done, 1)
                head_sums(0, BON, 3 * c + 1)
                head_sums(3, YC, 3 * c + 2)
                head_sums(1, SQ, 3 * c + 3)
            pe.wait_ge(chunk_done, NCH)
            product("out0", 4, "X")
            pe.wait_ge(tok_ready, 2)
            turn_rows(0, token_rows(X_TOK))
            product("dk", 4, "W")
            product("dq", 4, "W")
            product("dv", 4, "X")

            def diff_scores(i):
                h, t = divmod(i, TT)
                if i >= 2:
                    pe.wait_ge(score_read, i - 1)
                for m in range(2):
                    mm = pe.matmul(ps[:, 4 + i % 2, m * T:m * T + P * (t + 1)], hall[:, DQ, 2 * h + m, t * P:(t + 1) * P],
                                   hall[:, DK, 2 * h + m, 0:P * (t + 1)], start=True, stop=True)
                mm.then_inc(score_done, 1)

            def diff_turn(i):
                pe.wait_ge(attn_ready, i + 1)
                if i:
                    pe.wait_ge(attn_copied, i)
                for k in range(i % TT + 1):
                    mm = pe.transpose(ps[:, 6, k * P:(k + 1) * P], prob[i % 2][:, k * P:(k + 1) * P], ident)
                mm.then_inc(attn_turned, 1)

            def diff_values(i):
                h, t = divmod(i, TT)
                pe.wait_ge(attn_copied, i + 1)
                if i:
                    pe.wait_ge(o_copied, i)
                for k in range(t + 1):
                    mm = pe.matmul(ps[:, 7, 0:T], prob_t[i % 2][:, k * P:(k + 1) * P], token_rows(DV)[:, k, h * T:(h + 1) * T],
                                   start=(k == 0), stop=(k == t))
                mm.then_inc(o_done, 1)

            def diff_inside(s, b, k):
                if s and b == 1 and k == 2:
                    diff_turn(s - 1)

            def diff_after(s):
                diff_scores(s)
                if s:
                    diff_values(s - 1)

            evacuated(pe, PANELS["dq"] + 3)
            pe.wait_ge(tr_copied_v, 4)
            for p in range(4):
                panel(PANELS["dg"] + p, "X", hook=lambda q, p=p: diff_after(4 * p + q),
                      pass_hook=lambda q, b, k, p=p: diff_inside(4 * p + q, b, k))
            diff_turn(15)
            diff_values(15)
            pe.wait_ge(act_rows_ready, 1)
            turn_rows(1, token_rows(O_TOK))
            product("out1", 4, "X")

            pe.wait_ge(act_rows_ready, 3)
            turn_rows(2, token_rows(H_TOK))
            panel(PANELS["cmp"], "W")
            panel(PANELS["kk"], "W")

            def compress_hook(s):
                if s == 0:
                    pe.wait_ge(nsa_in, 96)
                    for a in range(DT):
                        mm = pe.matmul(ps[0:24, 6, 0:T], gate_w[:, a, :], hall[:, H_T, a, :], start=(a == 0), stop=(a == DT - 1))
                    mm.then_inc(gate_sum_done, 1)
                if s in (1, 2):
                    pe.wait_ge(blocks_ready, s)
                    for l in range(32):
                        mm = pe.matmul(ps[0:2 * NCMP, 3 + s, 0:P], windows[s - 1][:, l].rearrange("p g n -> p (g n)"),
                                       cmp_w1[s - 1][:, l, :], start=(l == 0), stop=(l == 31))
                    mm.then_inc(cmp_hid_done, 1)
                if s == 3:
                    pe.wait_ge(gate_sum_copied, 1)
                    for t in range(TT):
                        mm = pe.transpose(ps[:, 7, 24 * t:24 * t + 24], gate_sum[:, t * P:(t + 1) * P], ident[0:24, 0:24])
                    mm.then_inc(gate_turned, 1)
                if s == 4:
                    pe.wait_ge(cmp_hid_ready, 2)
                    for i in range(2):
                        mm = pe.transpose(ps[:, 6, 32 * i:32 * i + 30], cmp_hid[:, i, :], ident[0:30, 0:30])
                    mm.then_inc(cmp_hid_turned, 1)
                if s == 5:
                    pe.wait_ge(cmp_hid_copied, 1)
                    pe.matmul(ps[:, 4, 0:30], cmp_w2[:, 0, :], cmp_hid_t[:, 0, :], start=True, stop=True)
                    for g in range(2):
                        mm = pe.matmul(ps[0:NCMP, 5, g * P:(g + 1) * P], cmp_hid_t[:, 1, NCMP * g:NCMP * g + NCMP], cmp_w2[:, 1, :],
                                       start=True, stop=True)
                    mm.then_inc(cmp_made, 1)

            for p in range(2):
                panel(PANELS["kr"] + p, "W", hook=lambda q, p=p: compress_hook(4 * p + q))
            for name in ("qr", "qa"):
                for p in range(2):
                    panel(PANELS[name] + p, "W")

            def cmp_hook(s):
                if s == 1:
                    evacuated(pe, PANELS["qa"] + 1)
                    pe.wait_ge(cmp_copied, 2)
                    for i in range(SCORES):
                        h, t = divmod(i, TT)
                        mm = pe.matmul(ps[:, 4, NCMP * i:NCMP * i + NCMP], qa[:, h, t * P:(t + 1) * P],
                                       cmp_k[:, NCMP * (h // 4):NCMP * (h // 4) + NCMP], start=True, stop=True)
                    mm.then_inc(cmp_scored, 1)
                if s == 3:
                    pe.wait_ge(cmp_probs_ready, 1)
                    for i in range(SCORES):
                        mm = pe.transpose(ps[0:NCMP, 4 + i // 4, (i % 4) * P:(i % 4 + 1) * P],
                                          cmp_p[:, NCMP * i:NCMP * i + NCMP], ident)
                        if i % 4 == 3:
                            mm.then_inc(cmp_turned, 1)

            panel(PANELS["vv"], "X", hook=cmp_hook)

            def nsa_scores(i):
                h, t = divmod(i, TT)
                if i >= 2:
                    pe.wait_ge(score_read, SCORES + i - 1)
                for b in range(2):
                    mm = pe.matmul(ps[:, 4 + i % 2, b * T:b * T + P * (t + 1)], qa[:, h, t * P:(t + 1) * P],
                                   k4[:, 2 * b + h // 4, 0:P * (t + 1)], start=True, stop=True)
                mm.then_inc(score_done, 1)

            def nsa_turn(i):
                pe.wait_ge(attn_ready, SCORES + i + 1)
                pe.wait_ge(attn_copied, SCORES + i)
                for b in range(2):
                    for k in range(i % TT + 1):
                        mm = pe.transpose(ps[:, 6, b * T + k * P:b * T + (k + 1) * P],
                                          a_prob[i % 2][:, b * T + k * P:b * T + (k + 1) * P], ident)
                mm.then_inc(attn_turned, 1)

            def nsa_values(i):
                h, t = divmod(i, TT)
                g = h // 4
                pe.wait_ge(attn_copied, SCORES + i + 1)
                pe.wait_ge(o_copied, SCORES + i)
                pe.matmul(ps[:, 7, 0:P], cmp_v[:, g, :], cmp_prob_t[:, i, :], start=True, stop=False)
                for b in range(2):
                    for k in range(t + 1):
                        mm = pe.matmul(ps[:, 7, 0:P], vv[:, k, (2 * b + g) * P:(2 * b + g + 1) * P],
                                       a_prob_t[i % 2][:, b * T + k * P:b * T + (k + 1) * P], start=False,
                                       stop=(b == 1 and k == t))
                mm.then_inc(o_done, 1)

            def nsa_inside(s, b, k):
                if s and b == 1 and k == 2:
                    nsa_turn(s - 1)

            def nsa_after(s):
                if s == 0:
                    pe.wait_ge(cmp_turned_copied, 4)
                    evacuated(pe, PANELS["vv"])
                nsa_scores(s)
                if s:
                    nsa_values(s - 1)

            for m, name in enumerate(("vr", "gr")):
                for p in range(2):
                    panel(PANELS[name] + p, "X", hook=lambda q, p=p, m=m: nsa_after(8 * m + 4 * p + q),
                          pass_hook=lambda q, b, k, p=p, m=m: nsa_inside(8 * m + 4 * p + q, b, k))
            nsa_turn(15)
            nsa_values(15)

            def ret_scores(h):
                if h >= 2:
                    pe.wait_ge(ret_score_ready, h - 1)
                for k, lo, at in ((0, 0, 0), (1, P, T)):
                    for a in range(2):
                        mm = pe.matmul(ps[:, 4 + h % 2, at:at + T - lo], kr[:, 2 * h + a, k * P:(k + 1) * P],
                                       qr[:, 2 * h + a, lo:T], start=(a == 0), stop=(a == 1))
                mm.then_inc(ret_score_done, 1)

            def ret_values(h):
                pe.wait_ge(ret_score_ready, h + 1)
                if h >= 2:
                    pe.wait_ge(ret_o_ready, h - 1)
                for t, k, at in ((0, 0, 0), (1, 0, P), (1, 1, T)):
                    mm = pe.matmul(ps[:, 6 + h % 2, t * T:(t + 1) * T], ret_p[h % 2][:, at:at + P], vr[:, k, h * T:(h + 1) * T],
                                   start=(k == 0), stop=(k == t))
                mm.then_inc(ret_o_done, 1)

            pe.wait_ge(score_read, 2 * SCORES)
            pe.wait_ge(attn_copied, 2 * SCORES)
            pe.wait_ge(o_copied, 2 * SCORES)
            pe.wait_ge(rope_ready, 2)
            evacuated(pe, PANELS["gr"])
            evacuated(pe, PANELS["gr"] + 1)
            ret_scores(0)
            ret_scores(1)
            ret_values(0)
            ret_scores(2)
            ret_values(1)
            ret_scores(3)
            ret_values(2)
            ret_values(3)
            for h in range(4):
                pe.wait_ge(ret_o_ready, h + 1)
                for a in range(2):
                    for t in range(TT):
                        mm = pe.transpose(ps[:, h, a * T + t * P:a * T + (t + 1) * P], ret_o[h][:, t, a * P:(a + 1) * P], ident)
                mm.then_inc(ret_turned, 1)
            pe.wait_ge(ret_turned_copied, 4)
            product("out2", 4, "X")

            pe.wait_ge(act_rows_ready, 5)
            turn_rows(3, token_rows(H_TOK))
            product("up", 16, "W")
            with pe.Fori(0, 2) as i:
                for p in range(2):
                    panel(PANELS["down"] + p, "X", i=i, slots=16, slot=4 * PANELS["down"] + 16 * p)

        @block.vector
        def _(dve):
            steps = [0]

            def then(ins):
                steps[0] += 1
                ins.then_inc(dve_step, 1)
                dve.wait_ge(dve_step, steps[0])

            def split_half(h, turns=0):
                dve.wait_ge(weights_hi, turns + (h + 1))
                if h >= 2:
                    dve.wait_ge(halves_used, turns + (h - 1))
                dve.tensor_tensor(w_lo[:, h % 2], ring_half(h), w_hi[:, h % 2].bitcast(F32), ALU.subtract).then_inc(weights_split, 1)

            split = [0]

            def split_to(count):
                while split[0] < count:
                    split_half(split[0])
                    split[0] += 1

            for col, value in ((EPS_GN, GN_EPS), (EPS_LN, LN_EPS), (EPS_SUB, SUBLN_EPS), (EPS_6, EPS6)):
                ins = dve.memset(col, value)
            ins.then_inc(eps_ready, 1)

            def token_mix(m, quarters=range(4)):
                for q in quarters:
                    s = slice(4 * q, 4 * q + 4)
                    if 1 <= m <= 2:
                        dve.wait_ge(lora_read, 4 * (m - 1) + q + 1)
                    elif m > 2:
                        dve.wait_ge(activation_split, 8 * (4 * (m - 3) + 3) + 2 * q + 2)
                    x, y = hall[:, XT, s], hall[:, MIX, s]
                    dve.tensor_tensor(y[:, :, 1:], x[:, :, 0:T - 1], x[:, :, 1:], ALU.subtract)
                    then(dve.tensor_scalar(y[:, :, 0:1], x[:, :, 0:1], -1.0, None, ALU.mult))
                    then(dve.tensor_tensor(y, y, over(pv(MIXES[m])[:, s], [P, 4, T]), ALU.mult))
                    dve.tensor_tensor(y, y, x, ALU.add).then_inc(mix_ready, 1)

            dve.wait_ge(x_in, 48)
            for m in range(3):
                token_mix(m)
            split_to(2)
            dve.wait_ge(lora_in, 48)
            for j in range(DT):
                if j % 4 == 0:
                    dve.wait_ge(lora_up_copied, j // 4 + 1)
                ins = dve.tensor_tensor_scan(hall[:, LD, j], restart, hall[:, LD, j], 0.0, ALU.mult, ALU.add)
                if j % 4 == 3:
                    ins.then_inc(decay_summed, 1)

            def key_raw(g):
                s = slice(4 * g, 4 * g + 4)
                evacuated(dve, PANELS["k"] + g)
                if g == 0:
                    dve.wait_ge(lora_up_copied, 8)
                dve.tensor_tensor(hall[:, KN, s], hall[:, KK, s], over(pv("k_k")[:, s], [P, 4, T]), ALU.mult)\
                   .then_inc(key_raw_ready, 1)

            def key_group(g, at):
                s = slice(4 * g, 4 * g + 4)
                sq, kn, a, k, ld = key_sq[g % 2], hall[:, KN, s], hall[:, AA, s], hall[:, KK, s], hall[:, LD, s]
                dve.wait_ge(key_norm_ready, g + 1)
                then(dve.tensor_scalar(sq, sq, 1e-12, None, ALU.max))
                for j in range(4):
                    split_to(at + (j + 1) // 2)
                    ins = dve.reciprocal(sq[:, j], sq[:, j])
                then(ins)
                split_to(at + 3)
                then(dve.tensor_tensor(kn, kn, sq, ALU.mult))
                split_to(at + 4)
                then(dve.scalar_tensor_tensor(key_tmp, a, -1.0, over(pv("k_a")[:, s], [P, 4, T]), ALU.add, ALU.mult))
                split_to(at + 5)
                then(dve.scalar_tensor_tensor(k, key_tmp, 1.0, k, ALU.add, ALU.mult))
                split_to(at + 6)
                then(dve.tensor_tensor(a, a, kn, ALU.mult))
                split_to(at + 7)
                dve.wait_ge(decay_exp_ready, g + 1)
                dve.tensor_tensor(a, a, key_exp, ALU.mult)
                split_to(at + 8)
                dve.tensor_tensor(k, k, key_exp, ALU.mult)
                split_to(at + 9)
                chunks = lambda ap: ap.rearrange("p a (c t) -> p (a c) t", t=N)
                dve.tensor_tensor(chunks(kn)[:, :, 1:], chunks(kn)[:, :, 1:], chunks(ld)[:, :, 0:N - 1], ALU.mult)
                split_to(at + 10)
                dve.tensor_copy(wl[:, s], ld.rearrange("p a (c t) -> p a c t", t=N)[:, :, :, N - 1])\
                   .then_inc(key_group_done, 1)

            def mix_behind(m):
                for q in range(4):
                    split_to(HALF[("k", "r", "v")[m - 3]] + 24 + 2 * q + 2)
                    token_mix(m, (q,))

            for g in range(3):
                split_to(ahead(PANELS["k"] + g))
                key_raw(g)
            mix_behind(3)
            split_to(ahead(PANELS["k"] + 3))
            key_raw(3)
            split_to(HALF["r"] + 7)
            key_group(0, HALF["r"] + 7)
            key_group(1, HALF["r"] + 17)
            mix_behind(4)
            split_to(HALF["v"] + 2)
            key_group(2, HALF["v"] + 2)
            split_to(HALF["v"] + 14)
            key_group(3, HALF["v"] + 14)
            for g in range(4):
                s = slice(4 * g, 4 * g + 4)
                evacuated(dve, PANELS["r"] + g)
                dve.tensor_tensor(hall[:, RR, s], hall[:, RR, s], hall[:, LD, s], ALU.mult).then_inc(receptance_done, 1)
                split_to(HALF["v"] + 24 + g // 2)
            mix_behind(5)
            split_to(HALF["out0"])

            computed(dve, PANELS["g"] + 3)
            for c in range(NCH):
                cs = slice(c * N, (c + 1) * N)
                if c:
                    dve.wait_ge(chunk_done, c)
                dve.wait_ge(gram_done, 3 * c + 1)
                then(dve.tensor_tensor(X, gram(0)[:, :, 0], mask(C_NM1), ALU.mult))
                dve.tensor_tensor(X, X, mask(C_ID64), ALU.add)
                dve.tensor_tensor(ARB, gram(0)[:, :, 1], mask(C_UI), ALU.mult).then_inc(gram_masked, 1)
                dve.wait_ge(gram_done, 3 * c + 2)
                dve.tensor_tensor(AAK, gram(1)[:, :, 0], mask(C_U), ALU.mult)
                dve.tensor_tensor(ARK, gram(1)[:, :, 1], mask(C_UI), ALU.mult).then_inc(gram_masked, 1)
                dve.wait_ge(gram_done, 3 * c + 3)
                then(dve.tensor_tensor(AT, wide(0), mask(C_L), ALU.mult))
                then(dve.tensor_tensor(XTR, AT, mask(C_NM1T), ALU.mult))
                dve.tensor_tensor(XTR, XTR, mask(C_ID64), ALU.add).then_inc(gram_masked, 1)
                dve.wait_ge(gram_masked, 3 * c + 3)
                for i in range(5):
                    dve.wait_ge(z_done, 5 * c + i + 1)
                    dve.tensor_tensor(Z, wide(1), mask(C_MB + 64 * i), ALU.mult).then_inc(z_masked, 1)
                    if i:
                        dve.wait_ge(merged, 9 * c + 2 * i)
                    dve.wait_ge(merge_done, 9 * c + 2 * i + 1)
                    dve.tensor_tensor(X, X, wide(2), ALU.subtract).then_inc(merged, 1)
                    if i < 4:
                        dve.wait_ge(merge_done, 9 * c + 2 * i + 2)
                        dve.tensor_tensor(XTR, XTR, wide(3), ALU.subtract).then_inc(merged, 1)
                dve.wait_ge(rhs_done, c + 1)
                then(dve.tensor_tensor(BON, hall[:, RR, :, cs], hall[:, KK, :, cs], ALU.mult))
                dve.tensor_tensor(BON, BON, over(pv("r_k"), [P, DT, N]), ALU.mult).then_inc(head_in_ready, 1)
                dve.wait_ge(state_done, c + 1)
                decay = over(wl[:, :, c], [P, DT, N])
                if c == 0:
                    dve.tensor_tensor(ST, wide(2), decay, ALU.mult).then_inc(state_ready, 1)
                else:
                    then(dve.tensor_tensor(ST, wide(2), ST, ALU.add))
                    dve.tensor_tensor(ST, ST, decay, ALU.mult).then_inc(state_ready, 1)
                dve.wait_ge(state_ready, c + 1)
                dve.wait_ge(head_sum_done, 3 * c + 1)
                then(dve.tensor_tensor(BON, wide(0), hall[:, VV, :, cs], ALU.mult))
                dve.wait_ge(head_sum_done, 3 * c + 2)
                dve.scalar_tensor_tensor(YC, wide(3), -1.0 / N, YC, ALU.mult, ALU.add).then_inc(y_centred, 1)
                dve.wait_ge(y_centred, c + 1)
                dve.wait_ge(head_root_ready, c + 1)
                then(dve.reciprocal(SQ, SQ))
                then(dve.tensor_tensor(YC, YC, SQ, ALU.mult))
                then(dve.tensor_tensor(YC, YC, over(pv("gn_g"), [P, DT, N]), ALU.mult))
                then(dve.tensor_tensor(YC, YC, over(pv("gn_b"), [P, DT, N]), ALU.add))
                then(dve.tensor_tensor(YC, YC, BON, ALU.add))
                dve.tensor_tensor(hall[:, RR, :, cs], YC, hall[:, LD, :, cs], ALU.mult).then_inc(chunk_done, 1)

            def out_rows(name, m):
                z = token_rows(X_TOK)
                dve.wait_ge(rows_in, 48 if m == 0 else 80)
                for p in range(4):
                    n, c = PANELS[name] + p, slice(512 * p, 512 * p + 512)
                    split_to(ahead(n))
                    computed(dve, n)
                    for t in range(TT):
                        ins = dve.scalar_tensor_tensor(z[:, t, c], z[:, t, c], ALPHA, ps[:, 2 * (n % 2) + t, :], ALU.mult, ALU.add)
                    ins.then_inc(panel_evacuated[n % 2], 1)
                    evacuated(dve, n)
                    for t in range(TT):
                        ins = dve.bn_stats(stats[:, t, p, :], z[:, t, c])
                then(ins)
                for t in range(TT):
                    ins = dve.bn_aggr(mean_var[:, t, :], stats[:, t])
                ins.then_inc(ln_var_ready, 1)
                dve.wait_ge(ln_root_ready, m + 1)
                then(dve.reciprocal(root, root))
                for t in range(TT):
                    then(dve.tensor_scalar(z[:, t], z[:, t], mean_var[:, t, 0:1], root[:, t:t + 1], ALU.subtract, ALU.mult))
                    then(dve.tensor_tensor(z[:, t], z[:, t], token_rows(ROWS)[:, 0], ALU.mult))
                    dve.tensor_tensor(z[:, t], z[:, t], token_rows(ROWS)[:, 1], ALU.add).then_inc(tok_ready, 1)

            def copy_turned(v, dst, scale=None):
                for u in range(0, 8, 2):
                    dve.wait_ge(tr_done, 8 * v + u + 1)
                    src = ps[:, 4 + u % 4, :].rearrange("p (a t) -> p a t", a=2)
                    if scale is None:
                        dve.tensor_copy(dst[:, 2 * u:2 * u + 2, :], src).then_inc(tr_copied_v, 1)
                    else:
                        dve.tensor_tensor(dst[:, 2 * u:2 * u + 2, :], src, over(pv(scale)[:, 2 * u:2 * u + 2], [P, 2, T]), ALU.mult)\
                           .then_inc(tr_copied_v, 1)

            out_rows("out0", 0)
            copy_turned(0, hall[:, X_T])

            split_to(HALF["dk"] + 8)
            dve.wait_ge(diff_in, 32)
            then(dve.tensor_tensor(lam_tmp, lam_rows[:, 0:4:2, :], lam_rows[:, 1:4:2, :], ALU.mult))
            dve.tensor_reduce(lam_sum, lam_tmp, AX.X, ALU.add).then_inc(lam_parts, 1)
            split_to(HALF["dk"] + 24)
            dve.wait_ge(lam_exp, 1)
            then(dve.tensor_tensor(lam, lam_sum[:, 1:2], lam_sum[:, 0:1], ALU.subtract))
            then(dve.tensor_scalar(neg_lam, lam, -LAM_INIT, None, ALU.add))

            def diff_logits(i):
                h, t = divmod(i, TT)
                w = P * (t + 1)
                pr = prob[i % 2].rearrange("p (m k) -> p m k", m=2)[:, :, 0:w]
                slope = 2.0 ** (-(8.0 / DH) * (h + 1))
                dve.wait_ge(score_done, i + 1)
                if i >= 2:
                    dve.wait_ge(attn_turned, i - 1)
                dd = dist[:, T - w:T].unsqueeze(1).broadcast_to([P, 2, w])
                dve.scalar_tensor_tensor(pr, dd, -slope / D_SCALE, ps[:, 4 + i % 2, :].rearrange("p (m k) -> p m k", m=2)[:, :, 0:w],
                                         ALU.mult, ALU.add).then_inc(score_read, 1)
                dve.wait_ge(score_read, i + 1)
                then(dve.tensor_reduce(top[i % 2], pr, AX.X, ALU.max))
                dve.tensor_scalar(top[i % 2], top[i % 2], -D_SCALE, None, ALU.mult).then_inc(score_max, 1)

            def diff_weights(i):
                t = i % TT
                w = P * (t + 1)
                pr, r = prob[i % 2], share[i % 2]
                dve.wait_ge(score_exp, i + 1)
                then(dve.reciprocal(r, total[i % 2]))
                then(dve.tensor_tensor(r[:, 1:2], r[:, 1:2], neg_lam, ALU.mult))
                then(dve.tensor_scalar(pr[:, T:T + w], pr[:, T:T + w], r[:, 1:2], None, ALU.mult))
                dve.scalar_tensor_tensor(pr[:, 0:w], pr[:, 0:w], r[:, 0:1], pr[:, T:T + w], ALU.mult, ALU.add)\
                   .then_inc(attn_ready, 1)

            split_to(HALF["dg"] + 3)
            for i in range(SCORES):
                diff_logits(i)
                split_to(min(HALF["dg"] + 2 * i + 4, HALF["out1"]))
                diff_weights(i)
                split_to(min(HALF["dg"] + 2 * i + 5, HALF["out1"]))
            dve.wait_ge(squares_summed, 1)
            then(dve.reciprocal(o_squares, o_squares))
            then(dve.tensor_scalar(o_squares, o_squares, 1.0 - LAM_INIT, None, ALU.mult))
            evacuated(dve, PANELS["dg"] + 2)
            evacuated(dve, PANELS["dg"] + 3)
            for i in range(SCORES):
                h, t = divmod(i, TT)
                o, g = (token_rows(r)[:, t, h * T:(h + 1) * T] for r in (O_TOK, DG))
                ins = dve.scalar_tensor_tensor(o, o, o_squares[:, i:i + 1], g, ALU.mult, ALU.mult)
            ins.then_inc(act_rows_ready, 1)
            copy_turned(1, hall[:, DK], "subln")
            out_rows("out1", 1)

            def unit_rows(k, src, dst):
                dve.wait_ge(post_root_ready, k)
                then(dve.reciprocal(row_root, row_root))
                for t in range(TT):
                    dve.tensor_scalar(token_rows(dst)[:, t], token_rows(src)[:, t], row_root[:, t:t + 1], None, ALU.mult)\
                       .then_inc(act_rows_ready, 1)

            dve.wait_ge(tok_ready, 4)
            unit_rows(1, X_TOK, H_TOK)
            copy_turned(2, hall[:, H_T], "mix_pre")

            split_to(ahead(PANELS["kk"]))
            evacuated(dve, PANELS["cmp"])
            dve.wait_ge(nsa_in, 96)
            for i in range(2):
                for g in range(2):
                    tile = cm[:, 2 * i + g, :]
                    view = bass.AP(tile.tensor, tile.offset, [tile.ap[0], [1, 32], [16, NCMP]])
                    ins = dve.tensor_tensor(windows[i][:, :, g, :], view, over(block_pe[:, 32 * i:32 * i + 32], [P, 32, NCMP]), ALU.add)
                ins.then_inc(blocks_ready, 1)
            for i in range(2):
                split_to(HALF["kr"] + 6 + 2 * i)
                dve.wait_ge(cmp_hid_done, i + 1)
                dve.tensor_tensor(cmp_hid[:, i, :], ps[0:2 * NCMP, 4 + i, 0:P], cmp_b1[:, i, :], ALU.add).then_inc(cmp_step, 1)
            split_to(HALF["kr"] + 12)
            dve.wait_ge(cmp_hid_turned, 1)
            dve.tensor_copy(cmp_hid_t, ps[:, 6, 0:64].rearrange("p (a b) -> p a b", a=2)[:, :, 0:30]).then_inc(cmp_hid_copied, 1)
            split_to(HALF["kr"] + 14)
            dve.wait_ge(cmp_made, 1)
            dve.tensor_copy(cmp_k, ps[:, 4, 0:30]).then_inc(cmp_copied, 1)
            dve.tensor_copy(cmp_v, ps[0:NCMP, 5, 0:2 * P].rearrange("p (g c) -> p g c", g=2)).then_inc(cmp_copied, 1)

            dve.wait_ge(rope_in, 32)
            for x, name in ((kr, "kr"), (qr, "qr")):
                at = ahead(PANELS[name] + 1)
                split_to(at)
                evacuated(dve, PANELS[name])
                evacuated(dve, PANELS[name] + 1)
                x1, x2 = x[:, 0:8:2, :], x[:, 1:8:2, :]
                cos, sin = (rope[:, i, :].unsqueeze(1).broadcast_to([P, 4, T]) for i in range(2))
                dve.tensor_tensor(rope_tmp[0], x1, sin, ALU.mult)
                split_to(at + 1)
                then(dve.tensor_tensor(rope_tmp[1], x2, sin, ALU.mult))
                split_to(at + 2)
                dve.tensor_tensor(x1, x1, cos, ALU.mult)
                then(dve.tensor_tensor(x2, x2, cos, ALU.mult))
                split_to(at + 3)
                dve.tensor_tensor(x1, x1, rope_tmp[1], ALU.subtract)
                dve.tensor_tensor(x2, x2, rope_tmp[0], ALU.add).then_inc(rope_ready, 1)
                dve.wait_ge(rope_ready, 1 if name == "kr" else 2)

            split_to(HALF["vv"] + 6)
            dve.wait_ge(t5_copied, 9)
            dve.wait_ge(cmp_scored, 1)
            cmp_view = cmp_p.rearrange("p (i n) -> p i n", n=NCMP)
            then(dve.scalar_tensor_tensor(cmp_p, ps[:, 4, 0:SCORES * NCMP], A_SCALE, cmp_bias, ALU.mult, ALU.add))
            then(dve.tensor_reduce(cmp_top, cmp_view, AX.X, ALU.max))
            dve.tensor_tensor(cmp_view, cmp_view, over(cmp_top, [P, SCORES, NCMP]), ALU.subtract).then_inc(cmp_centred, 1)
            dve.wait_ge(cmp_exp, 1)
            then(dve.tensor_reduce(cmp_total, cmp_view, AX.X, ALU.add))
            then(dve.reciprocal(cmp_total, cmp_total))
            dve.wait_ge(gates_ready, 1)
            gate = gates.rearrange("p t (h b) -> p h t b", b=3)
            then(dve.tensor_tensor(cmp_total.rearrange("p (h t) -> p h t", t=TT), cmp_total.rearrange("p (h t) -> p h t", t=TT),
                                   gate[:, :, :, 0], ALU.mult))
            then(dve.tensor_tensor(cmp_p, cmp_p, cmp_valid, ALU.mult))
            dve.tensor_tensor(cmp_view, cmp_view, over(cmp_total, [P, SCORES, NCMP]), ALU.mult).then_inc(cmp_probs_ready, 1)

            def nsa_logits(i):
                h, t = divmod(i, TT)
                w = P * (t + 1)
                pr = a_prob[i % 2].rearrange("p (m k) -> p m k", m=2)[:, :, 0:w]
                dve.wait_ge(score_done, SCORES + i + 1)
                if i >= 2:
                    dve.wait_ge(attn_turned, SCORES + i - 1)
                bb = bias[:, h, T - w:T].unsqueeze(1).broadcast_to([P, 2, w])
                dve.scalar_tensor_tensor(pr, ps[:, 4 + i % 2, :].rearrange("p (m k) -> p m k", m=2)[:, :, 0:w], A_SCALE, bb,
                                         ALU.mult, ALU.add).then_inc(score_read, 1)
                dve.wait_ge(score_read, SCORES + i + 1)
                then(dve.tensor_reduce(top[i % 2], pr, AX.X, ALU.max))
                dve.tensor_scalar(top[i % 2], top[i % 2], -1.0, None, ALU.mult).then_inc(score_max, 1)

            def nsa_weights(i):
                h, t = divmod(i, TT)
                w = P * (t + 1)
                r = share[i % 2]
                dve.wait_ge(score_exp, SCORES + i + 1)
                then(dve.reciprocal(r, total[i % 2]))
                then(dve.tensor_tensor(r, r, gates[:, t, 3 * h + 1:3 * h + 3], ALU.mult))
                for b in range(2):
                    pr = a_prob[i % 2][:, b * T:b * T + w]
                    ins = dve.tensor_scalar(pr, pr, r[:, b:b + 1], None, ALU.mult)
                ins.then_inc(attn_ready, 1)

            split_to(HALF["vr"] + 3)
            for i in range(SCORES):
                nsa_logits(i)
                split_to(min(HALF["vr"] + 2 * i + 4, HALF["out2"]))
                nsa_weights(i)
                split_to(min(HALF["vr"] + 2 * i + 5, HALF["out2"]))

            dve.wait_ge(ret_in, 64)
            evacuated(dve, PANELS["gr"])
            evacuated(dve, PANELS["gr"] + 1)

            def ret_weights(h):
                dve.wait_ge(ret_score_done, h + 1)
                if h >= 2:
                    dve.wait_ge(ret_o_done, h - 1)
                dve.tensor_tensor(ret_p[h % 2], ps[:, 4 + h % 2, 0:384], decay_table[h], ALU.mult).then_inc(ret_score_ready, 1)

            def ret_norm(h):
                dve.wait_ge(ret_o_done, h + 1)
                o = ps[:, 6 + h % 2, :].rearrange("p (t c) -> p t c", t=TT)
                st, mv, rt = ret_stats[h % 2], ret_mv[h % 2], ret_root[h % 2]
                for t in range(TT):
                    ins = dve.bn_stats(st[:, t, :], o[:, t, :])
                then(ins)
                for t in range(TT):
                    ins = dve.bn_aggr(mv[:, t, :], st[:, t, :])
                ins.then_inc(ret_var_ready, 1)
                dve.wait_ge(ret_root_ready, h + 1)
                then(dve.reciprocal(rt, rt))
                for t in range(TT):
                    ins = dve.tensor_scalar(ret_o[h][:, t, :], o[:, t, :], mv[:, t, 0:1], rt[:, t:t + 1], ALU.subtract, ALU.mult)
                then(ins)
                dve.tensor_tensor(ret_o[h], ret_o[h], gr[:, :, h * T:(h + 1) * T], ALU.mult).then_inc(ret_o_ready, 1)

            ret_weights(0)
            ret_weights(1)
            ret_norm(0)
            ret_weights(2)
            ret_norm(1)
            ret_weights(3)
            ret_norm(2)
            ret_norm(3)

            def add_rows(k, src, row, dst, done):
                dve.wait_ge(post_root_ready, k)
                dve.wait_ge(post_in, 32)
                then(dve.reciprocal(row_root, row_root))
                for t in range(TT):
                    y = token_rows(src)[:, t]
                    then(dve.scalar_tensor_tensor(y, y, row_root[:, t:t + 1], token_rows(POST)[:, row], ALU.mult, ALU.mult))
                    dve.tensor_tensor(token_rows(dst)[:, t], y, token_rows(X_TOK)[:, t], ALU.add).then_inc(done, 1)

            split_to(HALF["up"])
            add_rows(2, MIX_TOK, 0, X_TOK, post_rows_ready)
            dve.wait_ge(post_rows_ready, 2)
            unit_rows(3, X_TOK, H_TOK)
            copy_turned(3, hall[:, H_T], "mlp_pre")
            split_to(HALF["up"] + 2)
            with dve.Fori(0, 8) as i:
                for p in range(2):
                    n = PANELS["up"] + p
                    for h in range(8 * n + 2, 8 * n + 10):
                        split_half(h, i * 16)
                    dve.wait_ge(halves_used, i * 16 + 8 * (n + 1))
                    four = up[:, bass.ds(i * 8 + 4 * p, 4), :]
                    dve.tensor_scalar(four, ps[:, 2 * (n % 2):2 * (n % 2) + 2, :].rearrange("p b (a t) -> p (b a) t", a=2),
                                      0.0, None, ALU.max).then_inc(panel_evacuated[n % 2], 1)
                    dve.wait_ge(panel_evacuated[n % 2], i + (n // 2 + 1))
                    dve.tensor_tensor(four, four, four, ALU.mult).then_inc(up_squared, 1)
            h0 = HALF["down"] + 2
            turns = (2 * SLOTS - h0) // TURN
            with dve.Fori(0, turns) as i:
                for h in range(h0, h0 + TURN):
                    split_half(h, i * TURN)
            for h in range(h0 + turns * TURN, 2 * SLOTS):
                split_half(h)
            add_rows(4, H_TOK, 1, H_TOK, out_rows_ready)

        @block.scalar
        def _(act):
            steps = [0]

            def then(ins):
                steps[0] += 1
                ins.then_inc(act_step, 1)
                act.wait_ge(act_step, steps[0])

            def activation_ready(h):
                name, tile = product_of(h)
                q = tile // 4
                if name in ("k", "r", "v", "g"):
                    act.wait_ge(mix_ready, 4 * (("k", "r", "v", "g").index(name) + 2) + q + 1)
                elif name == "out0":
                    act.wait_ge(chunk_done, NCH)
                elif name in ("dk", "out1", "cmp", "up"):
                    v = ("dk", "out1", "cmp", "up").index(name)
                    act.wait_ge(tr_copied_v, 4 * v + q + 1)
                    act.wait_ge(tr_copied_a, 4 * v + q + 1)
                elif name == "out2":
                    act.wait_ge(ret_turned_copied, 4)
                elif name == "down":
                    act.wait_ge(up_squared, q + 1)

            def split_half(h, turns=0):
                name, tile = product_of(h)
                if h % 2 == 0:
                    s = h // 2
                    act.wait_ge(slot_landed[s % RING], turns * (16 // TURN) + 16 * (s // RING + 1))
                if h >= 2:
                    act.wait_ge(halves_used, turns + (h - 1))
                act.activation(w_hi[:, h % 2], ring_half(h), ACT.Copy).then_inc(weights_hi, 1)
                if h - HALF[name] < (32 if name == "down" else 8):
                    activation_ready(h)
                act.activation(a_hi[:, h % 2], operand[name][:, tile:tile + 2], ACT.Copy).then_inc(activation_hi, 1)

            split = [0]

            def split_to(count):
                while split[0] < count:
                    split_half(split[0])
                    split[0] += 1

            def evacuate(n, dst, func=ACT.Copy):
                split_to(ahead(n))
                computed(act, n)
                for b in range(2):
                    ins = act.activation(dst[:, 2 * b:2 * b + 2, :], ps[:, 2 * (n % 2) + b, :].rearrange("p (a t) -> p a t", a=2), func)
                ins.then_inc(panel_evacuated[n % 2], 1)

            for h in range(8):
                act.wait_ge(t5_done, h + 1)
                act.activation(t5_rows[:, h, :], ps[:, 4 + h % 2, 0:384], ACT.Copy).then_inc(t5_copied, 1)
            act.wait_ge(t5_done, 9)
            act.activation(cmp_bias, ps[:, 6, 0:240], ACT.Copy).then_inc(t5_copied, 1)
            act.wait_ge(lora_read, 4)
            act.activation(lora_hid[:, 0], ps[0:LORA, 4, 0:T], ACT.Tanh).then_inc(lora_hid_copied, 1)
            act.wait_ge(lora_read, 8)
            act.activation(lora_hid[:, 1], ps[0:LORA, 5, 0:T], ACT.Copy).then_inc(lora_hid_copied, 1)
            split_to(2)
            for u in range(8):
                act.wait_ge(lora_up_done, u + 1)
                for c in range(4):
                    j = 4 * (u % 4) + c
                    ins = act.activation(hall[:, (LD, AA)[u // 4], j], ps[:, 4 + 2 * (u % 2) + c // 2, (c % 2) * T:(c % 2 + 1) * T],
                                         ACT.Sigmoid, bias=pv(("w0", "a0")[u // 4])[:, j:j + 1])
                ins.then_inc(lora_up_copied, 1)
            def square_keys(g):
                act.wait_ge(key_raw_ready, g + 1)
                if g >= 2:
                    act.wait_ge(key_group_done, g - 1)
                act.activation(key_sq[g % 2], hall[:, KN, 4 * g:4 * g + 4], ACT.Square).then_inc(key_squared, 1)

            def key_roots(g):
                act.wait_ge(key_norm_summed, g + 1)
                act.activation(key_sq[g % 2], ps[:, 4 + 2 * (g % 2):6 + 2 * (g % 2), :].rearrange("p b (a t) -> p (b a) t", a=2),
                               ACT.Sqrt).then_inc(key_norm_ready, 1)
                act.wait_ge(decay_summed, g + 1)
                if g >= 1:
                    act.wait_ge(key_group_done, g)
                ld = hall[:, LD, 4 * g:4 * g + 4]
                then(act.activation(key_exp, ld, ACT.Exp, scale=-DECAY))
                act.activation(ld, ld, ACT.Exp, scale=DECAY).then_inc(decay_exp_ready, 1)

            for p in range(4):
                evacuate(PANELS["k"] + p, hall[:, KK, 4 * p:4 * p + 4])
                if p in (1, 2):
                    square_keys(p - 1)
            split_to(HALF["r"] + 6)
            key_roots(0)
            act.wait_ge(t5_stored, 16)
            evacuate(PANELS["r"], hall[:, RR, 0:4])
            evacuate(PANELS["r"] + 1, hall[:, RR, 4:8])
            key_roots(1)
            split_to(HALF["r"] + 19)
            square_keys(2)
            evacuate(PANELS["r"] + 2, hall[:, RR, 8:12])
            split_to(HALF["r"] + 29)
            square_keys(3)
            key_roots(2)
            evacuate(PANELS["r"] + 3, hall[:, RR, 12:16])
            evacuate(PANELS["v"], hall[:, VV, 0:4])
            split_to(HALF["v"] + 13)
            key_roots(3)
            for p in range(1, 4):
                evacuate(PANELS["v"] + p, hall[:, VV, 4 * p:4 * p + 4])
            act.wait_ge(receptance_done, 4)
            for p in range(4):
                evacuate(PANELS["g"] + p, hall[:, LD, 4 * p:4 * p + 4], ACT.Silu)
            act.wait_ge(eps_ready, 1)
            for c in range(NCH):
                for w, dst in enumerate((BTOK, KTOK, VTOK)):
                    act.wait_ge(turned, 3 * c + w + 1)
                    act.activation(dst, wide(w), ACT.Copy).then_inc(turned_copied, 1)
                act.wait_ge(rhs_done, c + 1)
                act.activation(RHS, wide(3), ACT.Copy, scale=-1.0).then_inc(rhs_ready, 1)
                act.wait_ge(u_done, c + 1)
                act.activation(U, wide(0), ACT.Copy).then_inc(u_ready, 1)
                act.wait_ge(y_done, c + 1)
                act.wait_ge(head_in_ready, 3 * c + 1)
                act.activation(YC, wide(1), ACT.Copy).then_inc(head_in_ready, 1)
                act.wait_ge(y_centred, c + 1)
                act.activation(SQ, YC, ACT.Square).then_inc(head_in_ready, 1)
                act.wait_ge(head_sum_done, 3 * c + 3)
                act.activation(SQ, wide(1), ACT.Sqrt, scale=1.0 / N, bias=EPS_GN).then_inc(head_root_ready, 1)

            def copy_turned(v, dst, scale=None):
                for u in range(1, 8, 2):
                    act.wait_ge(tr_done, 8 * v + u + 1)
                    src = ps[:, 4 + u % 4, :].rearrange("p (a t) -> p a t", a=2)
                    if scale is None:
                        ins = act.activation(dst[:, 2 * u:2 * u + 2, :], src, ACT.Copy)
                    else:
                        for a in range(2):
                            ins = act.activation(dst[:, 2 * u + a, :], src[:, a, :], ACT.Copy, scale=pv(scale)[:, 2 * u + a:2 * u + a + 1])
                    ins.then_inc(tr_copied_a, 1)

            def evacuate_rows(n, dst, func=ACT.Copy):
                split_to(ahead(n))
                computed(act, n)
                for t in range(TT):
                    ins = act.activation(dst[:, t, :], ps[:, 2 * (n % 2) + t, :], func)
                ins.then_inc(panel_evacuated[n % 2], 1)

            def norm_root(m):
                act.wait_ge(ln_var_ready, m + 1)
                act.activation(root, mean_var[:, :, 1], ACT.Sqrt, bias=EPS_LN).then_inc(ln_root_ready, 1)

            split_to(HALF["dk"])
            norm_root(0)
            copy_turned(0, hall[:, X_T])
            for p in range(4):
                evacuate(PANELS["dk"] + p, hall[:, DK, 4 * p:4 * p + 4])
                if p == 0:
                    act.wait_ge(lam_parts, 1)
                    act.activation(lam_sum, lam_sum, ACT.Exp).then_inc(lam_exp, 1)
            for p in range(4):
                evacuate(PANELS["dq"] + p, hall[:, DQ, 4 * p:4 * p + 4])
            for p in range(4):
                evacuate_rows(PANELS["dv"] + p, token_rows(DV)[:, :, 512 * p:512 * p + 512])

            def diff_exp(i):
                w = P * (i % TT + 1)
                act.wait_ge(score_max, i + 1)
                for m in range(2):
                    pr = prob[i % 2][:, m * T:m * T + w]
                    ins = act.activation(pr, pr, ACT.Exp, bias=top[i % 2][:, m:m + 1], scale=D_SCALE, accum_out=total[i % 2][:, m:m + 1])
                ins.then_inc(score_exp, 1)

            def diff_copy_attn(i):
                w = P * (i % TT + 1)
                act.wait_ge(attn_turned, i + 1)
                if i >= 2:
                    act.wait_ge(o_done, i - 1)
                act.activation(prob_t[i % 2][:, 0:w], ps[:, 6, 0:w], ACT.Copy).then_inc(attn_copied, 1)

            def diff_copy_o(i):
                h, t = divmod(i, TT)
                act.wait_ge(o_done, i + 1)
                act.activation(junk, ps[:, 7, 0:T], ACT.Square, accum_out=o_squares[:, i:i + 1])
                act.activation(token_rows(O_TOK)[:, t, h * T:(h + 1) * T], ps[:, 7, 0:T], ACT.Copy).then_inc(o_copied, 1)

            for s in range(SCORES):
                split_to(min(HALF["dg"] + 2 * s + 4, HALF["out1"]))
                diff_exp(s)
                if s % 4 == 3:
                    p = s // 4
                    evacuate_rows(PANELS["dg"] + p, token_rows(DG)[:, :, 512 * p:512 * p + 512], ACT.Silu)
                if s:
                    diff_copy_o(s - 1)
                split_to(min(HALF["dg"] + 2 * s + 5, HALF["out1"]))
                diff_copy_attn(s)
            diff_copy_o(SCORES - 1)
            act.wait_ge(o_copied, SCORES)
            act.activation(o_squares, o_squares, ACT.Sqrt, scale=1.0 / T, bias=EPS_SUB).then_inc(squares_summed, 1)
            copy_turned(1, hall[:, DK], "subln")
            split_to(HALF["cmp"])
            norm_root(1)

            def row_rms(src, ready, dump):
                for t in range(TT):
                    act.wait_ge(ready[0], ready[1] + t)
                    ins = act.activation(token_rows(dump)[:, t], token_rows(src)[:, t], ACT.Square, accum_out=row_squares[:, t, 0:1])
                then(ins)
                act.activation(row_root, row_squares[:, :, 0], ACT.Sqrt, scale=1.0 / D, bias=EPS_6).then_inc(post_root_ready, 1)

            row_rms(X_TOK, (tok_ready, 3), DG)
            copy_turned(2, hall[:, H_T], "mix_pre")
            evacuate(PANELS["cmp"], cm)
            evacuate(PANELS["kk"], k4)
            split_to(HALF["kr"] + 4)
            act.wait_ge(gate_sum_done, 1)
            act.activation(gate_sum, ps[0:24, 6, 0:T], ACT.Copy).then_inc(gate_sum_copied, 1)
            for i in range(2):
                split_to(HALF["kr"] + 6 + 2 * i)
                act.wait_ge(cmp_step, i + 1)
                act.activation(cmp_hid[:, i, :], cmp_hid[:, i, :], ACT.Gelu_apprx_tanh).then_inc(cmp_hid_ready, 1)
            split_to(HALF["kr"] + 10)
            act.wait_ge(gate_turned, 1)
            act.activation(gates, ps[:, 7, 0:48].rearrange("p (t b) -> p t b", t=TT), ACT.Sigmoid).then_inc(gates_ready, 1)
            for name, dst in (("kr", kr), ("qr", qr), ("qa", qa)):
                for p in range(2):
                    evacuate(PANELS[name] + p, dst[:, 4 * p:4 * p + 4])
            split_to(HALF["vv"] + 6)
            act.wait_ge(cmp_centred, 1)
            act.activation(cmp_p, cmp_p, ACT.Exp).then_inc(cmp_exp, 1)
            split_to(ahead(PANELS["vv"]))
            for i in range(4):
                act.wait_ge(cmp_turned, i + 1)
                act.activation(cmp_prob_t[:, 4 * i:4 * i + 4, :], ps[0:NCMP, 4 + i, :].rearrange("p (i q) -> p i q", i=4), ACT.Copy)\
                   .then_inc(cmp_turned_copied, 1)
            evacuate_rows(PANELS["vv"], vv)

            def nsa_exp(i):
                w = P * (i % TT + 1)
                act.wait_ge(score_max, SCORES + i + 1)
                for m in range(2):
                    pr = a_prob[i % 2][:, m * T:m * T + w]
                    ins = act.activation(pr, pr, ACT.Exp, bias=top[i % 2][:, m:m + 1], accum_out=total[i % 2][:, m:m + 1])
                ins.then_inc(score_exp, 1)

            def nsa_copy_attn(i):
                w = P * (i % TT + 1)
                act.wait_ge(attn_turned, SCORES + i + 1)
                if i >= 2:
                    act.wait_ge(o_done, SCORES + i - 1)
                view = lambda ap: ap.rearrange("p (m k) -> p m k", m=2)[:, :, 0:w]
                act.activation(view(a_prob_t[i % 2]), view(ps[:, 6, :]), ACT.Copy).then_inc(attn_copied, 1)

            def nsa_copy_o(i):
                h, t = divmod(i, TT)
                act.wait_ge(o_done, SCORES + i + 1)
                act.activation(hall[:, CAT_T, h, t * P:(t + 1) * P], ps[:, 7, 0:P], ACT.Copy).then_inc(o_copied, 1)

            act.wait_ge(rope_ready, 2)
            for s in range(SCORES):
                split_to(min(HALF["vr"] + 2 * s + 4, HALF["out2"]))
                nsa_exp(s)
                if s % 4 == 3:
                    p = (s // 4) % 2
                    evacuate_rows(PANELS[("vr", "gr")[s // 8]] + p, (vr, gr)[s // 8][:, :, 512 * p:512 * p + 512],
                                  (ACT.Copy, ACT.Silu)[s // 8])
                if s:
                    nsa_copy_o(s - 1)
                split_to(min(HALF["vr"] + 2 * s + 5, HALF["out2"]))
                nsa_copy_attn(s)
            nsa_copy_o(SCORES - 1)
            for h in range(4):
                act.wait_ge(ret_var_ready, h + 1)
                act.activation(ret_root[h % 2], ret_mv[h % 2][:, :, 1], ACT.Sqrt, bias=EPS_6).then_inc(ret_root_ready, 1)
            for h in range(4):
                act.wait_ge(ret_turned, h + 1)
                act.activation(hall[:, CAT_T, 8 + 2 * h:10 + 2 * h, :], ps[:, h, :].rearrange("p (a t) -> p a t", a=2), ACT.Copy)\
                   .then_inc(ret_turned_copied, 1)

            def summed_rows(name, dst, dump, halves):
                for p in range(4):
                    n, done = PANELS[name] + p, HALF[name] + halves * (p + 1)
                    split_to(min(done + 2, HALF[name] + 4 * halves))
                    act.wait_ge(halves_used, done)
                    for t in range(TT):
                        act.activation(token_rows(dump)[:, t, 512 * p:512 * p + 512], ps[:, 2 * (n % 2) + t, :], ACT.Square, accum_out=row_squares[:, t, p:p + 1])
                    for t in range(TT):
                        ins = act.activation(token_rows(dst)[:, t, 512 * p:512 * p + 512], ps[:, 2 * (n % 2) + t, :], ACT.Copy)
                    ins.then_inc(panel_evacuated[n % 2], 1)
                evacuated(act, PANELS[name] + 3)
                for t in range(TT):
                    ins = act.activation(token_rows(dump)[:, t, 0:4], row_squares[:, t, :], ACT.Copy, accum_out=row_root[:, t:t + 1])
                then(ins)
                act.activation(row_root, row_root, ACT.Sqrt, scale=1.0 / D, bias=EPS_6).then_inc(post_root_ready, 1)

            summed_rows("out2", MIX_TOK, VR_GR, 8)
            row_rms(X_TOK, (post_rows_ready, 1), VR_GR)
            copy_turned(3, hall[:, H_T], "mlp_pre")
            with act.Fori(0, 8) as i:
                for h in range(HALF["up"], HALF["up"] + 16):
                    split_half(h, i * 16)
            split[0] = HALF["down"]
            summed_rows("down", H_TOK, H_T, 32)


def kernel(**inputs):
    import concourse.bacc as bacc
    from concourse.bass_utils import run_bass_kernel_spmd as run

    a = {k: np.asarray(v) for k, v in inputs.items()}
    nc = bacc.Bacc("TRN2", target_bir_lowering=False, num_devices=1)
    arrays, d = {}, {}

    def give(name, value):
        value = np.ascontiguousarray(value)
        arrays[name] = value
        d[name] = nc.dram_tensor(name, value.shape, mybir.dt.from_np(value.dtype), kind="ExternalInput").ap()

    def tiles(w):
        return w.reshape(DT, P, -1).transpose(1, 0, 2).reshape(P, -1)

    def rows_of(w):
        return w.reshape(TT, P, -1).transpose(1, 0, 2).reshape(P, -1)

    x = a["x"][0]
    slots = []

    def stream(w, columns=None):
        columns = np.arange(w.shape[1]) if columns is None else columns
        for c in range(0, len(columns), 512):
            slots.append(slot_panels(w, columns[c:c + 512]))

    stream(a["a_w_in"][0, 1])
    stream(a["a_w_in"][0, 0])
    stream(a["a_w_in"][0, 2])
    stream(a["a_w_in"][0, 3])
    stream(a["a_w_out"][0])
    stream(a["w_k_shared"])
    stream(a["b_w_qg"][0], np.arange(D))
    stream(a["w_v_shared"])
    stream(a["b_w_qg"][0], np.arange(D, 2 * D))
    stream(a["b_w_out"][0])
    w_in, kv = a["w_in_2"][0], [np.arange(1024 + 256 * i, 1280 + 256 * i) for i in range(6)]
    ret = [np.arange(2584 + 1024 * i, 3608 + 1024 * i) for i in range(4)]
    for columns in ((kv[0], kv[1]), (kv[2], kv[4]), (ret[1],), (ret[0],), (np.arange(1024),), (kv[3], kv[5]), (ret[2],), (ret[3],)):
        stream(w_in, np.concatenate(columns))
    stream(a["w_out_2"][0])
    stream(a["w_up_2"][0])
    stream(a["w_down_2"][0])
    give("stream", np.concatenate(slots))
    d["slots"] = arrays["stream"].shape[0]
    give("x_channels", tiles(x.T))
    give("resident", resident_constants())
    vectors = {
        "mu_r": a["a_mu_proj"][0, 0], "mu_k": a["a_mu_proj"][0, 1], "mu_v": a["a_mu_proj"][0, 2],
        "mu_g": a["a_mu_proj"][0, 3], "mu_w": a["a_mu_lora"][0, 0], "mu_a": a["a_mu_lora"][0, 1],
        "w0": a["a_w0"][0], "a0": a["a_a0"][0], "k_k": a["a_k_k"][0], "k_a": a["a_k_a"][0],
        "r_k": a["a_r_k"][0].reshape(-1), "gn_g": a["a_gn_g"][0], "gn_b": a["a_gn_b"][0],
        "mix_pre": a["norm_mix_pre_2"][0], "mlp_pre": a["norm_mlp_pre_2"][0],
        "subln": np.tile(a["b_subln_g"][0], DH),
    }
    give("params", np.stack([vectors[name].reshape(DT, P).T for name in PV], 1).reshape(P, -1))
    give("lora1", np.concatenate([tiles(a["a_w1"][0]), tiles(a["a_a1"][0])], 1))
    give("lora2", np.concatenate([a["a_w2"][0], a["a_a2"][0]], 1))
    give("restart", np.broadcast_to((np.arange(T) % N != 0).astype(np.float32), (P, T)))
    give("x_tokens", rows_of(x))
    give("rows", np.stack([a["ln_g"][0], a["ln_b"][0], a["ln_g"][1], a["ln_b"][1], a["norm_mix_post_2"][0],
                           a["norm_mlp_post_2"][0]]))
    give("dist", diff_constants())
    give("lambda", a["b_lambda"][0].reshape(-1))
    give("t5_table", np.broadcast_to(np.concatenate([a["t5_bias_2"], np.full((1, 8), NEG, np.float32)])[:, :, None],
                                     (33, 8, P)).reshape(33, -1))
    give("t5_one", t5_constants())
    give("cmp_small", np.concatenate([a["cmp_pe_k_2"][0].T, a["cmp_pe_v_2"][0].T, a["cmp_w2_k_2"][0], a["cmp_w2_v_2"][0]], 1))
    give("cmp_b1", np.concatenate([a["cmp_b1_k_2"][0], a["cmp_b1_v_2"][0]]))
    give("cmp_w1", np.stack([a[k][0].reshape(32, P, P).transpose(1, 0, 2).reshape(P, -1) for k in ("cmp_w1_k_2", "cmp_w1_v_2")]))
    give("gate_w", tiles(w_in[:, 2560:2584]))
    give("rope", rope_constants().reshape(P, -1))
    give("valid", np.broadcast_to(valid_constants()[:, None], (P, 8, TT, NCMP)).reshape(P, -1))
    give("decay", decay_constants().reshape(P, -1))
    d["t5_scratch"] = nc.dram_tensor("t5_scratch", (8, P, 384), F32, kind="Internal").ap()
    d["out"] = nc.dram_tensor("out", (T, D), F32, kind="ExternalOutput").ap()
    build(nc, d)
    r = run(nc, [arrays], core_ids=[0])
    return r.results[0]["out"].reshape(1, T, D)
```

```python
from contextlib import ExitStack
import math

import numpy as np

import concourse.bass as bass
from concourse import mybir

F32 = mybir.dt.float32
F32R = mybir.dt.float32r
ALU = mybir.AluOpType
ACT = mybir.ActivationFunctionType
AX = mybir.AxisListType

P = 128
D = 2048
T = 256
DT = D // P
TT = T // P
N = 64
NCH = T // N
LORA = 96
ALPHA = (2.0 * 2) ** 0.25
LN_EPS = 1e-5
RING = 4
TURN = 2 * RING
DECAY = -math.exp(-0.5)
GN_EPS = 64e-5

DH = 8
D_SCALE = 128 ** -0.5
LAM_INIT = 0.8 - 0.6 * math.exp(-0.3 * 1)
SUBLN_EPS = 1e-5
A_SCALE = 128 ** -0.5
NCMP = 15
NEG = -1e30
EPS6 = 1e-6

PANELS = {}
_n = 0
for _name, _count in (("k", 4), ("r", 4), ("v", 4), ("g", 4), ("out0", 4), ("dk", 4), ("dq", 4), ("dv", 4), ("dg", 4),
                      ("out1", 4), ("cmp", 1), ("kk", 1), ("kr", 2), ("qr", 2), ("qa", 2), ("vv", 1), ("vr", 2),
                      ("gr", 2), ("out2", 4), ("up", 16), ("down", 4)):
    PANELS[_name] = _n
    _n += _count
SLOTS = 4 * PANELS["down"] + 4 * 16
HALF = {name: 8 * first for name, first in PANELS.items()}
GROUP_ENDS = [HALF[name] for name in ("out0", "dk", "out1", "cmp", "out2", "up", "down")] + [2 * SLOTS]

PV = {name: i for i, name in enumerate(
    ("mu_w", "mu_a", "mu_k", "mu_r", "mu_v", "mu_g", "w0", "a0", "k_k", "k_a", "r_k", "gn_g", "gn_b", "mix_pre",
     "mlp_pre", "subln"))}
MIXES = ("mu_w", "mu_a", "mu_k", "mu_r", "mu_v", "mu_g")

C_ID, C_ONES64, C_ID64, C_NM1, C_NM1T, C_MB, C_U, C_UI = 0, 128, 256, 320, 384, 448, 768, 832
C_COLS = 960


def resident_constants():
    c = np.zeros((P, C_COLS), np.float32)
    c[:, C_ID:C_ID + P] = np.eye(P)
    c[:64, C_ONES64:C_ONES64 + 64] = 1
    c[64:, C_ONES64 + 64:C_ONES64 + 128] = 1
    r, s = np.arange(P)[:, None] % 64, np.arange(64)[None, :]
    c[:, C_ID64:C_ID64 + 64] = r == s

    def merge(b, lo, hi):
        return (lo // (2 * b) == hi // (2 * b)) & (lo % (2 * b) < b) & (hi % (2 * b) >= b)

    c[:, C_NM1:C_NM1 + 64] = -1.0 * merge(1, r, s)
    c[:, C_NM1T:C_NM1T + 64] = -1.0 * merge(1, s, r)
    for i, b in enumerate((2, 4, 8, 16, 32)):
        c[:, C_MB + 64 * i:C_MB + 64 * i + 64] = merge(b, r, s)
    c[:, C_U:C_U + 64] = r < s
    c[:, C_UI:C_UI + 64] = r <= s
    return c


def diff_constants():
    q, k = 128 + np.arange(P)[:, None], np.arange(T)[None, :]
    return np.where(k // 64 <= q // 64, np.abs(q - k), 1e30).astype(np.float32)


def t5_buckets(rel):
    n = np.maximum(rel, 0)
    nf = np.maximum(n, 1).astype(np.float32)
    large = 16 + (np.log(nf / np.float32(16)) / np.float32(np.log(128 / 16)) * np.float32(16)).astype(np.int32)
    return np.where(n < 16, n, np.minimum(large, 31))


def t5_constants():
    rel = np.concatenate([255 - np.arange(384), np.arange(512) - 255])
    one = np.zeros((33, 896), np.float32)
    one[np.where(rel < 0, 32, t5_buckets(rel)), np.arange(896)] = 1
    return one


def valid_constants():
    t = np.arange(T).reshape(TT, P).T[:, :, None]
    return (t >= 16 * np.arange(NCMP) + 31).astype(np.float32)


def rope_constants():
    inv = (np.float32(10000.0) ** (-np.arange(0, 256, 2, dtype=np.float32) / np.float32(256))).astype(np.float32)
    ang = (np.arange(T, dtype=np.float32)[:, None] * inv[None, :]).astype(np.float32)
    return np.stack([np.cos(ang).T, np.sin(ang).T], 1).astype(np.float32)


def decay_constants():
    lg = np.log(1.0 - np.exp2(-5.0 - np.arange(4)))
    m = np.arange(P)[:, None]
    out = np.zeros((P, 4, 384))
    for h in range(4):
        d0 = np.arange(T)[None, :] - m
        d1 = np.arange(P)[None, :] - m
        out[:, h, :256] = np.where(d0 >= 0, np.exp(np.maximum(d0, 0) * lg[h]), 0)
        out[:, h, 256:] = np.where(d1 >= 0, np.exp(np.maximum(d1, 0) * lg[h]), 0)
    return (out / 16.0).astype(np.float32)


def slot_panels(w, columns):
    part = w[:, columns]
    return part.reshape(-1, 4, P, 512).transpose(0, 2, 1, 3).reshape(-1, P, 2048)


def build(nc, d):
    ctx = ExitStack()
    with ctx:
        def sb(name, shape, kind=F32):
            return ctx.enter_context(nc.sbuf_tensor(name, shape, kind))

        def sem(name):
            return ctx.enter_context(nc.semaphore(name))

        ring = sb("ring", [P, RING, 4, 512])
        w_hi, w_lo = sb("w_hi", [P, 2, 2, 512], F32R), sb("w_lo", [P, 2, 2, 512], F32R)
        a_hi, a_lo = sb("a_hi", [P, 2, 2, T], F32R), sb("a_lo", [P, 2, 2, T], F32R)
        key_work = sb("key_work", [P, 2, 4, T])
        hall = sb("hall", [P, 8, DT, T])
        work = sb("work", [P, 2, DT, N])
        con = sb("con", [P, C_COLS])
        par = sb("par", [P, 16, DT])
        wl = sb("wl", [P, DT, NCH])
        small = sb("small", [P, 464])
        ps = ctx.enter_context(nc.psum_tensor("ps", [P, 8, 512], F32))

        XT, MIX, LD, AA, KK, KN, RR, VV = range(8)
        flat = [hall[:, i].rearrange("p a b -> p (a b)") for i in range(8)]
        ident = con[:, C_ID:C_ID + P]
        ones64 = con[:, C_ONES64:C_ONES64 + P]
        id64 = con[:, C_ID64:C_ID64 + 64]

        def pv(name):
            return par[:, PV[name], :]

        def over(ap, shape):
            return ap.unsqueeze(2).broadcast_to(shape)

        def mask(column, width=DT):
            return con[:, column:column + 64].unsqueeze(1).broadcast_to([P, width, 64])

        slot_landed = [sem(f"slot_landed{i}") for i in range(RING)]
        weights_hi = sem("weights_hi")
        activation_hi = sem("activation_hi")
        weights_split = sem("weights_split")
        activation_split = sem("activation_split")
        halves_used = sem("halves_used")
        panel_evacuated = [sem("even_panel_evacuated"), sem("odd_panel_evacuated")]
        x_in = sem("x_in")
        lora_in = sem("lora_in")
        mix_ready = sem("mix_ready")
        lora_read = sem("lora_read")
        lora_hid_copied = sem("lora_hid_copied")
        lora_up_done = sem("lora_up_done")
        lora_up_copied = sem("lora_up_copied")
        key_raw_ready = sem("key_raw_ready")
        key_squared = sem("key_squared")
        key_norm_summed = sem("key_norm_summed")
        key_norm_ready = sem("key_norm_ready")
        decay_summed = sem("decay_summed")
        decay_exp_ready = sem("decay_exp_ready")
        key_group_done = sem("key_group_done")
        receptance_done = sem("receptance_done")
        gram_done = sem("gram_done")
        dve_step = sem("dve_step")
        act_step = sem("act_step")
        gram_masked = sem("gram_masked")
        z_done = sem("z_done")
        z_masked = sem("z_masked")
        merge_done = sem("merge_done")
        merged = sem("merged")
        turned = sem("turned")
        turned_copied = sem("turned_copied")
        rhs_done = sem("rhs_done")
        rhs_ready = sem("rhs_ready")
        u_done = sem("u_done")
        u_ready = sem("u_ready")
        y_done = sem("y_done")
        y_copied = sem("y_copied")
        state_done = sem("state_done")
        state_ready = sem("state_ready")
        head_sum_done = sem("head_sum_done")
        bonus_ready = sem("bonus_ready")
        gain_applied = sem("gain_applied")
        x_turned = sem("x_turned")
        xt_copied = sem("xt_copied")
        o_scaled = sem("o_scaled")
        bonus_added = sem("bonus_added")
        y_squared = sem("y_squared")
        head_root_ready = sem("head_root_ready")
        out_rows_ready = sem("out_rows_ready")
        rows_in = sem("rows_in")
        ln_var_ready = sem("ln_var_ready")
        ln_root_ready = sem("ln_root_ready")
        act_rows_ready = sem("act_rows_ready")
        tok_ready = sem("tok_ready")
        tr_done = sem("tr_done")
        tr_copied_v = sem("tr_copied_v")
        tr_copied_a = sem("tr_copied_a")
        diff_in = sem("diff_in")
        lam_parts = sem("lam_parts")
        lam_exp = sem("lam_exp")
        score_done = sem("score_done")
        score_max = sem("score_max")
        score_exp = sem("score_exp")
        attn_ready = sem("attn_ready")
        attn_turned = sem("attn_turned")
        attn_copied = sem("attn_copied")
        o_done = sem("o_done")
        o_copied = sem("o_copied")
        nsa_in = sem("nsa_in")
        t5_done = sem("t5_done")
        t5_copied = sem("t5_copied")
        t5_stored = sem("t5_stored")
        blocks_ready = sem("blocks_ready")
        cmp_step = sem("cmp_step")
        rope_ready = sem("rope_ready")
        ret_score_done = sem("ret_score_done")
        ret_score_ready = sem("ret_score_ready")
        ret_o_done = sem("ret_o_done")
        ret_o_ready = sem("ret_o_ready")
        ret_var_ready = sem("ret_var_ready")
        ret_root_ready = sem("ret_root_ready")
        out_stored = sem("out_stored")
        chunk_done = sem("chunk_done")
        eps_ready = sem("eps_ready")
        y_centred = sem("y_centred")
        ret_in = sem("ret_in")


        more = ("squares_summed score_read post_in cmp_hid_done cmp_hid_ready cmp_hid_turned cmp_hid_copied "
                "cmp_made cmp_copied cmp_scored cmp_centred cmp_exp cmp_probs_ready cmp_turned cmp_turned_copied "
                "gate_sum_done gate_sum_copied gate_turned gates_ready rope_in post_root_ready post_rows_ready "
                "up_squared ret_turned ret_turned_copied t5_table_in").split()
        (squares_summed, score_read, post_in, cmp_hid_done, cmp_hid_ready, cmp_hid_turned, cmp_hid_copied,
         cmp_made, cmp_copied, cmp_scored, cmp_centred, cmp_exp, cmp_probs_ready, cmp_turned, cmp_turned_copied,
         gate_sum_done, gate_sum_copied, gate_turned, gates_ready, rope_in, post_root_ready, post_rows_ready,
         up_squared, ret_turned, ret_turned_copied, t5_table_in) = (sem(x) for x in more)
        block = ctx.enter_context(nc.Block())

        def evacuated(eng, n):
            eng.wait_ge(panel_evacuated[n % 2], n // 2 + 1)

        def computed(eng, n, quarter=3):
            eng.wait_ge(halves_used, 8 * n + 2 * (quarter + 1))

        def wide(w):
            return ps[:, 2 * w:2 * w + 2, :].rearrange("p b (j s) -> p (b j) s", s=N)

        def gram(w):
            return ps[:, 4 * w:4 * w + 4, :].rearrange("p b (j x s) -> p (b j) x s", x=2, s=N)

        bufs = [flat[i].rearrange("p (k j s) -> p k j s", k=4, s=N) for i in (XT, MIX)]
        X, XTR, AT, Z = (bufs[0][:, k] for k in range(4))
        ARB, AAK, ARK, VTOK = (bufs[1][:, k] for k in range(4))
        ST, KTOK = work[:, 0], work[:, 1]
        BTOK, RHS, U = AT, Z, XTR
        centred, bonus, squares = (lambda c, r=r: hall[:, r, :, c * N:(c + 1) * N] for r in (KN, KK, AA))
        TURNS = ((0, AA), (2, VV), (1, KK))
        HEADS = [x for j in range(DT) for x in ((j, 0), ((j + DT // 2) % DT, 1))]
        rows = (slice(0, N), slice(N, P))
        LAST = NCH - 1

        def group_heads(g):
            return [(j, h) for j in range(8 * g, 8 * g + 8) for h in range(2)]

        def part(ap, g):
            return ap[:, 8 * g:8 * g + 8]

        lora_w1 = flat[VV][:, 0:2 * DT * LORA].rearrange("p (m a r) -> p m a r", m=2, r=LORA)
        lora_w2 = flat[KN][0:LORA, :].rearrange("p (m c) -> p m c", m=2)
        restart = work[:, 0].rearrange("p j s -> p (j s)")[:, 0:T]
        lora_hid = work[0:LORA, 1].rearrange("p j s -> p (j s)")[:, 0:2 * T].rearrange("p (m t) -> p m t", m=2)
        key_sq = [work[:, i].rearrange("p j s -> p (j s)").rearrange("p (a t) -> p a t", a=4) for i in range(2)]
        key_tmp, key_exp = key_work[:, 0], key_work[:, 1]
        EPS_GN, EPS_LN, EPS_SUB, EPS_6 = (small[:, i:i + 1] for i in range(4))

        def token_rows(region, width=D):
            return flat[region][:, 0:TT * width].rearrange("p (a c) -> p a c", a=TT)

        X_TOK, ROWS, X_T, DK, DQ, DV, DG, O_TOK = range(8)
        prob = [flat[ROWS][:, 512 * i:512 * i + 512] for i in range(2)]
        prob_t = [flat[ROWS][:, 1024 + 512 * i:1536 + 512 * i] for i in range(2)]
        dist = flat[ROWS][:, 2048:2304]
        lam_rows = flat[ROWS][:, 2304:2816].rearrange("p (a b) -> p a b", a=4)
        lam_tmp = flat[ROWS][:, 2816:3072].rearrange("p (a b) -> p a b", a=2)
        junk = flat[ROWS][:, 3072:3328]
        stats = small[:, 8:56].rearrange("p (t k s) -> p t k s", t=TT, k=4)
        mean_var = small[:, 56:60].rearrange("p (t k) -> p t k", t=TT)
        root = small[:, 60:62]
        top = [small[:, 64 + 4 * i:66 + 4 * i] for i in range(2)]
        total = [small[:, 72 + 4 * i:74 + 4 * i] for i in range(2)]
        share = [small[:, 80 + 4 * i:82 + 4 * i] for i in range(2)]
        lam_sum, lam, neg_lam = small[:, 88:90], small[:, 90:91], small[:, 91:92]
        o_squares = small[:, 96:112]
        row_squares = small[:, 112:120].rearrange("p (t k) -> p t k", t=TT)
        row_root = small[:, 120:122]

        H_TOK, H_T, QA_CM_K4, QR_KR, VR_GR, CAT_T, BIAS_VV = 1, 2, 3, 4, 5, 6, 7
        qa, cm, k4 = hall[:, QA_CM_K4, 0:8], hall[:, QA_CM_K4, 8:12], hall[:, QA_CM_K4, 12:16]
        qr, kr = hall[:, QR_KR, 0:8], hall[:, QR_KR, 8:16]
        vr = flat[VR_GR][:, 0:2048].rearrange("p (t c) -> p t c", t=TT)
        gr = flat[VR_GR][:, 2048:4096].rearrange("p (t c) -> p t c", t=TT)
        bias = flat[BIAS_VV][:, 0:2048].rearrange("p (h k) -> p h k", h=8)
        vv = flat[BIAS_VV][:, 2048:3072].rearrange("p (t c) -> p t c", t=TT)
        misc = flat[BIAS_VV][:, 3072:4096]
        block_pe = misc[:, 0:64]
        cmp_w2 = misc[:, 64:320].rearrange("p (a b) -> p a b", a=2)
        cmp_b1 = misc[0:2 * NCMP, 320:576].rearrange("p (a b) -> p a b", a=2)
        cmp_hid = misc[0:2 * NCMP, 576:832].rearrange("p (a b) -> p a b", a=2)
        cmp_hid_t = misc[:, 832:892].rearrange("p (a b) -> p a b", a=2)
        gates = misc[:, 892:940].rearrange("p (t b) -> p t b", t=TT)
        gate_sum = flat[CAT_T][0:24, 0:T]
        work_flat = work[:].rearrange("p a j s -> p (a j s)")
        windows = [work_flat[:, 960 * i:960 * i + 960].rearrange("p (l g n) -> p l g n", l=32, g=2) for i in range(2)]
        cmp_prob_t = work_flat[0:NCMP, :].rearrange("p (i q) -> p i q", q=P)
        cmp_w1 = [flat[r].rearrange("p (l c) -> p l c", l=32) for r in (H_TOK, VR_GR)]
        gate_w = con[:, 256:640].rearrange("p (a b) -> p a b", a=DT)
        cmp_k = con[:, 640:670]
        cmp_v = con[0:NCMP, 670:926].rearrange("p (g c) -> p g c", g=2)
        cmp_bias = small[:, 224:464]
        cmp_top, cmp_total = small[:, 128:144], small[:, 144:160]
        a_prob = [flat[H_TOK][:, 512 * i:512 * i + 512] for i in range(2)]
        a_prob_t = [flat[H_TOK][:, 1024 + 512 * i:1536 + 512 * i] for i in range(2)]
        cmp_p = flat[H_TOK][:, 2048:2288]
        cmp_valid = flat[H_TOK][:, 2304:2544]
        rope = flat[H_TOK][:, 2560:3072].rearrange("p (a t) -> p a t", a=2)
        decay_table = [flat[r][:, at + 384 * i:at + 384 * i + 384] for r, at in ((H_TOK, 3072), (QA_CM_K4, 2048)) for i in range(2)]
        rope_tmp = [hall[:, CAT_T, 8:12], hall[:, CAT_T, 12:16]]
        ret_p = [flat[H_TOK][:, 512 * i:512 * i + 384] for i in range(2)]
        ret_o = [flat[H_TOK][:, 1024 + 512 * i:1536 + 512 * i].rearrange("p (t c) -> p t c", t=TT) for i in range(4)]
        ret_stats = [small[:, 160 + 12 * i:172 + 12 * i].rearrange("p (t s) -> p t s", t=TT) for i in range(2)]
        ret_mv = [small[:, 184 + 4 * i:188 + 4 * i].rearrange("p (t s) -> p t s", t=TT) for i in range(2)]
        ret_root = [small[:, 192 + 2 * i:194 + 2 * i] for i in range(2)]
        up = hall[:, 4:8].rearrange("p r a t -> p (r a) t")
        MIX_TOK, POST = 4, 3
        t5_table, t5_one = flat[KK][0:33, 0:1024].rearrange("p (h q) -> p h q", h=8), flat[KK][0:33, 1024:1920]
        t5_rows = flat[RR][:, 0:3072].rearrange("p (h m) -> p h m", h=8)
        SCORES = 16
        operand = {name: hall[:, region] for name, region in
                   (("k", MIX), ("r", MIX), ("v", MIX), ("g", MIX), ("out0", RR), ("dk", X_T), ("dq", X_T), ("dv", X_T),
                    ("dg", X_T), ("out1", DK), ("cmp", H_T), ("kk", H_T), ("kr", H_T), ("qr", H_T), ("qa", H_T),
                    ("vv", H_T), ("vr", H_T), ("gr", H_T), ("out2", CAT_T), ("up", H_T))}
        operand["down"] = up

        def product_of(h):
            name = [n for n in HALF if HALF[n] <= h][-1]
            return name, 2 * (h - HALF[name]) % (64 if name == "down" else DT)

        def ahead(n):
            return min(8 * n + 10, min(e for e in GROUP_ENDS if e > 8 * n))

        def ring_half(h):
            return ring[:, h // 2 % RING, 2 * (h % 2):2 * (h % 2) + 2]

        @block.sync
        def _(sp):
            stream = d["stream"]
            turns = d["slots"] // RING
            sp.wait_ge(lora_in, 48)
            for j in range(RING):
                sp.dma_start(ring[:, j].rearrange("p a b -> p (a b)"), stream[j]).then_inc(slot_landed[j], 16)
            with sp.Fori(1, turns) as i:
                for j in range(RING):
                    sp.wait_ge(weights_split, i * TURN + 2 * (j + 1 - RING))
                    sp.dma_start(ring[:, j].rearrange("p a b -> p (a b)"),
                                 stream[bass.ds(i * RING + j, 1)].rearrange("o p c -> (o p) c")).then_inc(slot_landed[j], 16)
            for s in range(turns * RING, d["slots"]):
                sp.wait_ge(weights_split, 2 * (s + 1 - RING))
                sp.dma_start(ring[:, s % RING].rearrange("p a b -> p (a b)"), stream[s])\
                  .then_inc(slot_landed[s % RING], 16)

        @block.gpsimd
        def _(pool):
            def split(name, panels=4, first=0, halves=8):
                h0 = HALF[name] + halves * first
                with pool.Fori(0, panels) as i:
                    for h in range(h0, h0 + halves):
                        tile = product_of(h)[1]
                        pool.wait_ge(activation_hi, i * halves + (h + 1))
                        if h >= 2:
                            pool.wait_ge(halves_used, i * halves + (h - 1))
                        pool.tensor_tensor(a_lo[:, h % 2], operand[name][:, tile:tile + 2], a_hi[:, h % 2].bitcast(F32), ALU.subtract)\
                            .then_inc(activation_split, 1)

            for dst, src in ((flat[KK][0:33, 0:1024], d["t5_table"]), (t5_one, d["t5_one"])):
                pool.dma_start(dst, src).then_inc(t5_table_in, 16)
            for dst, src in ((flat[XT], d["x_channels"]), (con[:], d["resident"]),
                             (par[:].rearrange("p a b -> p (a b)"), d["params"])):
                pool.dma_start(dst, src).then_inc(x_in, 16)
            for dst, src in ((flat[VV][:, 0:2 * DT * LORA], d["lora1"]), (flat[KN][0:LORA, :], d["lora2"]),
                             (restart, d["restart"])):
                pool.dma_start(dst, src).then_inc(lora_in, 16)
            pool.wait_ge(t5_copied, 8)
            pool.dma_start(d["t5_scratch"].rearrange("h p m -> p h m"), t5_rows).then_inc(t5_stored, 16)
            for h in range(8):
                pool.wait_ge(activation_hi, h + 1)
                if h >= 2:
                    pool.wait_ge(halves_used, h - 1)
                pool.tensor_tensor(a_lo[:, h % 2], hall[:, MIX, 2 * h:2 * h + 2], a_hi[:, h % 2].bitcast(F32), ALU.subtract)\
                    .then_inc(activation_split, 1)
            split("k", 3, first=1)
            for name in ("r", "v", "g"):
                split(name)
            pool.wait_ge(y_done, NCH + 1)
            pool.dma_start(flat[X_TOK], d["x_tokens"]).then_inc(rows_in, 16)
            for i in range(2):
                pool.dma_start(token_rows(ROWS)[:, i], d["rows"][i].partition_broadcast(P)).then_inc(rows_in, 16)
            split("out0")
            pool.wait_ge(tok_ready, 4)
            pool.dma_start(dist, d["dist"]).then_inc(diff_in, 16)
            pool.dma_start(flat[ROWS][:, 2304:2816], d["lambda"].partition_broadcast(P)).then_inc(diff_in, 16)
            for name in ("dk", "dq", "dv", "dg"):
                split(name)
            pool.wait_ge(o_copied, SCORES)
            for i in range(2):
                pool.dma_start(token_rows(ROWS)[:, i], d["rows"][2 + i].partition_broadcast(P)).then_inc(rows_in, 16)
            split("out1", 1)
            pool.wait_ge(tr_done, 16)
            pool.wait_ge(t5_stored, 16)
            scratch = d["t5_scratch"]
            pool.dma_start(bias, bass.AP(scratch.tensor, 127, [[383, P], [P * 384, 8], [1, T]])).then_inc(nsa_in, 16)
            for dst, src in ((misc[:, 0:320], d["cmp_small"]), (misc[0:2 * NCMP, 320:576], d["cmp_b1"].partition_broadcast(2 * NCMP)),
                             (con[:, 256:640], d["gate_w"]), (flat[VR_GR], d["cmp_w1"][1])):
                pool.dma_start(dst, src).then_inc(nsa_in, 16)
            split("out1", 3, first=1)
            pool.wait_ge(tr_done, 24)
            pool.dma_start(flat[H_TOK], d["cmp_w1"][0]).then_inc(nsa_in, 16)
            split("cmp", 1)
            split("kk", 1)
            split("kr", 1)
            pool.wait_ge(cmp_hid_done, 2)
            pool.dma_start(flat[H_TOK][:, 2560:3072], d["rope"]).then_inc(rope_in, 16)
            pool.dma_start(cmp_valid, d["valid"]).then_inc(rope_in, 16)
            for h in range(4):
                pool.dma_start(decay_table[h], d["decay"][:, 384 * h:384 * h + 384]).then_inc(ret_in, 16)
            split("kr", 1, first=1)
            split("qr", 2)
            split("qa", 2)
            split("vv", 1)
            split("vr", 2)
            split("gr", 2)
            pool.wait_ge(ret_turned, 4)
            pool.wait_ge(ret_score_ready, 4)
            for i in range(2):
                pool.dma_start(token_rows(POST)[:, i], d["rows"][4 + i].partition_broadcast(P)).then_inc(post_in, 16)
            split("out2")
            split("up", 16)
            split("down", 4, halves=32)
            for t in range(TT):
                pool.wait_ge(out_rows_ready, t + 1)
                pool.dma_start(d["out"][t * P:(t + 1) * P, :], token_rows(H_TOK)[:, t]).then_inc(out_stored, 16)
            pool.wait_ge(out_stored, 32)

        @block.tensor
        def _(pe):
            def half_products(kind, h, turns, bank, tile, last, q, pass_hook=None):
                b = h % 2
                pe.wait_ge(activation_hi, turns + (h + 1))
                for k, (w, x) in enumerate(((w_hi, a_hi), (w_lo, a_hi), (w_hi, a_lo))):
                    if pass_hook:
                        pass_hook(q, b, k)
                    if k == 1:
                        pe.wait_ge(weights_split, turns + (h + 1))
                    if k == 2:
                        pe.wait_ge(activation_split, turns + (h + 1))
                    for a in range(2):
                        first, final = tile + a == 0 and k == 0, tile + a == last and k == 2
                        if kind == "W":
                            for c in range(4):
                                mm = pe.matmul(ps[:, bank + c // 2, (c % 2) * T:(c % 2 + 1) * T],
                                               w[:, b, a, c * P:(c + 1) * P], x[:, b, a, :],
                                               start=(first and c % 2 == 0), stop=final, skip_group_check=True)
                        else:
                            for c in range(TT):
                                mm = pe.matmul(ps[:, bank + c, :], x[:, b, a, c * P:(c + 1) * P], w[:, b, a, :],
                                               start=first, stop=final)
                return mm

            def panel(n, kind, hook=None, i=0, slots=4, slot=None, pass_hook=None):
                if n >= 2:
                    pe.wait_ge(panel_evacuated[n % 2], (n - 2) // 2 + 1 + i)
                for q in range(slots):
                    for b in range(2):
                        h = 2 * ((4 * n if slot is None else slot) + q) + b
                        half_products(kind, h, i * (4 * slots), 2 * (n % 2), 4 * q + 2 * b, 4 * slots - 1, q, pass_hook)\
                            .then_inc(halves_used, 1)
                    if hook:
                        hook(q)

            def product(name, panels, kind):
                with pe.Fori(0, panels // 2) as i:
                    for p in range(2):
                        panel(PANELS[name] + p, kind, i=i)

            def turn_rows(v, src, ready=None):
                for u in range(8):
                    if ready:
                        ready(u)
                    if u >= 4:
                        pe.wait_ge((tr_copied_v, tr_copied_a)[u % 2], 4 * v + (u - 4) // 2 + 1)
                    for a in range(2):
                        for t in range(TT):
                            c = (2 * u + a) * P
                            mm = pe.transpose(ps[:, 4 + u % 4, a * T + t * P:a * T + (t + 1) * P], src[:, t, c:c + P], ident)
                    mm.then_inc(tr_done, 1)

            pe.wait_ge(t5_table_in, 32)
            for h in range(8):
                if h >= 2:
                    pe.wait_ge(t5_copied, h - 1)
                pe.matmul(ps[:, 4 + h % 2, 0:384], t5_table[:, h, :], t5_one[:, 0:384], start=True, stop=True)\
                  .then_inc(t5_done, 1)
            for t in range(TT):
                for n in range(NCMP):
                    at = 384 + 224 + P * t - 16 * n
                    mm = pe.matmul(ps[:, 6, 15 * t + n:240:30], t5_one[:, at:at + P], t5_table[:, :, 0], start=True, stop=True)
            mm.then_inc(t5_done, 1)
            pe.wait_ge(t5_copied, 9)

            pe.wait_ge(lora_in, 48)
            for m in range(2):
                for t in range(DT):
                    if t % 4 == 0:
                        pe.wait_ge(mix_ready, 4 * m + t // 4 + 1)
                    mm = pe.matmul(ps[0:LORA, 4 + m, 0:T], lora_w1[:, m, t, :], hall[:, MIX, t, :],
                                   start=(t == 0), stop=(t == DT - 1))
                    if t % 4 == 3:
                        mm.then_inc(lora_read, 1)
            pe.wait_ge(lora_hid_copied, 2)
            for u in range(8):
                if u >= 2:
                    pe.wait_ge(lora_up_copied, u - 1)
                for c in range(4):
                    j = 4 * (u % 4) + c
                    mm = pe.matmul(ps[:, 4 + 2 * (u % 2) + c // 2, (c % 2) * T:(c % 2 + 1) * T],
                                   lora_w2[:, u // 4, j * P:(j + 1) * P], lora_hid[:, u // 4, :], start=True, stop=True)
                mm.then_inc(lora_up_done, 1)

            def key_norms(g):
                pe.wait_ge(key_squared, g + 1)
                if g >= 2:
                    pe.wait_ge(key_norm_ready, g - 1)
                for b in range(2):
                    mm = pe.matmul(ps[:, 4 + 2 * (g % 2) + b, :], ones64, key_sq[g % 2][:, 2 * b:2 * b + 2, :],
                                   start=True, stop=True)
                mm.then_inc(key_norm_summed, 1)

            KEY_NORMS_AFTER = {("r", 0): {1: 0, 3: 1}, ("r", 2): {1: 2}, ("v", 0): {1: 3}}
            for name in ("k", "r", "v", "g"):
                for p in range(4):
                    hook = None
                    if (name, p) in KEY_NORMS_AFTER:
                        hook = lambda q, after=KEY_NORMS_AFTER[name, p]: key_norms(after[q]) if q in after else None
                    panel(PANELS[name] + p, "W", hook=hook)

            def head_sums(src, w=0, groups=(0, 1)):
                for g in groups:
                    mm = pe.matmul(ps[:, 2 * w + g, :], ones64, part(src, g), start=True, stop=True)
                mm.then_inc(head_sum_done, 1)

            def epilogue_sums(c, i):
                if i == 0:
                    pe.wait_ge(bonus_ready, c + 1)
                    head_sums(bonus(c))
                if i == 1:
                    pe.wait_ge(bonus_added, c + 1)
                    pe.wait_ge(y_copied, c + 1)
                    head_sums(centred(c))
                if i == 2:
                    pe.wait_ge(y_squared, c + 1)
                    head_sums(squares(c))

            for c in range(NCH):
                cs = slice(c * N, (c + 1) * N)
                if c == 0:
                    pe.wait_ge(key_group_done, 4)
                    pe.wait_ge(receptance_done, 4)
                    evacuated(pe, PANELS["g"] + 2)
                    evacuated(pe, PANELS["g"] + 3)
                for w, lhs in ((0, AA), (1, KK)):
                    if c and w == 0:
                        pe.wait_ge(u_ready, 2 * c)
                        pe.wait_ge(y_copied, c)
                    if c and w == 1:
                        pe.wait_ge(state_ready, c)
                    for j, h in HEADS:
                        mm = pe.matmul(gram(w)[rows[h], j], hall[rows[h], lhs, j, cs], hall[rows[h], KN:KN + 2, j, cs],
                                       start=True, stop=True)
                    mm.then_inc(gram_done, 1)
                pe.wait_ge(gram_masked, 5 * c + 1)
                for g in range(2):
                    for j, h in group_heads(g):
                        mm = pe.matmul(wide(0)[rows[h], j], Z[rows[h], j], id64[rows[h], :], start=True, stop=True)
                    mm.then_inc(gram_done, 1)
                for i in range(5):
                    upper, right = (slice(0, N), slice(0, N)) if i < 4 else (slice(0, N // 2), slice(N // 2, N))
                    upper_rows = rows if i < 4 else (slice(0, N // 2), slice(N, N + N // 2))
                    for g in range(2):
                        if i == 0:
                            pe.wait_ge(gram_masked, 5 * c + 3 + g)
                        else:
                            pe.wait_ge(merged, 10 * c + 2 * i - 1 + g)
                        for j, h in group_heads(g):
                            mm = pe.matmul(wide(1)[upper_rows[h], j, right], AT[rows[h], j, upper], X[rows[h], j, right],
                                           start=True, stop=True)
                        mm.then_inc(z_done, 1)
                    if i == 0:
                        pe.wait_ge(gram_masked, 5 * c + 5)
                    else:
                        for g in range(2):
                            for j, h in group_heads(g):
                                mm = pe.matmul(wide(3)[upper_rows[h], j, upper], X[upper_rows[h], j, upper], id64[upper_rows[h], upper],
                                               start=True, stop=True)
                            mm.then_inc(x_turned, 1)
                    for g in range(2):
                        pe.wait_ge(z_masked, 10 * c + 2 * i + g + 1)
                        if i:
                            pe.wait_ge(xt_copied, 8 * c + 2 * i - 1 + g)
                        for j, h in group_heads(g):
                            mm = pe.matmul(wide(2)[upper_rows[h], j, right], XTR[upper_rows[h], j, upper], Z[upper_rows[h], j, right],
                                           start=True, stop=True)
                        mm.then_inc(merge_done, 1)
                    if c:
                        epilogue_sums(c - 1, i)
                if c:
                    pe.wait_ge(head_root_ready, c)
                for w, src in TURNS if c < LAST else TURNS[1:2]:
                    if w == 2:
                        pe.wait_ge(merged, 10 * c + 10)
                    for j, h in HEADS:
                        mm = pe.matmul(wide(w)[rows[h], j], hall[rows[h], src, j, cs], id64[rows[h], :], start=True, stop=True)
                    mm.then_inc(turned, 1)
                pe.wait_ge(turned_copied, 3 * c + (2 if c < LAST else 1))
                if c:
                    pe.wait_ge(state_ready, c)
                for g in range(2):
                    for j, h in group_heads(g):
                        if c:
                            pe.matmul(wide(3)[rows[h], j], hall[rows[h], KN, j, cs], ST[rows[h], j], start=True, stop=False)
                        mm = pe.matmul(wide(3)[rows[h], j], AAK[rows[h], j], VTOK[rows[h], j], start=(c == 0), stop=True)
                    mm.then_inc(rhs_done, 1)
                for g in range(2):
                    pe.wait_ge(rhs_ready, 2 * c + g + 1)
                    for j, h in group_heads(g):
                        mm = pe.matmul(wide(0)[rows[h], j], X[rows[h], j], RHS[rows[h], j], start=True, stop=True)
                    mm.then_inc(u_done, 1)
                if c < LAST:
                    pe.wait_ge(turned_copied, 3 * c + 3)
                else:
                    pe.wait_ge(bonus_ready, NCH)
                    head_sums(bonus(LAST), w=2)
                for g in range(2):
                    pe.wait_ge(u_ready, 2 * c + g + 1)
                    for j, h in group_heads(g):
                        if c:
                            pe.matmul(wide(1)[rows[h], j], ST[rows[h], j], hall[rows[h], RR, j, cs], start=True, stop=False)
                        pe.matmul(wide(1)[rows[h], j], VTOK[rows[h], j], ARK[rows[h], j], start=(c == 0), stop=False)
                        mm = pe.matmul(wide(1)[rows[h], j], U[rows[h], j], ARB[rows[h], j], start=False, stop=True)
                    if g or c == LAST:
                        mm.then_inc(y_done, 1)
                if c < LAST:
                    for j, h in HEADS:
                        pe.matmul(wide(2)[rows[h], j], BTOK[rows[h], j], U[rows[h], j], start=True, stop=False)
                        mm = pe.matmul(wide(2)[rows[h], j], KTOK[rows[h], j], VTOK[rows[h], j], start=False, stop=True)
                    mm.then_inc(state_done, 1)
            for g in range(2):
                pe.wait_ge(y_copied, NCH + g)
                head_sums(centred(LAST), w=3, groups=(g,))
            for g in range(2):
                pe.wait_ge(y_squared, NCH + g)
                head_sums(squares(LAST), w=0, groups=(g,))
            pe.wait_ge(head_root_ready, NCH + 1)
            product("out0", 4, "X")
            turn_rows(0, token_rows(X_TOK), ready=lambda u: pe.wait_ge(tok_ready, u // 2 + 1))
            product("dk", 4, "W")
            product("dq", 4, "W")
            product("dv", 4, "X")

            def diff_scores(i):
                h, t = divmod(i, TT)
                if i >= 2:
                    pe.wait_ge(score_read, i - 1)
                for m in range(2):
                    mm = pe.matmul(ps[:, 4 + i % 2, m * T:m * T + P * (t + 1)], hall[:, DQ, 2 * h + m, t * P:(t + 1) * P],
                                   hall[:, DK, 2 * h + m, 0:P * (t + 1)], start=True, stop=True)
                mm.then_inc(score_done, 1)

            def diff_turn(i):
                pe.wait_ge(attn_ready, i + 1)
                if i:
                    pe.wait_ge(attn_copied, i)
                for k in range(i % TT + 1):
                    mm = pe.transpose(ps[:, 6, k * P:(k + 1) * P], prob[i % 2][:, k * P:(k + 1) * P], ident)
                mm.then_inc(attn_turned, 1)

            def diff_values(i):
                h, t = divmod(i, TT)
                pe.wait_ge(attn_copied, i + 1)
                if i:
                    pe.wait_ge(o_copied, i)
                for k in range(t + 1):
                    mm = pe.matmul(ps[:, 7, 0:T], prob_t[i % 2][:, k * P:(k + 1) * P], token_rows(DV)[:, k, h * T:(h + 1) * T],
                                   start=(k == 0), stop=(k == t))
                mm.then_inc(o_done, 1)

            def diff_inside(s, b, k):
                if b == 1 and k == 2:
                    diff_turn(s)

            def diff_after(s):
                if s + 1 < SCORES:
                    diff_scores(s + 1)
                diff_values(s)

            evacuated(pe, PANELS["dq"] + 3)
            pe.wait_ge(tr_copied_v, 4)
            diff_scores(0)
            for p in range(4):
                panel(PANELS["dg"] + p, "X", hook=lambda q, p=p: diff_after(4 * p + q),
                      pass_hook=lambda q, b, k, p=p: diff_inside(4 * p + q, b, k))
            turn_rows(1, token_rows(O_TOK), ready=lambda u: pe.wait_ge(o_scaled, u + 1))
            product("out1", 4, "X")

            pe.wait_ge(act_rows_ready, 2)
            turn_rows(2, token_rows(H_TOK))
            panel(PANELS["cmp"], "W")
            panel(PANELS["kk"], "W")

            def compress_hook(s):
                if s == 0:
                    pe.wait_ge(nsa_in, 96)
                    for a in range(DT):
                        mm = pe.matmul(ps[0:24, 6, 0:T], gate_w[:, a, :], hall[:, H_T, a, :], start=(a == 0), stop=(a == DT - 1))
                    mm.then_inc(gate_sum_done, 1)
                if s in (1, 2):
                    pe.wait_ge(blocks_ready, s)
                    for l in range(32):
                        mm = pe.matmul(ps[0:2 * NCMP, 3 + s, 0:P], windows[s - 1][:, l].rearrange("p g n -> p (g n)"),
                                       cmp_w1[s - 1][:, l, :], start=(l == 0), stop=(l == 31))
                    mm.then_inc(cmp_hid_done, 1)
                if s == 3:
                    pe.wait_ge(gate_sum_copied, 1)
                    for t in range(TT):
                        mm = pe.transpose(ps[:, 7, 24 * t:24 * t + 24], gate_sum[:, t * P:(t + 1) * P], ident[0:24, 0:24])
                    mm.then_inc(gate_turned, 1)
                if s == 4:
                    pe.wait_ge(cmp_hid_ready, 2)
                    for i in range(2):
                        mm = pe.transpose(ps[:, 6, 32 * i:32 * i + 30], cmp_hid[:, i, :], ident[0:30, 0:30])
                    mm.then_inc(cmp_hid_turned, 1)
                if s == 5:
                    pe.wait_ge(cmp_hid_copied, 1)
                    pe.matmul(ps[:, 4, 0:30], cmp_w2[:, 0, :], cmp_hid_t[:, 0, :], start=True, stop=True)
                    for g in range(2):
                        mm = pe.matmul(ps[0:NCMP, 5, g * P:(g + 1) * P], cmp_hid_t[:, 1, NCMP * g:NCMP * g + NCMP], cmp_w2[:, 1, :],
                                       start=True, stop=True)
                    mm.then_inc(cmp_made, 1)

            for p in range(2):
                panel(PANELS["kr"] + p, "W", hook=lambda q, p=p: compress_hook(4 * p + q))
            for name in ("qr", "qa"):
                for p in range(2):
                    panel(PANELS[name] + p, "W")

            def cmp_hook(s):
                if s == 1:
                    evacuated(pe, PANELS["qa"] + 1)
                    pe.wait_ge(cmp_copied, 2)
                    for i in range(SCORES):
                        h, t = divmod(i, TT)
                        mm = pe.matmul(ps[:, 4, NCMP * i:NCMP * i + NCMP], qa[:, h, t * P:(t + 1) * P],
                                       cmp_k[:, NCMP * (h // 4):NCMP * (h // 4) + NCMP], start=True, stop=True)
                    mm.then_inc(cmp_scored, 1)
                if s == 3:
                    pe.wait_ge(cmp_probs_ready, 1)
                    for i in range(SCORES):
                        mm = pe.transpose(ps[0:NCMP, 4 + i // 4, (i % 4) * P:(i % 4 + 1) * P],
                                          cmp_p[:, NCMP * i:NCMP * i + NCMP], ident)
                        if i % 4 == 3:
                            mm.then_inc(cmp_turned, 1)

            panel(PANELS["vv"], "X", hook=cmp_hook)

            def nsa_scores(i):
                h, t = divmod(i, TT)
                if i >= 2:
                    pe.wait_ge(score_read, SCORES + i - 1)
                for b in range(2):
                    mm = pe.matmul(ps[:, 4 + i % 2, b * T:b * T + P * (t + 1)], qa[:, h, t * P:(t + 1) * P],
                                   k4[:, 2 * b + h // 4, 0:P * (t + 1)], start=True, stop=True)
                mm.then_inc(score_done, 1)

            def nsa_turn(i):
                pe.wait_ge(attn_ready, SCORES + i + 1)
                pe.wait_ge(attn_copied, SCORES + i)
                for b in range(2):
                    for k in range(i % TT + 1):
                        mm = pe.transpose(ps[:, 6, b * T + k * P:b * T + (k + 1) * P],
                                          a_prob[i % 2][:, b * T + k * P:b * T + (k + 1) * P], ident)
                mm.then_inc(attn_turned, 1)

            def nsa_values(i):
                h, t = divmod(i, TT)
                g = h // 4
                pe.wait_ge(attn_copied, SCORES + i + 1)
                pe.wait_ge(o_copied, SCORES + i)
                pe.matmul(ps[:, 7, 0:P], cmp_v[:, g, :], cmp_prob_t[:, i, :], start=True, stop=False)
                for b in range(2):
                    for k in range(t + 1):
                        mm = pe.matmul(ps[:, 7, 0:P], vv[:, k, (2 * b + g) * P:(2 * b + g + 1) * P],
                                       a_prob_t[i % 2][:, b * T + k * P:b * T + (k + 1) * P], start=False,
                                       stop=(b == 1 and k == t))
                mm.then_inc(o_done, 1)

            def nsa_inside(s, b, k):
                if s and b == 1 and k == 2:
                    nsa_turn(s - 1)

            def nsa_after(s):
                if s == 0:
                    pe.wait_ge(cmp_turned_copied, 4)
                    evacuated(pe, PANELS["vv"])
                nsa_scores(s)
                if s:
                    nsa_values(s - 1)

            for m, name in enumerate(("vr", "gr")):
                for p in range(2):
                    panel(PANELS[name] + p, "X", hook=lambda q, p=p, m=m: nsa_after(8 * m + 4 * p + q),
                          pass_hook=lambda q, b, k, p=p, m=m: nsa_inside(8 * m + 4 * p + q, b, k))
            nsa_turn(15)
            nsa_values(15)

            def ret_scores(h):
                if h >= 2:
                    pe.wait_ge(ret_score_ready, h - 1)
                for k, lo, at in ((0, 0, 0), (1, P, T)):
                    for a in range(2):
                        mm = pe.matmul(ps[:, 4 + h % 2, at:at + T - lo], kr[:, 2 * h + a, k * P:(k + 1) * P],
                                       qr[:, 2 * h + a, lo:T], start=(a == 0), stop=(a == 1))
                mm.then_inc(ret_score_done, 1)

            def ret_values(h):
                pe.wait_ge(ret_score_ready, h + 1)
                if h >= 2:
                    pe.wait_ge(ret_o_ready, h - 1)
                for t, k, at in ((0, 0, 0), (1, 0, P), (1, 1, T)):
                    mm = pe.matmul(ps[:, 6 + h % 2, t * T:(t + 1) * T], ret_p[h % 2][:, at:at + P], vr[:, k, h * T:(h + 1) * T],
                                   start=(k == 0), stop=(k == t))
                mm.then_inc(ret_o_done, 1)

            pe.wait_ge(score_read, 2 * SCORES)
            pe.wait_ge(attn_copied, 2 * SCORES)
            pe.wait_ge(o_copied, 2 * SCORES)
            pe.wait_ge(rope_ready, 2)
            evacuated(pe, PANELS["gr"])
            evacuated(pe, PANELS["gr"] + 1)
            ret_scores(0)
            ret_scores(1)
            ret_values(0)
            ret_scores(2)
            ret_values(1)
            ret_scores(3)
            ret_values(2)
            ret_values(3)
            for h in range(4):
                pe.wait_ge(ret_o_ready, h + 1)
                for a in range(2):
                    for t in range(TT):
                        mm = pe.transpose(ps[:, h, a * T + t * P:a * T + (t + 1) * P], ret_o[h][:, t, a * P:(a + 1) * P], ident)
                mm.then_inc(ret_turned, 1)
            pe.wait_ge(ret_turned_copied, 4)
            product("out2", 4, "X")

            pe.wait_ge(act_rows_ready, 4)
            turn_rows(3, token_rows(H_TOK))
            product("up", 16, "W")
            with pe.Fori(0, 2) as i:
                for p in range(2):
                    panel(PANELS["down"] + p, "X", i=i, slots=16, slot=4 * PANELS["down"] + 16 * p)

        @block.vector
        def _(dve):
            steps = [0]

            def then(ins):
                steps[0] += 1
                ins.then_inc(dve_step, 1)
                dve.wait_ge(dve_step, steps[0])

            def split_half(h, turns=0):
                dve.wait_ge(weights_hi, turns + (h + 1))
                if h >= 2:
                    dve.wait_ge(halves_used, turns + (h - 1))
                dve.tensor_tensor(w_lo[:, h % 2], ring_half(h), w_hi[:, h % 2].bitcast(F32), ALU.subtract).then_inc(weights_split, 1)

            split = [0]

            def split_to(count):
                while split[0] < count:
                    split_half(split[0])
                    split[0] += 1

            for col, value in ((EPS_GN, GN_EPS), (EPS_LN, LN_EPS), (EPS_SUB, SUBLN_EPS), (EPS_6, EPS6)):
                ins = dve.memset(col, value)
            ins.then_inc(eps_ready, 1)

            def token_mix(m, quarters=range(4)):
                for q in quarters:
                    s = slice(4 * q, 4 * q + 4)
                    if 1 <= m <= 2:
                        dve.wait_ge(lora_read, 4 * (m - 1) + q + 1)
                    elif m > 2:
                        dve.wait_ge(activation_split, 8 * (4 * (m - 3) + 3) + 2 * q + 2)
                    x, y = hall[:, XT, s], hall[:, MIX, s]
                    dve.tensor_tensor(y[:, :, 1:], x[:, :, 0:T - 1], x[:, :, 1:], ALU.subtract)
                    then(dve.tensor_scalar(y[:, :, 0:1], x[:, :, 0:1], -1.0, None, ALU.mult))
                    for a in range(4):
                        mu = pv(MIXES[m])[:, 4 * q + a:4 * q + a + 1]
                        ins = dve.scalar_tensor_tensor(y[:, a], y[:, a], mu, x[:, a], ALU.mult, ALU.add)
                    ins.then_inc(mix_ready, 1)

            dve.wait_ge(x_in, 48)
            for m in range(3):
                token_mix(m)
            split_to(2)
            dve.wait_ge(lora_in, 48)
            for j in range(DT):
                if j % 4 == 0:
                    dve.wait_ge(lora_up_copied, j // 4 + 1)
                ins = dve.tensor_tensor_scan(hall[:, LD, j], restart, hall[:, LD, j], 0.0, ALU.mult, ALU.add)
                if j % 4 == 3:
                    ins.then_inc(decay_summed, 1)

            def key_raw(g):
                s = slice(4 * g, 4 * g + 4)
                evacuated(dve, PANELS["k"] + g)
                if g == 0:
                    dve.wait_ge(lora_up_copied, 8)
                dve.tensor_tensor(hall[:, KN, s], hall[:, KK, s], over(pv("k_k")[:, s], [P, 4, T]), ALU.mult)\
                   .then_inc(key_raw_ready, 1)

            def key_group(g, at):
                s = slice(4 * g, 4 * g + 4)
                sq, kn, a, k, ld = key_sq[g % 2], hall[:, KN, s], hall[:, AA, s], hall[:, KK, s], hall[:, LD, s]
                dve.wait_ge(key_norm_ready, g + 1)
                then(dve.tensor_scalar(sq, sq, 1e-12, None, ALU.max))
                for j in range(4):
                    split_to(at + (j + 1) // 2)
                    ins = dve.reciprocal(sq[:, j], sq[:, j])
                then(ins)
                split_to(at + 3)
                then(dve.tensor_tensor(kn, kn, sq, ALU.mult))
                split_to(at + 4)
                then(dve.scalar_tensor_tensor(key_tmp, a, -1.0, over(pv("k_a")[:, s], [P, 4, T]), ALU.add, ALU.mult))
                split_to(at + 5)
                then(dve.scalar_tensor_tensor(k, key_tmp, 1.0, k, ALU.add, ALU.mult))
                split_to(at + 6)
                then(dve.tensor_tensor(a, a, kn, ALU.mult))
                split_to(at + 7)
                dve.wait_ge(decay_exp_ready, g + 1)
                dve.tensor_tensor(a, a, key_exp, ALU.mult)
                split_to(at + 8)
                dve.tensor_tensor(k, k, key_exp, ALU.mult)
                split_to(at + 9)
                chunks = lambda ap: ap.rearrange("p a (c t) -> p (a c) t", t=N)
                dve.tensor_tensor(chunks(kn)[:, :, 1:], chunks(kn)[:, :, 1:], chunks(ld)[:, :, 0:N - 1], ALU.mult)
                split_to(at + 10)
                dve.tensor_copy(wl[:, s], ld.rearrange("p a (c t) -> p a c t", t=N)[:, :, :, N - 1])\
                   .then_inc(key_group_done, 1)

            def mix_behind(m):
                for q in range(4):
                    split_to(HALF[("k", "r", "v")[m - 3]] + 24 + 2 * q + 2)
                    token_mix(m, (q,))

            for g in range(3):
                split_to(ahead(PANELS["k"] + g))
                key_raw(g)
            mix_behind(3)
            split_to(ahead(PANELS["k"] + 3))
            key_raw(3)
            split_to(HALF["r"] + 7)
            key_group(0, HALF["r"] + 7)
            key_group(1, HALF["r"] + 17)
            mix_behind(4)
            split_to(HALF["v"] + 2)
            key_group(2, HALF["v"] + 2)
            split_to(HALF["v"] + 14)
            key_group(3, HALF["v"] + 14)
            for g in range(4):
                s = slice(4 * g, 4 * g + 4)
                evacuated(dve, PANELS["r"] + g)
                dve.tensor_tensor(hall[:, RR, s], hall[:, RR, s], hall[:, LD, s], ALU.mult).then_inc(receptance_done, 1)
                split_to(HALF["v"] + 24 + g // 2)
            mix_behind(5)
            split_to(HALF["out0"])

            def epilogue(c, i):
                cs = slice(c * N, (c + 1) * N)
                y, sq, add = centred(c), squares(c), bonus(c)
                if i == 0:
                    dve.wait_ge(head_sum_done, 3 * c + 1)
                    dve.tensor_tensor(add, wide(0), hall[:, VV, :, cs], ALU.mult).then_inc(bonus_added, 1)
                if i == 1:
                    dve.wait_ge(head_sum_done, 3 * c + 2)
                    dve.scalar_tensor_tensor(y, wide(0), -1.0 / N, y, ALU.mult, ALU.add).then_inc(y_centred, 1)
                if i in (3, 4):
                    half = slice(8 * (i - 3), 8 * (i - 2))
                    dve.wait_ge(head_root_ready, c + 1)
                    then(dve.reciprocal(sq[:, half], sq[:, half]))
                if i == 4:
                    dve.wait_ge(y_centred, c + 1)
                    dve.wait_ge(bonus_added, c + 1)
                    then(dve.tensor_tensor(y, y, sq, ALU.mult))
                    then(dve.tensor_tensor(y, y, over(pv("gn_g"), [P, DT, N]), ALU.mult))
                    then(dve.tensor_tensor(y, y, over(pv("gn_b"), [P, DT, N]), ALU.add))
                    then(dve.tensor_tensor(y, y, add, ALU.add))
                    dve.tensor_tensor(hall[:, RR, :, cs], y, hall[:, LD, :, cs], ALU.mult).then_inc(chunk_done, 1)

            computed(dve, PANELS["g"] + 3)
            for c in range(NCH):
                cs = slice(c * N, (c + 1) * N)
                dve.wait_ge(gram_done, 4 * c + 1)
                then(dve.tensor_tensor(Z, gram(0)[:, :, 0], mask(C_U), ALU.mult))
                then(dve.tensor_tensor(X, Z, mask(C_NM1), ALU.mult))
                dve.tensor_tensor(X, X, mask(C_ID64), ALU.add)
                dve.tensor_tensor(ARB, gram(0)[:, :, 1], mask(C_UI), ALU.mult).then_inc(gram_masked, 1)
                dve.wait_ge(gram_done, 4 * c + 2)
                dve.tensor_tensor(AAK, gram(1)[:, :, 0], mask(C_U), ALU.mult)
                dve.tensor_tensor(ARK, gram(1)[:, :, 1], mask(C_UI), ALU.mult).then_inc(gram_masked, 1)
                for g in range(2):
                    dve.wait_ge(gram_done, 4 * c + 3 + g)
                    dve.tensor_copy(part(AT, g), part(wide(0), g)).then_inc(gram_masked, 1)
                dve.wait_ge(gram_masked, 5 * c + 4)
                then(dve.tensor_tensor(XTR, AT, mask(C_NM1T), ALU.mult))
                dve.tensor_tensor(XTR, XTR, mask(C_ID64), ALU.add).then_inc(gram_masked, 1)
                dve.wait_ge(gram_masked, 5 * c + 5)
                for i in range(5):
                    right = slice(0, N) if i < 4 else slice(N // 2, N)
                    for g in range(2):
                        dve.wait_ge(z_done, 10 * c + 2 * i + g + 1)
                        dve.tensor_tensor(part(Z, g)[:, :, right], part(wide(1), g)[:, :, right],
                                          mask(C_MB + 64 * i, 8)[:, :, right], ALU.mult).then_inc(z_masked, 1)
                    for g in range(2):
                        dve.wait_ge(merge_done, 10 * c + 2 * i + g + 1)
                        x, update = part(X, g), part(wide(2), g)
                        for r in (slice(0, P),) if i < 4 else (slice(0, N // 2), slice(N, N + N // 2)):
                            ins = dve.tensor_tensor(x[r, :, right], x[r, :, right], update[r, :, right], ALU.subtract)
                        ins.then_inc(merged, 1)
                    if i < 4:
                        dve.wait_ge(merged, 10 * c + 2 * i + 2)
                    if c:
                        epilogue(c - 1, i)
                dve.wait_ge(turned, 3 * c + (3 if c < LAST else 1))
                then(dve.tensor_tensor(bonus(c), hall[:, RR, :, cs], hall[:, KK, :, cs], ALU.mult))
                dve.tensor_tensor(bonus(c), bonus(c), over(pv("r_k"), [P, DT, N]), ALU.mult).then_inc(bonus_ready, 1)
                if c == LAST:
                    break
                dve.wait_ge(state_done, c + 1)
                decay = over(wl[:, :, c], [P, DT, N])
                if c == 0:
                    dve.tensor_tensor(ST, wide(2), decay, ALU.mult).then_inc(state_ready, 1)
                else:
                    then(dve.tensor_tensor(ST, wide(2), ST, ALU.add))
                    dve.tensor_tensor(ST, ST, decay, ALU.mult).then_inc(state_ready, 1)
            cs = slice(LAST * N, T)
            y, sq, add = centred(LAST), squares(LAST), bonus(LAST)
            dve.wait_ge(head_sum_done, 3 * LAST + 1)
            then(dve.tensor_tensor(add, wide(2), hall[:, VV, :, cs], ALU.mult))
            then(dve.tensor_tensor(add, add, over(pv("gn_b"), [P, DT, N]), ALU.add))
            for g in range(2):
                dve.wait_ge(head_sum_done, 3 * LAST + 2 + g)
                dve.scalar_tensor_tensor(part(y, g), part(wide(3), g), -1.0 / N, part(y, g), ALU.mult, ALU.add).then_inc(y_centred, 1)
            for g in range(2):
                yg, sg, gain = part(y, g), part(sq, g), over(pv("gn_g")[:, 8 * g:8 * g + 8], [P, 8, N])
                dve.wait_ge(head_root_ready, NCH + g)
                then(dve.reciprocal(sg, sg))
                then(dve.tensor_tensor(yg, yg, sg, ALU.mult))
                then(dve.tensor_tensor(yg, yg, gain, ALU.mult))
                then(dve.tensor_tensor(yg, yg, part(add, g), ALU.add))
                dve.tensor_tensor(part(hall[:, RR, :, cs], g), yg, part(hall[:, LD, :, cs], g), ALU.mult).then_inc(chunk_done, 1)

            def out_rows(name, m):
                z = token_rows(X_TOK)
                for p in range(4):
                    n, c = PANELS[name] + p, slice(512 * p, 512 * p + 512)
                    split_to(ahead(n))
                    dve.wait_ge(rows_in, 48 if m == 0 else 80)
                    computed(dve, n)
                    for t in range(TT):
                        ins = dve.scalar_tensor_tensor(z[:, t, c], z[:, t, c], ALPHA, ps[:, 2 * (n % 2) + t, :], ALU.mult, ALU.add)
                    ins.then_inc(panel_evacuated[n % 2], 1)
                    evacuated(dve, n)
                    for t in range(TT):
                        ins = dve.bn_stats(stats[:, t, p, :], z[:, t, c])
                then(ins)
                for t in range(TT):
                    ins = dve.bn_aggr(mean_var[:, t, :], stats[:, t])
                ins.then_inc(ln_var_ready, 1)
                dve.wait_ge(ln_var_ready, m + 1)
                pieces = [((0, 1), slice(512 * q, 512 * q + 512)) for q in range(4)] if m == 0 else [((t,), slice(0, D)) for t in range(TT)]
                for k, (tiles, c) in enumerate(pieces):
                    for t in tiles:
                        ins = dve.scalar_tensor_tensor(z[:, t, c], z[:, t, c], mean_var[:, t, 0:1], token_rows(ROWS)[:, 0, c],
                                                       ALU.subtract, ALU.mult)
                    then(ins)
                    if k == 0:
                        dve.wait_ge(ln_root_ready, m + 1)
                        then(dve.reciprocal(root, root))
                    for t in tiles:
                        ins = dve.scalar_tensor_tensor(z[:, t, c], z[:, t, c], root[:, t:t + 1], token_rows(ROWS)[:, 1, c],
                                                       ALU.mult, ALU.add)
                    ins.then_inc(tok_ready, 1)

            def copy_turned(v, dst, scale=None):
                for u in range(0, 8, 2):
                    dve.wait_ge(tr_done, 8 * v + u + 1)
                    src = ps[:, 4 + u % 4, :].rearrange("p (a t) -> p a t", a=2)
                    if scale is None:
                        dve.tensor_copy(dst[:, 2 * u:2 * u + 2, :], src).then_inc(tr_copied_v, 1)
                    else:
                        dve.tensor_tensor(dst[:, 2 * u:2 * u + 2, :], src, over(pv(scale)[:, 2 * u:2 * u + 2], [P, 2, T]), ALU.mult)\
                           .then_inc(tr_copied_v, 1)

            out_rows("out0", 0)
            copy_turned(0, hall[:, X_T])

            split_to(HALF["dk"] + 8)
            dve.wait_ge(diff_in, 32)
            then(dve.tensor_tensor(lam_tmp, lam_rows[:, 0:4:2, :], lam_rows[:, 1:4:2, :], ALU.mult))
            dve.tensor_reduce(lam_sum, lam_tmp, AX.X, ALU.add).then_inc(lam_parts, 1)
            split_to(HALF["dk"] + 24)
            dve.wait_ge(lam_exp, 1)
            then(dve.tensor_tensor(lam, lam_sum[:, 1:2], lam_sum[:, 0:1], ALU.subtract))
            then(dve.tensor_scalar(neg_lam, lam, -LAM_INIT, None, ALU.add))

            def diff_logits(i):
                h, t = divmod(i, TT)
                w = P * (t + 1)
                pr = prob[i % 2].rearrange("p (m k) -> p m k", m=2)[:, :, 0:w]
                slope = 2.0 ** (-(8.0 / DH) * (h + 1))
                dve.wait_ge(score_done, i + 1)
                if i >= 2:
                    dve.wait_ge(attn_turned, i - 1)
                dd = dist[:, T - w:T].unsqueeze(1).broadcast_to([P, 2, w])
                dve.scalar_tensor_tensor(pr, dd, -slope / D_SCALE, ps[:, 4 + i % 2, :].rearrange("p (m k) -> p m k", m=2)[:, :, 0:w],
                                         ALU.mult, ALU.add).then_inc(score_read, 1)
                dve.wait_ge(score_read, i + 1)
                then(dve.tensor_reduce(top[i % 2], pr, AX.X, ALU.max))
                dve.tensor_scalar(top[i % 2], top[i % 2], -D_SCALE, None, ALU.mult).then_inc(score_max, 1)

            def diff_weights(i):
                t = i % TT
                w = P * (t + 1)
                pr, r = prob[i % 2], share[i % 2]
                dve.wait_ge(score_exp, i + 1)
                then(dve.reciprocal(r, total[i % 2]))
                then(dve.tensor_tensor(r[:, 1:2], r[:, 1:2], neg_lam, ALU.mult))
                then(dve.tensor_scalar(pr[:, T:T + w], pr[:, T:T + w], r[:, 1:2], None, ALU.mult))
                dve.scalar_tensor_tensor(pr[:, 0:w], pr[:, 0:w], r[:, 0:1], pr[:, T:T + w], ALU.mult, ALU.add)\
                   .then_inc(attn_ready, 1)

            split_to(HALF["dg"] + 1)
            for i in range(SCORES):
                diff_logits(i)
                split_to(HALF["dg"] + 2 * i + 2)
                diff_weights(i)
                split_to(min(HALF["dg"] + 2 * i + 3, HALF["out1"]))
            dve.wait_ge(squares_summed, 1)
            then(dve.reciprocal(o_squares, o_squares))
            then(dve.tensor_scalar(o_squares, o_squares, 1.0 - LAM_INIT, None, ALU.mult))
            evacuated(dve, PANELS["dg"] + 2)
            evacuated(dve, PANELS["dg"] + 3)
            for i in range(SCORES):
                h, t = divmod(i, TT)
                o, g = (token_rows(r)[:, t, h * T:(h + 1) * T] for r in (O_TOK, DG))
                ins = dve.scalar_tensor_tensor(o, o, o_squares[:, i:i + 1], g, ALU.mult, ALU.mult)
                if t:
                    ins.then_inc(o_scaled, 1)
            copy_turned(1, hall[:, DK], "subln")
            out_rows("out1", 1)

            def unit_rows(k, src, dst):
                dve.wait_ge(post_root_ready, k)
                then(dve.reciprocal(row_root, row_root))
                for t in range(TT):
                    dve.tensor_scalar(token_rows(dst)[:, t], token_rows(src)[:, t], row_root[:, t:t + 1], None, ALU.mult)\
                       .then_inc(act_rows_ready, 1)

            dve.wait_ge(tok_ready, 6)
            unit_rows(1, X_TOK, H_TOK)
            copy_turned(2, hall[:, H_T], "mix_pre")

            split_to(ahead(PANELS["kk"]))
            evacuated(dve, PANELS["cmp"])
            dve.wait_ge(nsa_in, 96)
            for i in range(2):
                for g in range(2):
                    tile = cm[:, 2 * i + g, :]
                    view = bass.AP(tile.tensor, tile.offset, [tile.ap[0], [1, 32], [16, NCMP]])
                    ins = dve.tensor_tensor(windows[i][:, :, g, :], view, over(block_pe[:, 32 * i:32 * i + 32], [P, 32, NCMP]), ALU.add)
                ins.then_inc(blocks_ready, 1)
            for i in range(2):
                split_to(HALF["kr"] + 6 + 2 * i)
                dve.wait_ge(cmp_hid_done, i + 1)
                dve.tensor_tensor(cmp_hid[:, i, :], ps[0:2 * NCMP, 4 + i, 0:P], cmp_b1[:, i, :], ALU.add).then_inc(cmp_step, 1)
            split_to(HALF["kr"] + 12)
            dve.wait_ge(cmp_hid_turned, 1)
            dve.tensor_copy(cmp_hid_t, ps[:, 6, 0:64].rearrange("p (a b) -> p a b", a=2)[:, :, 0:30]).then_inc(cmp_hid_copied, 1)
            split_to(HALF["kr"] + 14)
            dve.wait_ge(cmp_made, 1)
            dve.tensor_copy(cmp_k, ps[:, 4, 0:30]).then_inc(cmp_copied, 1)
            dve.tensor_copy(cmp_v, ps[0:NCMP, 5, 0:2 * P].rearrange("p (g c) -> p g c", g=2)).then_inc(cmp_copied, 1)

            dve.wait_ge(rope_in, 32)
            for x, name in ((kr, "kr"), (qr, "qr")):
                at = ahead(PANELS[name] + 1)
                split_to(at)
                evacuated(dve, PANELS[name])
                evacuated(dve, PANELS[name] + 1)
                x1, x2 = x[:, 0:8:2, :], x[:, 1:8:2, :]
                cos, sin = (rope[:, i, :].unsqueeze(1).broadcast_to([P, 4, T]) for i in range(2))
                dve.tensor_tensor(rope_tmp[0], x1, sin, ALU.mult)
                split_to(at + 1)
                then(dve.tensor_tensor(rope_tmp[1], x2, sin, ALU.mult))
                split_to(at + 2)
                dve.tensor_tensor(x1, x1, cos, ALU.mult)
                then(dve.tensor_tensor(x2, x2, cos, ALU.mult))
                split_to(at + 3)
                dve.tensor_tensor(x1, x1, rope_tmp[1], ALU.subtract)
                dve.tensor_tensor(x2, x2, rope_tmp[0], ALU.add).then_inc(rope_ready, 1)
                dve.wait_ge(rope_ready, 1 if name == "kr" else 2)

            split_to(HALF["vv"] + 6)
            dve.wait_ge(t5_copied, 9)
            dve.wait_ge(cmp_scored, 1)
            cmp_view = cmp_p.rearrange("p (i n) -> p i n", n=NCMP)
            then(dve.scalar_tensor_tensor(cmp_p, ps[:, 4, 0:SCORES * NCMP], A_SCALE, cmp_bias, ALU.mult, ALU.add))
            then(dve.tensor_reduce(cmp_top, cmp_view, AX.X, ALU.max))
            dve.tensor_tensor(cmp_view, cmp_view, over(cmp_top, [P, SCORES, NCMP]), ALU.subtract).then_inc(cmp_centred, 1)
            dve.wait_ge(cmp_exp, 1)
            then(dve.tensor_reduce(cmp_total, cmp_view, AX.X, ALU.add))
            then(dve.reciprocal(cmp_total, cmp_total))
            dve.wait_ge(gates_ready, 1)
            gate = gates.rearrange("p t (h b) -> p h t b", b=3)
            then(dve.tensor_tensor(cmp_total.rearrange("p (h t) -> p h t", t=TT), cmp_total.rearrange("p (h t) -> p h t", t=TT),
                                   gate[:, :, :, 0], ALU.mult))
            then(dve.tensor_tensor(cmp_p, cmp_p, cmp_valid, ALU.mult))
            dve.tensor_tensor(cmp_view, cmp_view, over(cmp_total, [P, SCORES, NCMP]), ALU.mult).then_inc(cmp_probs_ready, 1)

            def nsa_logits(i):
                h, t = divmod(i, TT)
                w = P * (t + 1)
                pr = a_prob[i % 2].rearrange("p (m k) -> p m k", m=2)[:, :, 0:w]
                dve.wait_ge(score_done, SCORES + i + 1)
                if i >= 2:
                    dve.wait_ge(attn_turned, SCORES + i - 1)
                bb = bias[:, h, T - w:T].unsqueeze(1).broadcast_to([P, 2, w])
                dve.scalar_tensor_tensor(pr, ps[:, 4 + i % 2, :].rearrange("p (m k) -> p m k", m=2)[:, :, 0:w], A_SCALE, bb,
                                         ALU.mult, ALU.add).then_inc(score_read, 1)
                dve.wait_ge(score_read, SCORES + i + 1)
                then(dve.tensor_reduce(top[i % 2], pr, AX.X, ALU.max))
                dve.tensor_scalar(top[i % 2], top[i % 2], -1.0, None, ALU.mult).then_inc(score_max, 1)

            def nsa_weights(i):
                h, t = divmod(i, TT)
                w = P * (t + 1)
                r = share[i % 2]
                dve.wait_ge(score_exp, SCORES + i + 1)
                then(dve.reciprocal(r, total[i % 2]))
                then(dve.tensor_tensor(r, r, gates[:, t, 3 * h + 1:3 * h + 3], ALU.mult))
                for b in range(2):
                    pr = a_prob[i % 2][:, b * T:b * T + w]
                    ins = dve.tensor_scalar(pr, pr, r[:, b:b + 1], None, ALU.mult)
                ins.then_inc(attn_ready, 1)

            split_to(HALF["vr"] + 3)
            for i in range(SCORES):
                nsa_logits(i)
                split_to(min(HALF["vr"] + 2 * i + 4, HALF["out2"]))
                nsa_weights(i)
                split_to(min(HALF["vr"] + 2 * i + 5, HALF["out2"]))

            dve.wait_ge(ret_in, 64)
            evacuated(dve, PANELS["gr"])
            evacuated(dve, PANELS["gr"] + 1)

            def ret_weights(h):
                dve.wait_ge(ret_score_done, h + 1)
                if h >= 2:
                    dve.wait_ge(ret_o_done, h - 1)
                dve.tensor_tensor(ret_p[h % 2], ps[:, 4 + h % 2, 0:384], decay_table[h], ALU.mult).then_inc(ret_score_ready, 1)

            def ret_norm(h):
                dve.wait_ge(ret_o_done, h + 1)
                o = ps[:, 6 + h % 2, :].rearrange("p (t c) -> p t c", t=TT)
                st, mv, rt = ret_stats[h % 2], ret_mv[h % 2], ret_root[h % 2]
                for t in range(TT):
                    ins = dve.bn_stats(st[:, t, :], o[:, t, :])
                then(ins)
                for t in range(TT):
                    ins = dve.bn_aggr(mv[:, t, :], st[:, t, :])
                ins.then_inc(ret_var_ready, 1)
                dve.wait_ge(ret_root_ready, h + 1)
                then(dve.reciprocal(rt, rt))
                for t in range(TT):
                    ins = dve.tensor_scalar(ret_o[h][:, t, :], o[:, t, :], mv[:, t, 0:1], rt[:, t:t + 1], ALU.subtract, ALU.mult)
                then(ins)
                dve.tensor_tensor(ret_o[h], ret_o[h], gr[:, :, h * T:(h + 1) * T], ALU.mult).then_inc(ret_o_ready, 1)

            ret_weights(0)
            ret_weights(1)
            ret_norm(0)
            ret_weights(2)
            ret_norm(1)
            ret_weights(3)
            ret_norm(2)
            ret_norm(3)

            def times_gain(name, src, row, p):
                evacuated(dve, PANELS[name] + p)
                dve.wait_ge(post_in, 32)
                for t in range(TT):
                    y = token_rows(src)[:, t, 512 * p:512 * p + 512]
                    ins = dve.tensor_tensor(y, y, token_rows(POST)[:, row, 512 * p:512 * p + 512], ALU.mult)
                ins.then_inc(gain_applied, 1)

            def add_rows(k, src, dst, done):
                dve.wait_ge(gain_applied, 4 * (k // 2))
                dve.wait_ge(post_root_ready, k)
                then(dve.reciprocal(row_root, row_root))
                for t in range(TT):
                    dve.scalar_tensor_tensor(token_rows(dst)[:, t], token_rows(src)[:, t], row_root[:, t:t + 1], token_rows(X_TOK)[:, t],
                                             ALU.mult, ALU.add).then_inc(done, 1)

            for p in range(4):
                split_to(ahead(PANELS["out2"] + p))
                times_gain("out2", MIX_TOK, 0, p)
            add_rows(2, MIX_TOK, X_TOK, post_rows_ready)
            dve.wait_ge(post_rows_ready, 2)
            unit_rows(3, X_TOK, H_TOK)
            copy_turned(3, hall[:, H_T], "mlp_pre")
            split_to(HALF["up"] + 2)
            with dve.Fori(0, 8) as i:
                for p in range(2):
                    n = PANELS["up"] + p
                    for h in range(8 * n + 2, 8 * n + 10):
                        split_half(h, i * 16)
                    dve.wait_ge(halves_used, i * 16 + 8 * (n + 1))
                    four = up[:, bass.ds(i * 8 + 4 * p, 4), :]
                    dve.tensor_scalar(four, ps[:, 2 * (n % 2):2 * (n % 2) + 2, :].rearrange("p b (a t) -> p (b a) t", a=2),
                                      0.0, None, ALU.max).then_inc(panel_evacuated[n % 2], 1)
                    dve.wait_ge(panel_evacuated[n % 2], i + (n // 2 + 1))
                    dve.tensor_tensor(four, four, four, ALU.mult).then_inc(up_squared, 1)
            for p in range(4):
                h0 = HALF["down"] + 32 * p + 2
                rest = 32 if p < 3 else 30
                with dve.Fori(0, rest // TURN) as i:
                    for h in range(h0, h0 + TURN):
                        split_half(h, i * TURN)
                for h in range(h0 + rest // TURN * TURN, h0 + rest):
                    split_half(h)
                times_gain("down", H_TOK, 1, p)
            add_rows(4, H_TOK, H_TOK, out_rows_ready)

        @block.scalar
        def _(act):
            steps = [0]

            def then(ins):
                steps[0] += 1
                ins.then_inc(act_step, 1)
                act.wait_ge(act_step, steps[0])

            def activation_ready(h):
                name, tile = product_of(h)
                q = tile // 4
                if name in ("k", "r", "v", "g"):
                    act.wait_ge(mix_ready, 4 * (("k", "r", "v", "g").index(name) + 2) + q + 1)
                elif name == "out0":
                    act.wait_ge(chunk_done, NCH + q // 2)
                elif name in ("dk", "out1", "cmp", "up"):
                    v = ("dk", "out1", "cmp", "up").index(name)
                    act.wait_ge(tr_copied_v, 4 * v + q + 1)
                    act.wait_ge(tr_copied_a, 4 * v + q + 1)
                elif name == "out2":
                    act.wait_ge(ret_turned_copied, 4)
                elif name == "down":
                    act.wait_ge(up_squared, q + 1)

            def split_half(h, turns=0):
                name, tile = product_of(h)
                if h % 2 == 0:
                    s = h // 2
                    act.wait_ge(slot_landed[s % RING], turns * (16 // TURN) + 16 * (s // RING + 1))
                if h >= 2:
                    act.wait_ge(halves_used, turns + (h - 1))
                act.activation(w_hi[:, h % 2], ring_half(h), ACT.Copy).then_inc(weights_hi, 1)
                if h - HALF[name] < (32 if name == "down" else 8):
                    activation_ready(h)
                act.activation(a_hi[:, h % 2], operand[name][:, tile:tile + 2], ACT.Copy).then_inc(activation_hi, 1)

            split = [0]

            def split_to(count):
                while split[0] < count:
                    split_half(split[0])
                    split[0] += 1

            def evacuate(n, dst, func=ACT.Copy):
                split_to(ahead(n))
                computed(act, n)
                for b in range(2):
                    ins = act.activation(dst[:, 2 * b:2 * b + 2, :], ps[:, 2 * (n % 2) + b, :].rearrange("p (a t) -> p a t", a=2), func)
                ins.then_inc(panel_evacuated[n % 2], 1)

            for h in range(8):
                act.wait_ge(t5_done, h + 1)
                act.activation(t5_rows[:, h, :], ps[:, 4 + h % 2, 0:384], ACT.Copy).then_inc(t5_copied, 1)
            act.wait_ge(t5_done, 9)
            act.activation(cmp_bias, ps[:, 6, 0:240], ACT.Copy).then_inc(t5_copied, 1)
            act.wait_ge(lora_read, 4)
            act.activation(lora_hid[:, 0], ps[0:LORA, 4, 0:T], ACT.Tanh).then_inc(lora_hid_copied, 1)
            act.wait_ge(lora_read, 8)
            act.activation(lora_hid[:, 1], ps[0:LORA, 5, 0:T], ACT.Copy).then_inc(lora_hid_copied, 1)
            split_to(2)
            for u in range(8):
                act.wait_ge(lora_up_done, u + 1)
                for c in range(4):
                    j = 4 * (u % 4) + c
                    ins = act.activation(hall[:, (LD, AA)[u // 4], j], ps[:, 4 + 2 * (u % 2) + c // 2, (c % 2) * T:(c % 2 + 1) * T],
                                         ACT.Sigmoid, bias=pv(("w0", "a0")[u // 4])[:, j:j + 1])
                ins.then_inc(lora_up_copied, 1)
            def square_keys(g):
                act.wait_ge(key_raw_ready, g + 1)
                if g >= 2:
                    act.wait_ge(key_group_done, g - 1)
                act.activation(key_sq[g % 2], hall[:, KN, 4 * g:4 * g + 4], ACT.Square).then_inc(key_squared, 1)

            def key_roots(g):
                act.wait_ge(key_norm_summed, g + 1)
                act.activation(key_sq[g % 2], ps[:, 4 + 2 * (g % 2):6 + 2 * (g % 2), :].rearrange("p b (a t) -> p (b a) t", a=2),
                               ACT.Sqrt).then_inc(key_norm_ready, 1)
                act.wait_ge(decay_summed, g + 1)
                if g >= 1:
                    act.wait_ge(key_group_done, g)
                ld = hall[:, LD, 4 * g:4 * g + 4]
                then(act.activation(key_exp, ld, ACT.Exp, scale=-DECAY))
                act.activation(ld, ld, ACT.Exp, scale=DECAY).then_inc(decay_exp_ready, 1)

            for p in range(4):
                evacuate(PANELS["k"] + p, hall[:, KK, 4 * p:4 * p + 4])
                if p in (1, 2):
                    square_keys(p - 1)
            split_to(HALF["r"] + 6)
            key_roots(0)
            act.wait_ge(t5_stored, 16)
            evacuate(PANELS["r"], hall[:, RR, 0:4])
            evacuate(PANELS["r"] + 1, hall[:, RR, 4:8])
            key_roots(1)
            split_to(HALF["r"] + 19)
            square_keys(2)
            evacuate(PANELS["r"] + 2, hall[:, RR, 8:12])
            split_to(HALF["r"] + 29)
            square_keys(3)
            key_roots(2)
            evacuate(PANELS["r"] + 3, hall[:, RR, 12:16])
            evacuate(PANELS["v"], hall[:, VV, 0:4])
            split_to(HALF["v"] + 13)
            key_roots(3)
            for p in range(1, 4):
                evacuate(PANELS["v"] + p, hall[:, VV, 4 * p:4 * p + 4])
            act.wait_ge(receptance_done, 4)
            for p in range(4):
                evacuate(PANELS["g"] + p, hall[:, LD, 4 * p:4 * p + 4], ACT.Silu)
            act.wait_ge(eps_ready, 1)
            def square(c):
                act.wait_ge(y_centred, c + 1)
                act.activation(squares(c), centred(c), ACT.Square).then_inc(y_squared, 1)

            def head_root(c):
                act.wait_ge(head_sum_done, 3 * c + 3)
                act.activation(squares(c), wide(0), ACT.Sqrt, scale=1.0 / N, bias=EPS_GN).then_inc(head_root_ready, 1)

            for c in range(NCH):
                for i in range(1, 5):
                    if c and i == 3:
                        square(c - 1)
                    if c and i == 4:
                        head_root(c - 1)
                    upper = slice(0, N) if i < 4 else slice(0, N // 2)
                    for g in range(2):
                        act.wait_ge(x_turned, 8 * c + 2 * i - 1 + g)
                        act.activation(part(XTR, g)[:, :, upper], part(wide(3), g)[:, :, upper], ACT.Copy).then_inc(xt_copied, 1)
                for k, (w, _) in enumerate(TURNS if c < LAST else TURNS[1:2]):
                    act.wait_ge(turned, 3 * c + k + 1)
                    act.activation((BTOK, KTOK, VTOK)[w], wide(w), ACT.Copy).then_inc(turned_copied, 1)
                for g in range(2):
                    act.wait_ge(rhs_done, 2 * c + g + 1)
                    act.activation(part(RHS, g), part(wide(3), g), ACT.Copy, scale=-1.0).then_inc(rhs_ready, 1)
                for g in range(2):
                    act.wait_ge(u_done, 2 * c + g + 1)
                    act.activation(part(U, g), part(wide(0), g), ACT.Copy).then_inc(u_ready, 1)
                if c < LAST:
                    act.wait_ge(y_done, c + 1)
                    act.activation(centred(c), wide(1), ACT.Copy).then_inc(y_copied, 1)
            for g in range(2):
                act.wait_ge(y_done, NCH + g)
                act.activation(part(centred(LAST), g), part(wide(1), g), ACT.Copy).then_inc(y_copied, 1)
            for g in range(2):
                act.wait_ge(y_centred, NCH + g)
                act.activation(part(squares(LAST), g), part(centred(LAST), g), ACT.Square).then_inc(y_squared, 1)
            for g in range(2):
                act.wait_ge(head_sum_done, 3 * LAST + 4 + g)
                act.activation(part(squares(LAST), g), part(wide(0), g), ACT.Sqrt, scale=1.0 / N, bias=EPS_GN).then_inc(head_root_ready, 1)

            def copy_turned(v, dst, scale=None):
                for u in range(1, 8, 2):
                    act.wait_ge(tr_done, 8 * v + u + 1)
                    src = ps[:, 4 + u % 4, :].rearrange("p (a t) -> p a t", a=2)
                    if scale is None:
                        ins = act.activation(dst[:, 2 * u:2 * u + 2, :], src, ACT.Copy)
                    else:
                        for a in range(2):
                            ins = act.activation(dst[:, 2 * u + a, :], src[:, a, :], ACT.Copy, scale=pv(scale)[:, 2 * u + a:2 * u + a + 1])
                    ins.then_inc(tr_copied_a, 1)

            def evacuate_rows(n, dst, func=ACT.Copy):
                split_to(ahead(n))
                computed(act, n)
                for t in range(TT):
                    ins = act.activation(dst[:, t, :], ps[:, 2 * (n % 2) + t, :], func)
                ins.then_inc(panel_evacuated[n % 2], 1)

            def norm_root(m):
                act.wait_ge(ln_var_ready, m + 1)
                act.activation(root, mean_var[:, :, 1], ACT.Sqrt, bias=EPS_LN).then_inc(ln_root_ready, 1)

            split_to(HALF["dk"])
            norm_root(0)
            copy_turned(0, hall[:, X_T])
            for p in range(4):
                evacuate(PANELS["dk"] + p, hall[:, DK, 4 * p:4 * p + 4])
                if p == 0:
                    act.wait_ge(lam_parts, 1)
                    act.activation(lam_sum, lam_sum, ACT.Exp).then_inc(lam_exp, 1)
            for p in range(4):
                evacuate(PANELS["dq"] + p, hall[:, DQ, 4 * p:4 * p + 4])
            for p in range(4):
                evacuate_rows(PANELS["dv"] + p, token_rows(DV)[:, :, 512 * p:512 * p + 512])

            def diff_exp(i):
                w = P * (i % TT + 1)
                act.wait_ge(score_max, i + 1)
                for m in range(2):
                    pr = prob[i % 2][:, m * T:m * T + w]
                    ins = act.activation(pr, pr, ACT.Exp, bias=top[i % 2][:, m:m + 1], scale=D_SCALE, accum_out=total[i % 2][:, m:m + 1])
                ins.then_inc(score_exp, 1)

            def diff_copy_attn(i):
                w = P * (i % TT + 1)
                act.wait_ge(attn_turned, i + 1)
                if i >= 2:
                    act.wait_ge(o_done, i - 1)
                act.activation(prob_t[i % 2][:, 0:w], ps[:, 6, 0:w], ACT.Copy).then_inc(attn_copied, 1)

            def diff_gate(p):
                evacuate_rows(PANELS["dg"] + p, token_rows(DG)[:, :, 512 * p:512 * p + 512], ACT.Silu)

            def diff_copy_o(i):
                h, t = divmod(i, TT)
                act.wait_ge(o_done, i + 1)
                act.activation(junk, ps[:, 7, 0:T], ACT.Square, accum_out=o_squares[:, i:i + 1])
                act.activation(token_rows(O_TOK)[:, t, h * T:(h + 1) * T], ps[:, 7, 0:T], ACT.Copy).then_inc(o_copied, 1)

            for s in range(SCORES):
                split_to(HALF["dg"] + 2 * s + 2)
                diff_exp(s)
                if s % 4 == 0 and s:
                    diff_gate(s // 4 - 1)
                if s:
                    diff_copy_o(s - 1)
                split_to(min(HALF["dg"] + 2 * s + 3, HALF["out1"]))
                diff_copy_attn(s)
            diff_gate(3)
            diff_copy_o(SCORES - 1)
            act.wait_ge(o_copied, SCORES)
            act.activation(o_squares, o_squares, ACT.Sqrt, scale=1.0 / T, bias=EPS_SUB).then_inc(squares_summed, 1)
            copy_turned(1, hall[:, DK], "subln")
            split_to(HALF["cmp"])
            norm_root(1)

            def row_rms(src, ready, dump):
                for t in range(TT):
                    act.wait_ge(ready[0], ready[1] + t)
                    ins = act.activation(token_rows(dump)[:, t], token_rows(src)[:, t], ACT.Square, accum_out=row_squares[:, t, 0:1])
                then(ins)
                act.activation(row_root, row_squares[:, :, 0], ACT.Sqrt, scale=1.0 / D, bias=EPS_6).then_inc(post_root_ready, 1)

            row_rms(X_TOK, (tok_ready, 5), DG)
            copy_turned(2, hall[:, H_T], "mix_pre")
            evacuate(PANELS["cmp"], cm)
            evacuate(PANELS["kk"], k4)
            split_to(HALF["kr"] + 4)
            act.wait_ge(gate_sum_done, 1)
            act.activation(gate_sum, ps[0:24, 6, 0:T], ACT.Copy).then_inc(gate_sum_copied, 1)
            for i in range(2):
                split_to(HALF["kr"] + 6 + 2 * i)
                act.wait_ge(cmp_step, i + 1)
                act.activation(cmp_hid[:, i, :], cmp_hid[:, i, :], ACT.Gelu_apprx_tanh).then_inc(cmp_hid_ready, 1)
            split_to(HALF["kr"] + 10)
            act.wait_ge(gate_turned, 1)
            act.activation(gates, ps[:, 7, 0:48].rearrange("p (t b) -> p t b", t=TT), ACT.Sigmoid).then_inc(gates_ready, 1)
            for name, dst in (("kr", kr), ("qr", qr), ("qa", qa)):
                for p in range(2):
                    evacuate(PANELS[name] + p, dst[:, 4 * p:4 * p + 4])
            split_to(HALF["vv"] + 6)
            act.wait_ge(cmp_centred, 1)
            act.activation(cmp_p, cmp_p, ACT.Exp).then_inc(cmp_exp, 1)
            split_to(ahead(PANELS["vv"]))
            for i in range(4):
                act.wait_ge(cmp_turned, i + 1)
                act.activation(cmp_prob_t[:, 4 * i:4 * i + 4, :], ps[0:NCMP, 4 + i, :].rearrange("p (i q) -> p i q", i=4), ACT.Copy)\
                   .then_inc(cmp_turned_copied, 1)
            evacuate_rows(PANELS["vv"], vv)

            def nsa_exp(i):
                w = P * (i % TT + 1)
                act.wait_ge(score_max, SCORES + i + 1)
                for m in range(2):
                    pr = a_prob[i % 2][:, m * T:m * T + w]
                    ins = act.activation(pr, pr, ACT.Exp, bias=top[i % 2][:, m:m + 1], accum_out=total[i % 2][:, m:m + 1])
                ins.then_inc(score_exp, 1)

            def nsa_copy_attn(i):
                w = P * (i % TT + 1)
                act.wait_ge(attn_turned, SCORES + i + 1)
                if i >= 2:
                    act.wait_ge(o_done, SCORES + i - 1)
                view = lambda ap: ap.rearrange("p (m k) -> p m k", m=2)[:, :, 0:w]
                act.activation(view(a_prob_t[i % 2]), view(ps[:, 6, :]), ACT.Copy).then_inc(attn_copied, 1)

            def nsa_copy_o(i):
                h, t = divmod(i, TT)
                act.wait_ge(o_done, SCORES + i + 1)
                act.activation(hall[:, CAT_T, h, t * P:(t + 1) * P], ps[:, 7, 0:P], ACT.Copy).then_inc(o_copied, 1)

            act.wait_ge(rope_ready, 2)
            for s in range(SCORES):
                split_to(min(HALF["vr"] + 2 * s + 4, HALF["out2"]))
                nsa_exp(s)
                if s % 4 == 3:
                    p = (s // 4) % 2
                    evacuate_rows(PANELS[("vr", "gr")[s // 8]] + p, (vr, gr)[s // 8][:, :, 512 * p:512 * p + 512],
                                  (ACT.Copy, ACT.Silu)[s // 8])
                if s:
                    nsa_copy_o(s - 1)
                split_to(min(HALF["vr"] + 2 * s + 5, HALF["out2"]))
                nsa_copy_attn(s)
            nsa_copy_o(SCORES - 1)
            for h in range(4):
                act.wait_ge(ret_var_ready, h + 1)
                act.activation(ret_root[h % 2], ret_mv[h % 2][:, :, 1], ACT.Sqrt, bias=EPS_6).then_inc(ret_root_ready, 1)
            for h in range(4):
                act.wait_ge(ret_turned, h + 1)
                act.activation(hall[:, CAT_T, 8 + 2 * h:10 + 2 * h, :], ps[:, h, :].rearrange("p (a t) -> p a t", a=2), ACT.Copy)\
                   .then_inc(ret_turned_copied, 1)

            def summed_rows(name, dst, dump, halves):
                for p in range(4):
                    n, done = PANELS[name] + p, HALF[name] + halves * (p + 1)
                    split_to(min(done + 2, HALF[name] + 4 * halves))
                    act.wait_ge(halves_used, done)
                    for t in range(TT):
                        act.activation(token_rows(dump)[:, t, 512 * p:512 * p + 512], ps[:, 2 * (n % 2) + t, :], ACT.Square, accum_out=row_squares[:, t, p:p + 1])
                    for t in range(TT):
                        ins = act.activation(token_rows(dst)[:, t, 512 * p:512 * p + 512], ps[:, 2 * (n % 2) + t, :], ACT.Copy)
                    ins.then_inc(panel_evacuated[n % 2], 1)
                evacuated(act, PANELS[name] + 3)
                for t in range(TT):
                    ins = act.activation(token_rows(dump)[:, t, 0:4], row_squares[:, t, :], ACT.Copy, accum_out=row_root[:, t:t + 1])
                then(ins)
                act.activation(row_root, row_root, ACT.Sqrt, scale=1.0 / D, bias=EPS_6).then_inc(post_root_ready, 1)

            summed_rows("out2", MIX_TOK, VR_GR, 8)
            row_rms(X_TOK, (post_rows_ready, 1), VR_GR)
            copy_turned(3, hall[:, H_T], "mlp_pre")
            with act.Fori(0, 8) as i:
                for h in range(HALF["up"], HALF["up"] + 16):
                    split_half(h, i * 16)
            split[0] = HALF["down"]
            summed_rows("down", H_TOK, H_T, 32)


def kernel(**inputs):
    import concourse.bacc as bacc
    from concourse.bass_utils import run_bass_kernel_spmd as run

    a = {k: np.asarray(v) for k, v in inputs.items()}
    nc = bacc.Bacc("TRN2", target_bir_lowering=False, num_devices=1)
    arrays, d = {}, {}

    def give(name, value):
        value = np.ascontiguousarray(value)
        arrays[name] = value
        d[name] = nc.dram_tensor(name, value.shape, mybir.dt.from_np(value.dtype), kind="ExternalInput").ap()

    def tiles(w):
        return w.reshape(DT, P, -1).transpose(1, 0, 2).reshape(P, -1)

    def rows_of(w):
        return w.reshape(TT, P, -1).transpose(1, 0, 2).reshape(P, -1)

    x = a["x"][0]
    slots = []

    def stream(w, columns=None):
        columns = np.arange(w.shape[1]) if columns is None else columns
        for c in range(0, len(columns), 512):
            slots.append(slot_panels(w, columns[c:c + 512]))

    stream(a["a_w_in"][0, 1])
    stream(a["a_w_in"][0, 0])
    stream(a["a_w_in"][0, 2])
    stream(a["a_w_in"][0, 3])
    stream(a["a_w_out"][0])
    stream(a["w_k_shared"])
    stream(a["b_w_qg"][0], np.arange(D))
    stream(a["w_v_shared"])
    stream(a["b_w_qg"][0], np.arange(D, 2 * D))
    stream(a["b_w_out"][0])
    w_in, kv = a["w_in_2"][0], [np.arange(1024 + 256 * i, 1280 + 256 * i) for i in range(6)]
    ret = [np.arange(2584 + 1024 * i, 3608 + 1024 * i) for i in range(4)]
    for columns in ((kv[0], kv[1]), (kv[2], kv[4]), (ret[1],), (ret[0],), (np.arange(1024),), (kv[3], kv[5]), (ret[2],), (ret[3],)):
        stream(w_in, np.concatenate(columns))
    stream(a["w_out_2"][0])
    stream(a["w_up_2"][0])
    stream(a["w_down_2"][0])
    give("stream", np.concatenate(slots))
    d["slots"] = arrays["stream"].shape[0]
    give("x_channels", tiles(x.T))
    give("resident", resident_constants())
    vectors = {
        "mu_r": a["a_mu_proj"][0, 0], "mu_k": a["a_mu_proj"][0, 1], "mu_v": a["a_mu_proj"][0, 2],
        "mu_g": a["a_mu_proj"][0, 3], "mu_w": a["a_mu_lora"][0, 0], "mu_a": a["a_mu_lora"][0, 1],
        "w0": a["a_w0"][0], "a0": a["a_a0"][0], "k_k": a["a_k_k"][0], "k_a": a["a_k_a"][0],
        "r_k": a["a_r_k"][0].reshape(-1), "gn_g": a["a_gn_g"][0], "gn_b": a["a_gn_b"][0],
        "mix_pre": a["norm_mix_pre_2"][0], "mlp_pre": a["norm_mlp_pre_2"][0],
        "subln": np.tile(a["b_subln_g"][0], DH),
    }
    give("params", np.stack([vectors[name].reshape(DT, P).T for name in PV], 1).reshape(P, -1))
    give("lora1", np.concatenate([tiles(a["a_w1"][0]), tiles(a["a_a1"][0])], 1))
    give("lora2", np.concatenate([a["a_w2"][0], a["a_a2"][0]], 1))
    give("restart", np.broadcast_to((np.arange(T) % N != 0).astype(np.float32), (P, T)))
    give("x_tokens", rows_of(x))
    give("rows", np.stack([a["ln_g"][0], a["ln_b"][0], a["ln_g"][1], a["ln_b"][1], a["norm_mix_post_2"][0],
                           a["norm_mlp_post_2"][0]]))
    give("dist", diff_constants())
    give("lambda", a["b_lambda"][0].reshape(-1))
    give("t5_table", np.broadcast_to(np.concatenate([a["t5_bias_2"], np.full((1, 8), NEG, np.float32)])[:, :, None],
                                     (33, 8, P)).reshape(33, -1))
    give("t5_one", t5_constants())
    give("cmp_small", np.concatenate([a["cmp_pe_k_2"][0].T, a["cmp_pe_v_2"][0].T, a["cmp_w2_k_2"][0], a["cmp_w2_v_2"][0]], 1))
    give("cmp_b1", np.concatenate([a["cmp_b1_k_2"][0], a["cmp_b1_v_2"][0]]))
    give("cmp_w1", np.stack([a[k][0].reshape(32, P, P).transpose(1, 0, 2).reshape(P, -1) for k in ("cmp_w1_k_2", "cmp_w1_v_2")]))
    give("gate_w", tiles(w_in[:, 2560:2584]))
    give("rope", rope_constants().reshape(P, -1))
    give("valid", np.broadcast_to(valid_constants()[:, None], (P, 8, TT, NCMP)).reshape(P, -1))
    give("decay", decay_constants().reshape(P, -1))
    d["t5_scratch"] = nc.dram_tensor("t5_scratch", (8, P, 384), F32, kind="Internal").ap()
    d["out"] = nc.dram_tensor("out", (T, D), F32, kind="ExternalOutput").ap()
    build(nc, d)
    r = run(nc, [arrays], core_ids=[0])
    return r.results[0]["out"].reshape(1, T, D)
```
